# Optimizing a Trainium2 kernel written in Bass

```python
import jax, jax.numpy as jnp
from jax import lax
import numpy as np

D_MODEL = 1024
BATCH = 1
SEQ = 1024
DEPTH = 1
DEC_BATCH = 8
DEC_SEQ = 4
PAST_LEN = 1024
PAGE_SIZE = 128

N_META = 16
CONV_WIDTH = 512
CONV_K = 3
N_HEADS = 8
QK_NOPE = 64
QK_ROPE = 32
QK_HEAD = QK_NOPE + QK_ROPE
V_HEAD = 64
Q_LORA = 384
KV_LORA = 256
ROPE_THETA = 10000.0
ATTN_SCALE = QK_HEAD ** -0.5
NEG_INF = -1e30
Q_BLOCK = 128
PEER_HEADS = 8
PEER_NKEYS = 128
PEER_EXPERTS = PEER_NKEYS * PEER_NKEYS
PEER_QDIM = 256
PEER_HALF = PEER_QDIM // 2
PEER_TOPK = 16
PEER_BLOCK = 256
EPS = 1e-6
IN_WIDTHS = (CONV_WIDTH, CONV_WIDTH, CONV_WIDTH, Q_LORA, KV_LORA, QK_ROPE, D_MODEL, D_MODEL)
IN_TOTAL = sum(IN_WIDTHS)
IN_OFFSETS = np.cumsum(IN_WIDTHS)[:-1].tolist()

kernel_name = 'mla_shortconv_peer_hybrid'

def rmsnorm(x, g):
    xf = x.astype(jnp.float32)
    y = xf * lax.rsqrt(jnp.mean(jnp.square(xf), axis=-1, keepdims=True) + EPS)
    return (y * g.astype(jnp.float32)).astype(x.dtype)

def rope_tables(pos):
    inv_freq = ROPE_THETA ** (-jnp.arange(0, QK_ROPE, 2, dtype=jnp.float32) / QK_ROPE)
    ang = pos.astype(jnp.float32)[:, None] * inv_freq[None, :]
    return jnp.cos(ang), jnp.sin(ang)

def apply_rope(x, cos, sin):
    xf = x.astype(jnp.float32)
    x1, x2 = xf[..., :QK_ROPE // 2], xf[..., QK_ROPE // 2:]
    return jnp.concatenate([x1 * cos - x2 * sin, x2 * cos + x1 * sin], axis=-1).astype(x.dtype)

def in_projection(h, w_in):
    return jnp.split(h @ w_in, IN_OFFSETS, axis=-1)

def short_conv(u_ext, conv_w, n_out):
    return sum(conv_w[k] * u_ext[:, k:k + n_out] for k in range(CONV_K))

def mla_queries(q_lat, cos, sin, g_q_lat, w_uq, g_q_nope, g_q_rope):
    cq = rmsnorm(q_lat, g_q_lat)
    q = jnp.einsum('blc,chd->blhd', cq, w_uq)
    qn = rmsnorm(q[..., :QK_NOPE], g_q_nope)
    qr = apply_rope(rmsnorm(q[..., QK_NOPE:], g_q_rope), cos[:, None, :], sin[:, None, :])
    return qn, qr

def mla_latent(kv_lat, kr_raw, cos, sin, g_kv_lat, g_k_rope):
    return rmsnorm(kv_lat, g_kv_lat), apply_rope(rmsnorm(kr_raw, g_k_rope), cos, sin)

def mla_keys(ckv, w_uk, g_k_nope):
    return rmsnorm(jnp.einsum('...kc,chd->...khd', ckv, w_uk), g_k_nope)

def attend(qn, qr, q_pos, kn, kr, ckv, k_pos, w_uv):
    s = (jnp.einsum('bqhd,bkhd->bhqk', qn, kn, preferred_element_type=jnp.float32)
         + jnp.einsum('bqhd,bkd->bhqk', qr, kr, preferred_element_type=jnp.float32))
    s = jnp.where(k_pos[None, :] <= q_pos[:, None], s * ATTN_SCALE, NEG_INF)
    p = jax.nn.softmax(s, axis=-1).astype(ckv.dtype)
    o_lat = jnp.einsum('bhqk,bkc->bqhc', p, ckv)
    return jnp.einsum('bqhc,chd->bqhd', o_lat, w_uv)

def prompt_attention(qn, qr, kn, kr, ckv, w_uv, with_meta):
    b, n_tot = kn.shape[:2]
    n_real = n_tot - N_META
    nb = n_real // Q_BLOCK
    pos = jnp.arange(n_tot)

    def blocks(a):
        a = a[:, a.shape[1] - n_real:]
        return jnp.moveaxis(a.reshape(b, nb, Q_BLOCK, *a.shape[2:]), 1, 0)

    def one_block(args):
        bqn, bqr, bpos = args
        return attend(bqn, bqr, bpos, kn, kr, ckv, pos, w_uv)

    out = lax.map(one_block, (blocks(qn), blocks(qr), pos[N_META:].reshape(nb, Q_BLOCK)))
    out = jnp.moveaxis(out, 0, 1).reshape(b, n_real, N_HEADS, V_HEAD)
    if with_meta:
        mp = pos[:N_META]
        meta = attend(qn[:, :N_META], qr[:, :N_META], mp, kn[:, :N_META], kr[:, :N_META], ckv[:, :N_META], mp, w_uv)
        out = jnp.concatenate([meta, out], axis=1)
    return out

def sample_attention(qn, qr, ckv_new, kr_new, pool_ckv, pool_kr, page_table, w_uk, w_uv, g_k_nope):
    dec_seq = qn.shape[1]
    q_pos = PAST_LEN + jnp.arange(dec_seq)
    k_pos = jnp.arange(PAST_LEN + dec_seq)

    def one_seq(args):
        pages, sqn, sqr, sckv, skr = args
        ckv_all = jnp.concatenate([pool_ckv[pages].reshape(-1, KV_LORA), sckv], axis=0)
        kr_all = jnp.concatenate([pool_kr[pages].reshape(-1, QK_ROPE), skr], axis=0)
        kn = mla_keys(ckv_all, w_uk, g_k_nope)
        return attend(sqn[None], sqr[None], q_pos, kn[None], kr_all[None], ckv_all[None], k_pos, w_uv)[0]

    return lax.map(one_seq, (page_table, qn, qr, ckv_new, kr_new))

def branch_merge(b_gate, conv_y, attn_heads, gate_c, gate_a, w_conv_out, w_attn_out, w_mix_out):
    conv_o = (b_gate * conv_y) @ w_conv_out
    attn_o = attn_heads.reshape(*attn_heads.shape[:-2], N_HEADS * V_HEAD) @ w_attn_out
    return (jax.nn.sigmoid(gate_c) * conv_o + jax.nn.sigmoid(gate_a) * attn_o) @ w_mix_out

def peer_block(h, w_peer_q, sub_keys, expert_u, expert_v):
    t = h.shape[0]
    q = (h @ w_peer_q).reshape(t, PEER_HEADS, 2, PEER_HALF)
    s = jnp.einsum('thcd,chnd->thcn', q, sub_keys, preferred_element_type=jnp.float32)
    s1, i1 = lax.top_k(s[:, :, 0], PEER_TOPK)
    s2, i2 = lax.top_k(s[:, :, 1], PEER_TOPK)
    cand = (s1[..., :, None] + s2[..., None, :]).reshape(t, PEER_HEADS, PEER_TOPK * PEER_TOPK)
    cidx = (i1[..., :, None] * PEER_NKEYS + i2[..., None, :]).reshape(t, PEER_HEADS, PEER_TOPK * PEER_TOPK)
    best, sel = lax.top_k(cand, PEER_TOPK)
    eidx = jnp.take_along_axis(cidx, sel, axis=-1)
    g = jax.nn.softmax(best, axis=-1).astype(h.dtype)
    a = jax.nn.gelu(jnp.einsum('thkd,td->thk', expert_u[eidx], h), approximate=False)
    return jnp.einsum('thk,thkd->td', g * a, expert_v[eidx])

def peer(h, w_peer_q, sub_keys, expert_u, expert_v):
    b, l, d = h.shape
    n = b * l
    nb = -(-n // PEER_BLOCK)
    flat = jnp.pad(h.reshape(n, d), ((0, nb * PEER_BLOCK - n), (0, 0))).reshape(nb, PEER_BLOCK, d)
    out = lax.map(lambda hb: peer_block(hb, w_peer_q, sub_keys, expert_u, expert_v), flat)
    return out.reshape(nb * PEER_BLOCK, d)[:n].reshape(b, l, d)

def setup_inputs(seed: int = 0) -> dict:
    key = jax.random.key(seed)
    ks = iter(jax.random.split(key, 40))
    nrm = lambda shape, scale: jax.random.normal(next(ks), shape, jnp.float32) * scale
    gain = lambda shape: 1.0 + 0.02 * jax.random.normal(next(ks), shape, jnp.float32)
    n_pages = PAST_LEN // PAGE_SIZE
    n_used = DEC_BATCH * n_pages
    n_phys = n_used + max(1, n_used // 4)
    page_table = jax.random.permutation(next(ks), n_phys)[:n_used].reshape(DEC_BATCH, n_pages).astype(jnp.int32)
    return {
        'x_prompt': nrm((BATCH, SEQ, D_MODEL), 1.0),
        'x_sample': nrm((DEC_BATCH, DEC_SEQ, D_MODEL), 1.0),
        'cache_ckv': nrm((DEPTH, n_phys, PAGE_SIZE, KV_LORA), 1.0),
        'cache_krope': nrm((DEPTH, n_phys, PAGE_SIZE, QK_ROPE), 1.0),
        'state_conv': nrm((DEPTH, DEC_BATCH, CONV_K - 1, CONV_WIDTH), 1.0),
        'page_table': page_table,
        'meta_tokens': nrm((N_META, D_MODEL), 1.0),
        'norm_mix': gain((DEPTH, D_MODEL)),
        'w_in': nrm((DEPTH, D_MODEL, IN_TOTAL), D_MODEL ** -0.5),
        'conv_w': nrm((DEPTH, CONV_K, CONV_WIDTH), CONV_K ** -0.5),
        'w_conv_out': nrm((DEPTH, CONV_WIDTH, D_MODEL), CONV_WIDTH ** -0.5),
        'g_q_lat': gain((DEPTH, Q_LORA)),
        'w_uq': nrm((DEPTH, Q_LORA, N_HEADS, QK_HEAD), Q_LORA ** -0.5),
        'g_q_nope': gain((DEPTH, QK_NOPE)),
        'g_q_rope': gain((DEPTH, QK_ROPE)),
        'g_kv_lat': gain((DEPTH, KV_LORA)),
        'g_k_rope': gain((DEPTH, QK_ROPE)),
        'w_uk': nrm((DEPTH, KV_LORA, N_HEADS, QK_NOPE), KV_LORA ** -0.5),
        'w_uv': nrm((DEPTH, KV_LORA, N_HEADS, V_HEAD), KV_LORA ** -0.5),
        'g_k_nope': gain((DEPTH, QK_NOPE)),
        'w_attn_out': nrm((DEPTH, N_HEADS * V_HEAD, D_MODEL), (N_HEADS * V_HEAD) ** -0.5),
        'w_mix_out': nrm((DEPTH, D_MODEL, D_MODEL), D_MODEL ** -0.5),
        'norm_ffn': gain((DEPTH, D_MODEL)),
        'w_peer_q': nrm((DEPTH, D_MODEL, PEER_HEADS * PEER_QDIM), D_MODEL ** -0.5),
        'peer_sub_keys': nrm((DEPTH, 2, PEER_HEADS, PEER_NKEYS, PEER_HALF), PEER_HALF ** -0.5),
        'peer_u': nrm((DEPTH, PEER_EXPERTS, D_MODEL), D_MODEL ** -0.5),
        'peer_v': nrm((DEPTH, PEER_EXPERTS, D_MODEL), PEER_HEADS ** -0.5),
    }

def reference(x_prompt, x_sample, cache_ckv, cache_krope, state_conv, page_table, meta_tokens, norm_mix, w_in,
              conv_w, w_conv_out, g_q_lat, w_uq, g_q_nope, g_q_rope, g_kv_lat, g_k_rope, w_uk, w_uv, g_k_nope,
              w_attn_out, w_mix_out, norm_ffn, w_peer_q, peer_sub_keys, peer_u, peer_v):
    n_batch, n_real, _ = x_prompt.shape
    n_tot = N_META + n_real
    dec_seq = x_sample.shape[1]
    cos_p, sin_p = rope_tables(jnp.arange(n_tot))
    cos_s, sin_s = rope_tables(PAST_LEN + jnp.arange(dec_seq))
    meta = jnp.broadcast_to(meta_tokens[None].astype(x_prompt.dtype), (n_batch, N_META, D_MODEL))
    xp = jnp.concatenate([meta, x_prompt], axis=1)
    xs = x_sample
    ckv_p, kr_p, conv_p, ckv_s, kr_s, conv_s = [], [], [], [], [], []
    for layer in range(DEPTH):
        r0 = N_META if layer == DEPTH - 1 else 0
        hp = rmsnorm(xp, norm_mix[layer])
        b_g, c_g, x_in, q_lat, kv_lat, kr_raw, gate_c, gate_a = in_projection(hp, w_in[layer])
        u = c_g * x_in
        u_ext = jnp.pad(u, ((0, 0), (CONV_K - 1, 0), (0, 0)))[:, r0:]
        conv_y = short_conv(u_ext, conv_w[layer], n_tot - r0)
        ckv, kr = mla_latent(kv_lat, kr_raw, cos_p, sin_p, g_kv_lat[layer], g_k_rope[layer])
        qn, qr = mla_queries(q_lat[:, r0:], cos_p[r0:], sin_p[r0:], g_q_lat[layer], w_uq[layer],
                             g_q_nope[layer], g_q_rope[layer])
        kn = mla_keys(ckv, w_uk[layer], g_k_nope[layer])
        attn = prompt_attention(qn, qr, kn, kr, ckv, w_uv[layer], r0 == 0)
        mix = branch_merge(b_g[:, r0:], conv_y, attn, gate_c[:, r0:], gate_a[:, r0:],
                           w_conv_out[layer], w_attn_out[layer], w_mix_out[layer])
        xp = xp[:, r0:] + mix
        xp = xp + peer(rmsnorm(xp, norm_ffn[layer]), w_peer_q[layer], peer_sub_keys[layer], peer_u[layer], peer_v[layer])
        ckv_p.append(ckv)
        kr_p.append(kr)
        conv_p.append(u[:, n_tot - (CONV_K - 1):])
        hs = rmsnorm(xs, norm_mix[layer])
        b_g, c_g, x_in, q_lat, kv_lat, kr_raw, gate_c, gate_a = in_projection(hs, w_in[layer])
        u_ext = jnp.concatenate([state_conv[layer], c_g * x_in], axis=1)
        conv_y = short_conv(u_ext, conv_w[layer], dec_seq)
        ckv, kr = mla_latent(kv_lat, kr_raw, cos_s, sin_s, g_kv_lat[layer], g_k_rope[layer])
        qn, qr = mla_queries(q_lat, cos_s, sin_s, g_q_lat[layer], w_uq[layer], g_q_nope[layer], g_q_rope[layer])
        attn = sample_attention(qn, qr, ckv, kr, cache_ckv[layer], cache_krope[layer], page_table,
                                w_uk[layer], w_uv[layer], g_k_nope[layer])
        mix = branch_merge(b_g, conv_y, attn, gate_c, gate_a, w_conv_out[layer], w_attn_out[layer], w_mix_out[layer])
        xs = xs + mix
        xs = xs + peer(rmsnorm(xs, norm_ffn[layer]), w_peer_q[layer], peer_sub_keys[layer], peer_u[layer], peer_v[layer])
        ckv_s.append(ckv)
        kr_s.append(kr)
        conv_s.append(u_ext[:, dec_seq:])
    return (xp, xs, jnp.stack(ckv_p), jnp.stack(kr_p), jnp.stack(conv_p),
            jnp.stack(ckv_s), jnp.stack(kr_s), jnp.stack(conv_s))


_drawn_inputs = setup_inputs


def setup_inputs(seed=0):
    import zlib

    import numpy as np

    out = dict(_drawn_inputs(seed))
    spreads = {}
    factors = {'g_q_lat': 8.0,
     'g_q_nope': 8.0,
     'g_q_rope': 35.844,
     'g_kv_lat': 3.026,
     'g_k_nope': 8.0,
     'norm_ffn': 2.843}
    for name, (base, spread) in spreads.items():
        noise = np.random.default_rng([zlib.crc32(name.encode()), seed]).standard_normal(out[name].shape)
        drawn = base * np.exp(spread * noise) if base else spread * noise
        out[name] = __import__('jax').numpy.asarray(drawn.astype(out[name].dtype))
    for name, factor in factors.items():
        out[name] = (out[name] * factor).astype(out[name].dtype)
    return out
```

```python
from contextlib import ExitStack

import numpy as np

import concourse.bass as bass
from concourse import mybir

F32 = mybir.dt.float32
U32 = mybir.dt.uint32
I32 = mybir.dt.int32
ALU = mybir.AluOpType
ACT = mybir.ActivationFunctionType
AX = mybir.AxisListType

P = 128
D = 1024
KD = D // P
META, SEQ = 16, 1024
NSEQ, DSEQ = 8, 4
NS = NSEQ * DSEQ
T = META + SEQ + NS
KEYS = META + SEQ
TQ = SEQ + NS
CW = 512
CT = CW // P
QL, KVL, ROPE, NOPE, VH, NH = 384, 256, 32, 64, 64, 8
QT, KT = QL // P, KVL // P
HD = NOPE + ROPE
SCALE = float(HD) ** -0.5
PAST, PAGE = 1024, 128
NPG = PAST // PAGE
SK = PAST + DSEQ
NEG = -1e30
PH, NK, TOPK = 8, 128, 16
HC = PH * 2
TT = 96
NT = TQ // TT
PICK = PH * TOPK
EPS = 1e-6
CHUNKS = [(0, 360), (360, 360), (720, 352)]
QCH = [(0, 352), (352, 352), (704, 352)]
GRP = 4
TILES = [(0, 4), (4, 4), (8, 3)]

C_ONES = 0
C_MEAN = C_ONES + P
C_KV = C_MEAN + P
C_R32 = C_KV + P
C_HEAD = C_R32 + P
C_ID = C_HEAD + P
C_SEL = C_ID + P
C_MASK = C_SEL + 4 * NS
C_SMASK = C_MASK + P + META
C_IOTA = C_SMASK + DSEQ
C_EPS = C_IOTA + P
C_ALL = C_EPS + 1


def norm_stage(nc, tag, X, H, K, g_dram, x_dram=None):
    with ExitStack() as ctx:
        sb = lambda n, s, d=F32: ctx.enter_context(nc.sbuf_tensor(tag + n, s, d))
        sem = lambda n: ctx.enter_context(nc.semaphore(tag + n))
        G = sb("gain", [P, KD])
        SQ = sb("sq", [P, 2, T])
        RT = sb("root", [P, T])
        SS = ctx.enter_context(nc.psum_tensor(tag + "ss", [P, 3, 512], F32))
        gain_in, sq_ready, sq_used, root_ready, inv_ready, h_ready = (
            sem(n) for n in ("gain_in", "sq_ready", "sq_used", "root_ready", "inv_ready", "h_ready"))
        x_in = [sem(f"x_in{k}") for k in range(KD)] if x_dram is not None else None
        block = ctx.enter_context(nc.Block())

        @block.sync
        def _(sp):
            if x_dram is not None:
                for k in range(KD):
                    sp.dma_start(X[:, k, :], x_dram[:, k, :]).then_inc(x_in[k], 16)
            sp.dma_start(G[:], g_dram).then_inc(gain_in, 16)

        @block.scalar
        def _(act):
            for k in range(KD):
                if x_dram is not None:
                    act.wait_ge(x_in[k], 16)
                if k >= 2:
                    act.wait_ge(sq_used, k - 1)
                act.activation(SQ[:, k % 2, :], X[:, k, :], ACT.Square).then_inc(sq_ready, 1)
            act.wait_ge(sq_used, KD)
            for c, (a, n) in enumerate(CHUNKS):
                act.activation(RT[:, a:a + n], SS[:, c, 0:n], ACT.Sqrt,
                               bias=K[:, C_EPS:C_EPS + 1]).then_inc(root_ready, 1)

        @block.tensor
        def _(pe):
            for k in range(KD):
                pe.wait_ge(sq_ready, k + 1)
                for c, (a, n) in enumerate(CHUNKS):
                    mm = pe.matmul(SS[:, c, 0:n], K[:, C_MEAN:C_MEAN + P], SQ[:, k % 2, a:a + n],
                                   start=(k == 0), stop=(k == KD - 1))
                mm.then_inc(sq_used, 1)

        @block.vector
        def _(dve):
            for c, (a, n) in enumerate(CHUNKS):
                dve.wait_ge(root_ready, c + 1)
                dve.reciprocal(RT[:, a:a + n], RT[:, a:a + n]).then_inc(inv_ready, 1)
            dve.wait_ge(inv_ready, 3)
            dve.wait_ge(gain_in, 16)
            for k in range(KD):
                dve.scalar_tensor_tensor(H[:, k, :], X[:, k, :], G[:, k:k + 1], RT[:],
                                         ALU.mult, ALU.mult).then_inc(h_ready, 1)
            dve.wait_ge(h_ready, KD)


def conv_stage(nc, H, YC, d):
    with ExitStack() as ctx:
        sb = lambda n, s, dt=F32: ctx.enter_context(nc.sbuf_tensor("cv_" + n, s, dt))
        sem = lambda n: ctx.enter_context(nc.semaphore("cv_" + n))
        W = sb("w", [P, 2, 3, KD, P])
        U = sb("u", [P, T])
        US = sb("us", [P, NSEQ, 2 + DSEQ])
        BS = sb("b", [P, T])
        XS = sb("xin", [P, 2, 360])
        Y = sb("y", [P, TQ])
        CWT = sb("taps", [P, CT, 3])
        ST = sb("state", [P, CT, NSEQ, 2])
        NP_ = sb("newp", [P, CT, 2])
        NS_ = sb("news", [P, CT, NSEQ, 2])
        PS = ctx.enter_context(nc.psum_tensor("cv_ps", [P, 2, 3, 512], F32))
        w_in = [sem(f"w_in{s}") for s in range(2)]
        small_in, proj, copied, u_part, chan_done, step, stored = (
            sem(n) for n in ("small_in", "proj", "copied", "u_part", "chan_done", "step", "stored"))
        block = ctx.enter_context(nc.Block())
        STEPS = 10

        @block.sync
        def _(sp):
            sp.dma_start(CWT[:], d["taps"]).then_inc(small_in, 16)
            sp.dma_start(ST[:], d["state"]).then_inc(small_in, 16)
            for s in range(2):
                sp.dma_start(W[:, s], d["w_conv"][s].rearrange("a p k n -> p a k n")).then_inc(w_in[s], 16)
            with sp.Fori(0, CT // 2 - 1) as o:
                for s in range(2):
                    sp.wait_ge(proj, o * 6 + 3 * (s + 1))
                    sp.dma_start(W[:, s], d["w_conv"][bass.ds(o * 2 + s + 2, 1)].rearrange(
                        "o a p k n -> (o p) a k n")).then_inc(w_in[s], 16)
            sp.wait_ge(chan_done, CT)
            sp.dma_start(d["o_convp"], NP_[:]).then_inc(stored, 16)
            sp.dma_start(d["o_convs"], NS_[:]).then_inc(stored, 16)
            sp.wait_ge(stored, 32)

        @block.tensor
        def _(pe):
            with pe.Fori(0, CT // 2) as o:
                for s in range(2):
                    pe.wait_ge(w_in[s], (o + 1) * 16)
                    for c, (a, n) in enumerate(CHUNKS):
                        g = 3 * s + c
                        if g >= 2:
                            pe.wait_ge(u_part, o * 6 + g - 1)
                        else:
                            pe.wait_ge(u_part, o * 6)
                        for m in range(3):
                            for k in range(KD):
                                mm = pe.matmul(PS[:, g % 2, m, 0:n], W[:, s, m, k, :], H[:, k, a:a + n],
                                               start=(k == 0), stop=(k == KD - 1))
                        mm.then_inc(proj, 1)

        @block.scalar
        def _(act):
            with act.Fori(0, CT // 2) as o:
                for s in range(2):
                    for c, (a, n) in enumerate(CHUNKS):
                        g = 3 * s + c
                        act.wait_ge(proj, o * 6 + g + 1)
                        if c == 0:
                            act.wait_ge(chan_done, o * 2 + s)
                        if g >= 2:
                            act.wait_ge(u_part, o * 6 + g - 1)
                        else:
                            act.wait_ge(u_part, o * 6)
                        act.activation(BS[:, a:a + n], PS[:, g % 2, 0, 0:n], ACT.Copy)
                        act.activation(XS[:, g % 2, 0:n], PS[:, g % 2, 2, 0:n], ACT.Copy).then_inc(copied, 1)

        @block.vector
        def _(dve):
            dve.wait_ge(small_in, 32)
            with dve.Fori(0, CT // 2) as o:
                for s in range(2):
                    c_ = o * 2 + s
                    at = c_ * STEPS
                    for c, (a, n) in enumerate(CHUNKS):
                        dve.wait_ge(copied, o * 6 + 3 * s + c + 1)
                        dve.tensor_tensor(U[:, a:a + n], PS[:, (3 * s + c) % 2, 1, 0:n],
                                          XS[:, (3 * s + c) % 2, 0:n], ALU.mult).then_inc(u_part, 1)
                    dve.wait_ge(u_part, c_ * 3 + 3)
                    tap = lambda k: CWT[:, bass.ds(c_, 1), k:k + 1].rearrange("p a k -> p (a k)")
                    us = U[:, META + SEQ:T].rearrange("p (s q) -> p s q", q=DSEQ)
                    dve.tensor_copy(US[:, :, 2:], us).then_inc(step, 1)
                    dve.tensor_copy(US[:, :, 0:2], ST[:, bass.ds(c_, 1)].rearrange("p a s k -> p (a s) k")
                                    ).then_inc(step, 1)
                    dve.tensor_copy(NP_[:, bass.ds(c_, 1), :].rearrange("p a k -> p (a k)"),
                                    U[:, META + SEQ - 2:META + SEQ]).then_inc(step, 1)
                    dve.tensor_scalar(Y[:, 0:SEQ], U[:, META - 2:META - 2 + SEQ], tap(0), None, ALU.mult
                                      ).then_inc(step, 1)
                    dve.wait_ge(step, at + 4)
                    dve.tensor_copy(NS_[:, bass.ds(c_, 1)].rearrange("p a s k -> p (a s) k"),
                                    US[:, :, DSEQ:]).then_inc(step, 1)
                    dve.scalar_tensor_tensor(Y[:, 0:SEQ], U[:, META - 1:META - 1 + SEQ], tap(1), Y[:, 0:SEQ],
                                             ALU.mult, ALU.add).then_inc(step, 1)
                    ys = Y[:, SEQ:TQ].rearrange("p (s q) -> p s q", q=DSEQ)
                    dve.tensor_scalar(ys, US[:, :, 0:DSEQ], tap(0), None, ALU.mult).then_inc(step, 1)
                    dve.wait_ge(step, at + 7)
                    dve.scalar_tensor_tensor(Y[:, 0:SEQ], U[:, META:META + SEQ], tap(2), Y[:, 0:SEQ],
                                             ALU.mult, ALU.add).then_inc(step, 1)
                    dve.scalar_tensor_tensor(ys, US[:, :, 1:1 + DSEQ], tap(1), ys, ALU.mult, ALU.add
                                             ).then_inc(step, 1)
                    dve.wait_ge(step, at + 9)
                    dve.scalar_tensor_tensor(ys, US[:, :, 2:2 + DSEQ], tap(2), ys, ALU.mult, ALU.add
                                             ).then_inc(step, 1)
                    dve.wait_ge(step, at + 10)
                    dve.tensor_tensor(YC[:, bass.ds(c_, 1), :].rearrange("p a t -> p (a t)"), Y[:],
                                      BS[:, META:T], ALU.mult).then_inc(chan_done, 1)


def rope(dve, out, x, swapped, CS, a, n, step, at, rows=slice(0, P)):
    r = rows
    dve.stream_shuffle(swapped, x, [(i + 16) % 32 for i in range(32)]).then_inc(step, 1)
    dve.wait_ge(step, at + 1)
    dve.tensor_tensor(swapped, swapped, CS[r, 1, a:a + n], ALU.mult).then_inc(step, 1)
    dve.tensor_tensor(out, x, CS[r, 0, a:a + n], ALU.mult).then_inc(step, 1)
    dve.wait_ge(step, at + 3)
    dve.tensor_tensor(out, out, swapped, ALU.add).then_inc(step, 1)


def latent_stage(nc, H, K, CQ, CKV, KR, CS, d):
    with ExitStack() as ctx:
        sb = lambda n, s, dt=F32: ctx.enter_context(nc.sbuf_tensor("lt_" + n, s, dt))
        sem = lambda n: ctx.enter_context(nc.semaphore("lt_" + n))
        NB = QT + KT + 1
        W = sb("w", [P, 2, KD, P])
        SQ = sb("sq", [P, 2, T])
        RT = sb("root", [P, 3, T])
        G = sb("gains", [P, NB])
        SW = sb("swap", [P, T])
        PS = ctx.enter_context(nc.psum_tensor("lt_ps", [P, 3, 512], F32))
        SS = ctx.enter_context(nc.psum_tensor("lt_ss", [P, 3, 512], F32))
        w_in = [sem(f"w_in{s}") for s in range(2)]
        small_in, proj, lat, sq_ready, sq_used, root, step, stored = (
            sem(n) for n in ("small_in", "proj", "lat", "sq_ready", "sq_used", "root", "step", "stored"))
        block = ctx.enter_context(nc.Block())
        dst = [CQ[:, i, :] for i in range(QT)] + [CKV[:, i, :] for i in range(KT)] + [KR[:, :]]
        first = {0: 0, 1: 0, 2: 0, 3: 1, 4: 1, 5: 2}
        last = {2: 0, 4: 1, 5: 2}
        mean = [C_ONES, C_KV, C_R32]

        @block.sync
        def _(sp):
            sp.dma_start(G[:], d["g_lat"]).then_inc(small_in, 16)
            sp.dma_start(CS[:], d["cossin"]).then_inc(small_in, 16)
            for b in range(NB):
                if b >= 2:
                    sp.wait_ge(proj, b - 1)
                sp.dma_start(W[:, b % 2], d["w_lat"][b]).then_inc(w_in[b % 2], 16)
            sp.wait_ge(step, 13)
            sp.dma_start(d["o_ckv"], CKV[:]).then_inc(stored, 16)
            sp.dma_start(d["o_kr"], KR[0:ROPE, :]).then_inc(stored, 16)
            sp.wait_ge(stored, 32)

        @block.tensor
        def _(pe):
            def squares(b):
                pe.wait_ge(sq_ready, b + 1)
                if b in (3, 5):
                    pe.wait_ge(root, 1 + (b == 5))
                for c, (a, n) in enumerate(CHUNKS):
                    m = mean[first[b]]
                    mm = pe.matmul(SS[:, c, 0:n], K[:, m:m + P], SQ[:, b % 2, a:a + n],
                                   start=(b in (0, 3, 5)), stop=(b in last))
                mm.then_inc(sq_used, 1)

            for b in range(NB):
                pe.wait_ge(w_in[b % 2], 16 * (b // 2 + 1))
                if b:
                    pe.wait_ge(lat, b)
                for c, (a, n) in enumerate(CHUNKS):
                    for k in range(KD):
                        mm = pe.matmul(PS[:, c, 0:n], W[:, b % 2, k, :], H[:, k, a:a + n],
                                       start=(k == 0), stop=(k == KD - 1))
                mm.then_inc(proj, 1)
                if b:
                    squares(b - 1)
            squares(NB - 1)

        @block.scalar
        def _(act):
            def roots(b):
                act.wait_ge(sq_used, b + 1)
                i = last[b]
                for c, (a, n) in enumerate(CHUNKS):
                    ins = act.activation(RT[:, i, a:a + n], SS[:, c, 0:n], ACT.Sqrt, bias=K[:, C_EPS:C_EPS + 1],
                                         scale=1.0 / QL if i == 0 else 1.0)
                ins.then_inc(root, 1)

            for b in range(NB):
                act.wait_ge(proj, b + 1)
                for c, (a, n) in enumerate(CHUNKS):
                    ins = act.activation(dst[b][:, a:a + n], PS[:, c, 0:n], ACT.Copy)
                ins.then_inc(lat, 1)
                act.wait_ge(lat, b + 1)
                if b >= 2:
                    act.wait_ge(sq_used, b - 1)
                act.activation(SQ[:, b % 2, :], dst[b], ACT.Square).then_inc(sq_ready, 1)
                if b - 1 in last:
                    roots(b - 1)
            roots(NB - 1)

        @block.vector
        def _(dve):
            dve.wait_ge(small_in, 32)
            at = 0
            for i, blocks in enumerate(([0, 1, 2], [3, 4], [5])):
                dve.wait_ge(root, i + 1)
                dve.reciprocal(RT[:, i, :], RT[:, i, :]).then_inc(step, 1)
                at += 1
                dve.wait_ge(step, at)
                for b in blocks:
                    dve.scalar_tensor_tensor(dst[b], dst[b], G[:, b:b + 1], RT[:, i, :], ALU.mult, ALU.mult
                                             ).then_inc(step, 1)
                    at += 1
            dve.wait_ge(step, at)
            rope(dve, KR[:, :], KR[:, :], SW[:], CS, 0, T, step, at)
            assert at + 4 == 13
            dve.wait_ge(step, at + 4)


def head_stage(nc, K, CQ, CKV, KR, CS, QABS, QRS, d):
    with ExitStack() as ctx:
        sb = lambda n, s, dt=F32: ctx.enter_context(nc.sbuf_tensor("hd_" + n, s, dt))
        sem = lambda n: ctx.enter_context(nc.semaphore("hd_" + n))
        WQ, WK, WV = 0, QT * HD, QT * HD + KT * NOPE
        WALL = WV + KT * VH
        W = sb("w", [P, WALL])
        WUT = sb("wukT", [NOPE, KVL])
        G = sb("gains", [P, 3])
        SQ = sb("sq", [HD, 2, 360])
        RQ = sb("rq", [HD, TQ])
        RK = sb("rk", [NOPE, T])
        Q = sb("q", [HD, TQ])
        KH = sb("k", [HD, T])
        SW = sb("swap", [HD, TQ])
        QG = sb("qg", [NOPE, NS])
        V = sb("v", [P, 9, VH])
        PR = sb("p", [P, 2, KEYS])
        PT = sb("pt", [P, 10, P])
        PAD = sb("pad", [1, 1])
        MX = sb("mx", [P, 8])
        NM = sb("nm", [P, 8])
        SM = sb("sum", [P, 8])
        RI = sb("ri", [P, 8])
        O = sb("o", [P, 2, VH])
        AT = sb("at", [VH, SEQ])
        PS = ctx.enter_context(nc.psum_tensor("hd_ps", [P, 8, 512], F32))
        (w_in, small_in, qraw, kraw, sq_ready, ss, root, vraw, vset, qabs, qabs_set, qk, step, score, negmax,
         probs, inv, turned, pt_act, pt_dve, pv, oset, ot, oT, stored) = (
            sem(n) for n in ("w_in", "small_in", "qraw", "kraw", "sq_ready", "ss", "root", "vraw", "vset", "qabs",
                             "qabs_set", "qk", "step", "score", "negmax", "probs", "inv", "turned", "pt_act", "pt_dve",
                             "pv", "oset", "ot", "oT", "stored"))
        block = ctx.enter_context(nc.Block())
        NQ = SEQ // P
        nkeys = lambda i: META + P * (i + 1)
        blocks = lambda i: i + 2
        groups = lambda i: (blocks(i) + 3) // 4
        before = lambda i: sum(groups(j) for j in range(i))
        GR = before(NQ)
        even = lambda n: (n + 1) // 2
        odd = lambda n: n // 2
        assert GR % 2 == 0
        STEPS = 8 + 2 * NQ

        @block.sync
        def _(sp):
            sp.dma_start(G[:], d["g_head"]).then_inc(small_in, 16)
            with sp.Fori(0, NH) as h:
                sp.wait_ge(qabs, h)
                sp.dma_start(W[:], d["w_head"][bass.ds(h, 1)].rearrange("o p n -> (o p) n")).then_inc(w_in, 16)
                sp.dma_start(WUT[:], d["w_ukT"][bass.ds(h, 1)].rearrange("o p n -> (o p) n")).then_inc(w_in, 16)
                sp.wait_ge(oT, (h + 1) * NQ)
                sp.dma_start(d["s_attn"][bass.ds(h, 1), :, 0:SEQ].rearrange("o p n -> (o p) n"), AT[:]
                             ).then_inc(stored, 16)
            sp.wait_ge(stored, 16 * NH)

        @block.tensor
        def _(pe):
            with pe.Fori(0, NH) as h:
                pe.wait_ge(w_in, (h + 1) * 32)
                pe.wait_ge(probs, h * NQ)
                pe.wait_ge(oT, h * NQ)
                for c, (a, n) in enumerate(QCH):
                    for k in range(QT):
                        mm = pe.matmul(PS[0:HD, c, 0:n], W[:, WQ + k * HD:WQ + (k + 1) * HD],
                                       CQ[:, k, META + a:META + a + n], start=(k == 0), stop=(k == QT - 1))
                    mm.then_inc(qraw, 1)
                for c, (a, n) in enumerate(CHUNKS):
                    for k in range(KT):
                        mm = pe.matmul(PS[0:NOPE, 3 + c, 0:n], W[:, WK + k * NOPE:WK + (k + 1) * NOPE],
                                       CKV[:, k, a:a + n], start=(k == 0), stop=(k == KT - 1))
                    mm.then_inc(kraw, 1)
                for i in range(6):
                    n = QCH[i][1] if i < 3 else CHUNKS[i - 3][1]
                    R = HD if i < 3 else NOPE
                    pe.wait_ge(sq_ready, h * 6 + i + 1)
                    if i >= 2:
                        pe.wait_ge(root, h * 6 + i - 1)
                    pe.matmul(PS[0:HD, 6 + i % 2, 0:n], K[0:R, C_HEAD:C_HEAD + HD], SQ[0:R, i % 2, 0:n],
                              start=True, stop=True).then_inc(ss, 1)
                pe.wait_ge(root, h * 6 + 6)
                for j in range(9):
                    m = P if j < 8 else META
                    out = PS[0:m, 6, j * VH:(j + 1) * VH] if j < 8 else PS[0:m, 7, 0:VH]
                    for k in range(KT):
                        mm = pe.matmul(out, CKV[:, k, j * P:j * P + m], W[:, WV + k * VH:WV + (k + 1) * VH],
                                       start=(k == 0), stop=(k == KT - 1), skip_group_check=True)
                mm.then_inc(vraw, 1)
                pe.wait_ge(vset, h + 1)
                pe.wait_ge(qk, h + 1)
                for k in range(KT):
                    mm = pe.matmul(PS[:, 7, k * NS:(k + 1) * NS], WUT[:, k * P:(k + 1) * P], QG[:],
                                   start=True, stop=True, skip_group_check=True)
                mm.then_inc(qabs, 1)

                def back(i):
                    pe.wait_ge(w_in, 32)
                    pe.wait_ge(probs, h * NQ + i + 1)
                    if i == 0:
                        pe.wait_ge(qabs_set, h + 1)
                    for g in range(groups(i)):
                        G_ = before(i) + g
                        pe.wait_ge(w_in, 32)
                        if G_:
                            if G_ % 2:
                                pe.wait_ge(pt_act, h * (GR // 2) + even(G_))
                            else:
                                pe.wait_ge(pt_dve, h * (GR // 2) + odd(G_))
                        for j in range(4 * g, min(4 * g + 4, blocks(i))):
                            m = P if j < blocks(i) - 1 else META
                            mm = pe.transpose(PS[0:m, 6, (j % 4) * P:(j % 4 + 1) * P],
                                              PR[:, i % 2, j * P:j * P + m], K[:, C_ID:C_ID + P])
                        mm.then_inc(turned, 1)
                    n = before(i + 1)
                    pe.wait_ge(pt_act, h * (GR // 2) + even(n))
                    if odd(n):
                        pe.wait_ge(pt_dve, h * (GR // 2) + odd(n))
                    if i:
                        pe.wait_ge(oT, h * NQ + i)
                    for j in range(blocks(i)):
                        m = P if j < blocks(i) - 1 else META
                        mm = pe.matmul(PS[:, 7, 0:VH], PT[0:m, j, :], V[0:m, j, :],
                                       start=(j == 0), stop=(j == blocks(i) - 1))
                    mm.then_inc(pv, 1)
                    pe.wait_ge(w_in, 32)
                    pe.wait_ge(oset, h * NQ + i + 1)
                    pe.transpose(PS[0:VH, 7, P:2 * P], O[:, i % 2, :], K[:, C_ID:C_ID + P]).then_inc(ot, 1)

                for i in range(NQ + 1):
                    if i < NQ:
                        if i >= 2:
                            pe.wait_ge(probs, h * NQ + i - 1)
                        for c in range(-(-nkeys(i) // 512)):
                            n = min(512, nkeys(i) - 512 * c)
                            mm = pe.matmul(PS[:, 3 * (i % 2) + c, 0:n], Q[:, i * P:(i + 1) * P],
                                           KH[:, 512 * c:512 * c + n], start=True, stop=True)
                        mm.then_inc(score, 1)
                    if i:
                        back(i - 1)

        def roots(act, h, i):
            a, n = QCH[i] if i < 3 else CHUNKS[i - 3]
            M, R = (HD, RQ) if i < 3 else (NOPE, RK)
            act.wait_ge(ss, h * 6 + i + 1)
            if i == 0:
                act.wait_ge(qk, h)
            act.activation(R[:, a:a + n], PS[0:M, 6 + i % 2, 0:n], ACT.Sqrt, bias=K[0:M, C_EPS:C_EPS + 1]
                           ).then_inc(root, 1)

        def copy_turned(eng, i, g, G_, copy):
            j0, j1 = 4 * g, min(4 * g + 4, blocks(i))
            full = min(j1, blocks(i) - 1)
            if full > j0:
                ins = copy(PT[:, j0:full, :], PS[:, 6, 0:(full - j0) * P].rearrange("p (a b) -> p a b", b=P))
            if full < j1:
                ins = copy(PT[0:META, full, :], PS[0:META, 6, (full % 4) * P:(full % 4 + 1) * P])
            return ins

        @block.scalar
        def _(act):
            with act.Fori(0, NH) as h:
                for i in range(6):
                    n = QCH[i][1] if i < 3 else CHUNKS[i - 3][1]
                    M = HD if i < 3 else NOPE
                    act.wait_ge(qraw if i < 3 else kraw, h * 3 + i % 3 + 1)
                    if i >= 2:
                        act.wait_ge(ss, h * 6 + i - 1)
                    act.activation(SQ[0:M, i % 2, 0:n], PS[0:M, i, 0:n], ACT.Square).then_inc(sq_ready, 1)
                    if i:
                        roots(act, h, i - 1)
                roots(act, h, 5)
                act.wait_ge(vraw, h + 1)
                act.activation(V[:, 0:8, :].rearrange("p a b -> p (a b)"), PS[:, 6, :], ACT.Copy)
                act.activation(V[0:META, 8, :], PS[0:META, 7, 0:VH], ACT.Copy).then_inc(vset, 1)

                def back(i):
                    for g in range(groups(i)):
                        G_ = before(i) + g
                        if G_ % 2:
                            continue
                        act.wait_ge(turned, h * GR + G_ + 1)
                        copy_turned(act, i, g, G_, lambda o, x: act.activation(o, x, ACT.Copy)).then_inc(pt_act, 1)
                    act.wait_ge(ot, h * NQ + i + 1)
                    if i == 0:
                        act.wait_ge(stored, h * 16)
                    act.activation(AT[:, i * P:(i + 1) * P], PS[0:VH, 7, P:2 * P], ACT.Copy).then_inc(oT, 1)

                for i in range(NQ + 1):
                    if i < NQ:
                        act.wait_ge(negmax, h * NQ + i + 1)
                        if i >= 2:
                            act.wait_ge(pv, h * NQ + i - 1)
                        ps = PS[:, 3 * (i % 2):3 * (i % 2) + 3, :].rearrange("p a b -> p (a b)")
                        act.activation(PR[:, i % 2, 0:nkeys(i)], ps[:, 0:nkeys(i)], ACT.Exp,
                                       bias=NM[:, i:i + 1], scale=SCALE, accum_out=SM[:, i:i + 1]).then_inc(probs, 1)
                    if i:
                        back(i - 1)

        @block.vector
        def _(dve):
            dve.wait_ge(small_in, 16)
            dve.tensor_copy(KH[NOPE:HD, :], KR[NOPE:HD, :]).then_inc(small_in, 1)
            dve.wait_ge(small_in, 17)
            with dve.Fori(0, NH) as h:
                at = h * STEPS
                dve.wait_ge(root, h * 6 + 6)
                dve.reciprocal(RQ[:], RQ[:]).then_inc(step, 1)
                dve.reciprocal(RK[:], RK[:]).then_inc(step, 1)
                dve.wait_ge(step, at + 2)
                for c, (a, n) in enumerate(QCH):
                    ins = dve.scalar_tensor_tensor(Q[:, a:a + n], PS[0:HD, c, 0:n], G[0:HD, 0:1], RQ[:, a:a + n],
                                                   ALU.mult, ALU.mult)
                ins.then_inc(step, 1)
                for c, (a, n) in enumerate(CHUNKS):
                    ins = dve.scalar_tensor_tensor(KH[0:NOPE, a:a + n], PS[0:NOPE, 3 + c, 0:n], G[0:NOPE, 1:2],
                                                   RK[:, a:a + n], ALU.mult, ALU.mult)
                ins.then_inc(step, 1)
                dve.wait_ge(step, at + 4)
                dve.memset(PAD[:], 0.0)
                r = slice(NOPE, HD)
                rope(dve, Q[r, :], Q[r, :], SW[r, :], CS, META, TQ, step, at + 4, r)
                dve.wait_ge(step, at + 8)
                dve.tensor_scalar(QG[:], Q[0:NOPE, SEQ:TQ], G[0:NOPE, 1:2], None, ALU.mult)
                dve.tensor_copy(QRS[:, :, bass.ds(h, 1), :].rearrange("p s h q -> p s (h q)"),
                                Q[r, SEQ:TQ].rearrange("p (s q) -> p s q", q=DSEQ)).then_inc(qk, 1)
                dve.wait_ge(qabs, h + 1)
                for k in range(KT):
                    ins = dve.tensor_copy(QABS[:, k, :, bass.ds(h, 1), :].rearrange("p s h q -> p s (h q)"),
                                          PS[:, 7, k * NS:(k + 1) * NS].rearrange("p (s q) -> p s q", q=DSEQ))
                ins.then_inc(qabs_set, 1)

                def front(i):
                    b = at + 8 + 2 * i
                    ps = PS[:, 3 * (i % 2):3 * (i % 2) + 3, :].rearrange("p a b -> p (a b)")
                    n = nkeys(i)
                    dve.wait_ge(score, h * NQ + i + 1)
                    m = ps[:, n - P - META:n]
                    dve.tensor_tensor(m, m, K[:, C_MASK:C_MASK + P + META], ALU.add).then_inc(step, 1)
                    dve.wait_ge(step, b + 1)
                    dve.tensor_reduce(MX[:, i:i + 1], ps[:, 0:n], AX.X, ALU.max).then_inc(step, 1)
                    dve.wait_ge(step, b + 2)
                    dve.tensor_scalar(NM[:, i:i + 1], MX[:, i:i + 1], -SCALE, None, ALU.mult).then_inc(negmax, 1)

                def back(i):
                    dve.wait_ge(probs, h * NQ + i + 1)
                    dve.reciprocal(RI[:, i:i + 1], SM[:, i:i + 1]).then_inc(inv, 1)
                    for g in range(groups(i)):
                        G_ = before(i) + g
                        if G_ % 2 == 0:
                            continue
                        dve.wait_ge(turned, h * GR + G_ + 1)
                        copy_turned(dve, i, g, G_, lambda o, x: dve.tensor_copy(o, x)).then_inc(pt_dve, 1)
                    dve.wait_ge(pv, h * NQ + i + 1)
                    dve.wait_ge(inv, h * NQ + i + 1)
                    dve.tensor_scalar(O[:, i % 2, :], PS[:, 7, 0:VH], RI[:, i:i + 1], None, ALU.mult
                                      ).then_inc(oset, 1)

                for i in range(NQ + 1):
                    if i < NQ:
                        front(i)
                    if i:
                        back(i - 1)


def decode_stage(nc, K, CKV, QABS, QRS, OLAT, d):
    with ExitStack() as ctx:
        sb = lambda n, s, dt=F32: ctx.enter_context(nc.sbuf_tensor("dc_" + n, s, dt))
        sem = lambda n: ctx.enter_context(nc.semaphore("dc_" + n))
        PTB = sb("pages", [1, NSEQ * NPG], I32)
        C = sb("c", [P, 2, NPG, KVL])
        R = sb("r", [P, 2, NPG, ROPE])
        CT_ = sb("cT", [P, KT, SK])
        RT_ = sb("rT", [ROPE, SK])
        WK = sb("wuk", [P, KT, NH * NOPE])
        WV = sb("wuv", [P, KT, NH * VH])
        QA = sb("qa", [P, KT, NS])
        QR = sb("qr", [ROPE, NS])
        SQ = sb("sq", [P, 2, 512])
        RS = sb("rs", [NS, SK])
        L = sb("l", [NS, SK])
        PR = sb("p", [NS, SK])
        PT = sb("pt", [P, NPG + 1, NS])
        CN = sb("cn", [DSEQ, KVL])
        ST = sb("st", [NS, 4])
        AS = sb("as", [VH, NH, NS])
        PS = ctx.enter_context(nc.psum_tensor("dc_ps", [P, 8, 512], F32))
        page_in = [sem(f"page_in{s}") for s in range(2)]
        (tbl_in, w_in, newk, turned, ct, kraw, sq, ss, root, sc, step, expo, probs, pturn, pt, ol, olset, av, stored) = (
            sem(n) for n in ("tbl_in", "w_in", "newk", "turned", "ct", "kraw", "sq", "ss", "root", "sc", "step",
                             "expo", "probs", "pturn", "pt", "ol", "olset", "av", "stored"))
        block = ctx.enter_context(nc.Block())
        CK = [(0, 512), (512, 512), (PAST, DSEQ)]
        TB = 6
        STEPS = 13
        NF = NH * NOPE // P

        @block.sync
        def _(sp):
            sp.dma_start(PTB[:], d["pages"]).then_inc(tbl_in, 16)
            sp.dma_start(WK[:], d["w_uk"]).then_inc(w_in, 16)
            sp.dma_start(WV[:], d["w_uv"]).then_inc(w_in, 16)
            sp.wait_ge(tbl_in, 16)
            with sp.Fori(0, NSEQ // 2) as o:
                for s in range(2):
                    sp.wait_ge(ol, 2 * o)
                    for j in range(NPG):
                        page = sp.value_load(PTB[0:1, bass.ds((o * 2 + s) * NPG + j, 1)], min_val=0,
                                             max_val=d["cache"].shape[0] - 1)
                        sp.dma_start(C[:, s, j, :], d["cache"][bass.ds(page, 1)].rearrange("o p n -> (o p) n")
                                     ).then_inc(page_in[s], 16)
                        sp.dma_start(R[:, s, j, :], d["krope"][bass.ds(page, 1)].rearrange("o p n -> (o p) n")
                                     ).then_inc(page_in[s], 16)
            sp.wait_ge(av, 2)
            sp.dma_start(d["s_attn"][:, :, SEQ:TQ].rearrange("h p n -> p h n"), AS[:]).then_inc(stored, 16)
            sp.wait_ge(stored, 16)

        @block.tensor
        def _(pe):
            pe.wait_ge(w_in, 32)
            I_ = K[:, C_ID:C_ID + P]
            with pe.Fori(0, NSEQ // 2) as o:
                for s in range(2):
                    q = o * 2 + s
                    pe.wait_ge(w_in, 32)
                    pe.wait_ge(page_in[s], (o + 1) * NPG * 32)
                    for b in range(TB):
                        pe.wait_ge(w_in, 32)
                        if b >= 2:
                            pe.wait_ge(ct, q * TB + b - 1)
                        if b < 4:
                            k, half = b // 2, b % 2
                            for j in range(4):
                                mm = pe.transpose(PS[:, b % 2, j * P:(j + 1) * P],
                                                  C[:, s, half * 4 + j, k * P:(k + 1) * P], I_)
                        else:
                            for j in range(4):
                                mm = pe.transpose(PS[0:ROPE, b % 2, j * P:(j + 1) * P],
                                                  R[:, s, (b - 4) * 4 + j, :], I_)
                        mm.then_inc(turned, 1)
                    pe.wait_ge(ct, q * TB + TB)
                    pe.wait_ge(newk, q + 1)
                    for c, (a, n) in enumerate(CK):
                        if c:
                            pe.wait_ge(step, q * STEPS + 3 * c)
                        for k in range(KT):
                            pe.matmul(PS[0:NS, 5, 0:n], QA[:, k, :], CT_[:, k, a:a + n],
                                      start=(k == 0), stop=(k == KT - 1))
                        pe.matmul(PS[0:NS, 6, 0:n], QR[:], RT_[:, a:a + n], start=True, stop=True).then_inc(sc, 1)
                        for f in range(NF + 1):
                            if f < NF:
                                g = NF * c + f
                                if g >= 2:
                                    pe.wait_ge(sq, q * 3 * NF + g - 1)
                                for k in range(KT):
                                    mm = pe.matmul(PS[:, g % 2, 0:n], WK[:, k, f * P:(f + 1) * P],
                                                   CT_[:, k, a:a + n], start=(k == 0), stop=(k == KT - 1))
                                mm.then_inc(kraw, 1)
                            if f:
                                g = NF * c + f - 1
                                pe.wait_ge(sq, q * 3 * NF + g + 1)
                                if c and f == 1:
                                    pe.wait_ge(root, q * 3 + c)
                                mm = pe.matmul(PS[0:NS, 4, 0:n], K[:, C_SEL + (f - 1) * NS:C_SEL + f * NS],
                                               SQ[:, g % 2, 0:n], start=(f == 1), stop=(f == NF))
                                mm.then_inc(ss, 1)
                    for k in range(KT):
                        mm = pe.transpose(PS[0:DSEQ, 2, k * P:(k + 1) * P], CT_[:, k, PAST:SK], I_)
                    pe.wait_ge(w_in, 32)
                    pe.wait_ge(probs, q + 1)
                    for j in range(NPG):
                        pe.transpose(PS[:, 3, j * NS:(j + 1) * NS], PR[:, j * P:(j + 1) * P], K[0:NS, C_ID:C_ID + NS])
                    pe.transpose(PS[0:DSEQ, 3, NPG * NS:(NPG + 1) * NS], PR[:, PAST:SK], K[0:NS, C_ID:C_ID + NS]
                                 ).then_inc(pturn, 1)
                    pe.wait_ge(pt, q + 1)
                    pe.wait_ge(olset, q)
                    for k in range(KT):
                        for j in range(NPG + 1):
                            if j < NPG:
                                lhs, rhs = C[:, s, j, k * P:(k + 1) * P], PT[:, j, :]
                            else:
                                lhs, rhs = CN[:, k * P:(k + 1) * P], PT[0:DSEQ, j, :]
                            mm = pe.matmul(PS[:, 7, k * NS:(k + 1) * NS], lhs, rhs,
                                           start=(j == 0), stop=(j == NPG), skip_group_check=True)
                    mm.then_inc(ol, 1)
            pe.wait_ge(olset, NSEQ)
            for h in range(NH):
                for k in range(KT):
                    mm = pe.matmul(PS[0:VH, 0, h * NS:(h + 1) * NS], WV[:, k, h * VH:(h + 1) * VH],
                                   OLAT[:, k, h].rearrange("p s q -> p (s q)"), start=(k == 0), stop=(k == KT - 1),
                                   skip_group_check=True)
            mm.then_inc(av, 1)

        @block.scalar
        def _(act):
            with act.Fori(0, NSEQ // 2) as o:
                for s in range(2):
                    q = o * 2 + s
                    act.wait_ge(pt, q)
                    for b in range(TB):
                        act.wait_ge(turned, q * TB + b + 1)
                        if b < 4:
                            out = CT_[:, b // 2, (b % 2) * 512:(b % 2 + 1) * 512]
                            act.activation(out, PS[:, b % 2, :], ACT.Copy).then_inc(ct, 1)
                        else:
                            out = RT_[:, (b - 4) * 512:(b - 3) * 512]
                            act.activation(out, PS[0:ROPE, b % 2, :], ACT.Copy).then_inc(ct, 1)
                    for c, (a, n) in enumerate(CK):
                        for f in range(NF):
                            g = NF * c + f
                            act.wait_ge(kraw, q * 3 * NF + g + 1)
                            if g >= 2:
                                act.wait_ge(ss, q * 3 * NF + g - 1)
                            act.activation(SQ[:, g % 2, 0:n], PS[:, g % 2, 0:n], ACT.Square).then_inc(sq, 1)
                        act.wait_ge(ss, q * 3 * NF + NF * (c + 1))
                        act.activation(RS[:, a:a + n], PS[0:NS, 4, 0:n], ACT.Sqrt, bias=K[0:NS, C_EPS:C_EPS + 1]
                                       ).then_inc(root, 1)
                    act.wait_ge(step, q * STEPS + 12)
                    act.activation(PR[:], L[:], ACT.Exp, bias=ST[:, 1:2], scale=SCALE, accum_out=ST[:, 2:3]
                                   ).then_inc(expo, 1)
                    act.wait_ge(ol, q + 1)
                    for k in range(KT):
                        ins = act.activation(OLAT[:, k, :, bass.ds(q, 1), :].rearrange("p h s q -> p h (s q)"),
                                             PS[:, 7, k * NS:(k + 1) * NS].rearrange("p (h q) -> p h q", q=DSEQ),
                                             ACT.Copy)
                    ins.then_inc(olset, 1)
            act.wait_ge(av, 1)
            act.activation(AS[:].rearrange("p h n -> p (h n)"), PS[0:VH, 0, 0:NH * NS], ACT.Copy).then_inc(av, 1)

        @block.vector
        def _(dve):
            with dve.Fori(0, NSEQ // 2) as o:
                for s in range(2):
                    q = o * 2 + s
                    at = q * STEPS
                    dve.wait_ge(ol, q)
                    a = META + SEQ + q * DSEQ
                    dve.tensor_copy(CT_[:, :, PAST:SK], CKV[:, :, bass.ds(a, DSEQ)])
                    dve.tensor_copy(RT_[:, PAST:SK], d["KR"][0:ROPE, bass.ds(a, DSEQ)])
                    dve.tensor_copy(QA[:], QABS[:, :, bass.ds(q, 1)].rearrange("p k s h q -> p k (s h q)"))
                    dve.tensor_copy(QR[:], QRS[:, bass.ds(q, 1)].rearrange("p s h q -> p (s h q)")).then_inc(newk, 1)
                    for c, (a, n) in enumerate(CK):
                        dve.wait_ge(root, q * 3 + c + 1)
                        dve.reciprocal(RS[:, a:a + n], RS[:, a:a + n]).then_inc(step, 1)
                        dve.wait_ge(step, at + 3 * c + 1)
                        dve.wait_ge(sc, q * 3 + c + 1)
                        dve.tensor_tensor(L[:, a:a + n], PS[0:NS, 5, 0:n], RS[:, a:a + n], ALU.mult).then_inc(step, 1)
                        dve.wait_ge(step, at + 3 * c + 2)
                        dve.tensor_tensor(L[:, a:a + n], PS[0:NS, 6, 0:n], L[:, a:a + n], ALU.add).then_inc(step, 1)
                    dve.wait_ge(step, at + 9)
                    m = L[:, PAST:SK]
                    dve.tensor_tensor(m, m, K[0:NS, C_SMASK:C_SMASK + DSEQ], ALU.add).then_inc(step, 1)
                    dve.wait_ge(step, at + 10)
                    dve.tensor_reduce(ST[:, 0:1], L[:], AX.X, ALU.max).then_inc(step, 1)
                    dve.wait_ge(step, at + 11)
                    dve.tensor_scalar(ST[:, 1:2], ST[:, 0:1], -SCALE, None, ALU.mult).then_inc(step, 1)
                    dve.wait_ge(expo, q + 1)
                    dve.reciprocal(ST[:, 3:4], ST[:, 2:3]).then_inc(step, 1)
                    dve.wait_ge(step, at + 13)
                    dve.tensor_scalar(PR[:], PR[:], ST[:, 3:4], None, ALU.mult).then_inc(probs, 1)
                    dve.wait_ge(pturn, q + 1)
                    dve.tensor_copy(CN[:], PS[0:DSEQ, 2, 0:KVL])
                    dve.tensor_copy(PT[:, 0:NPG, :].rearrange("p a b -> p (a b)"), PS[:, 3, 0:NPG * NS])
                    dve.tensor_copy(PT[0:DSEQ, NPG, :], PS[0:DSEQ, 3, NPG * NS:(NPG + 1) * NS]).then_inc(pt, 1)


def merge_stage(nc, H, YC, M, d):
    with ExitStack() as ctx:
        sb = lambda n, s, dt=F32: ctx.enter_context(nc.sbuf_tensor("mg_" + n, s, dt))
        sem = lambda n: ctx.enter_context(nc.semaphore("mg_" + n))
        NB = 2 * KD + 2 * CT
        W = sb("w", [P, 2, NB, P])
        A = sb("a", [P, CT, TQ])
        S = sb("s", [P, 2, 2, 352])
        PS = ctx.enter_context(nc.psum_tensor("mg_ps", [P, 2, 4, 512], F32))
        w_in = [sem(f"w_in{s}") for s in range(2)]
        a_in, proj, gates, step, done = (sem(n) for n in ("a_in", "proj", "gates", "step", "done"))
        block = ctx.enter_context(nc.Block())

        @block.sync
        def _(sp):
            for s in range(2):
                sp.dma_start(W[:, s], d["w_merge"][s]).then_inc(w_in[s], 16)
            for k in range(CT):
                sp.dma_start(A[:, k, :], d["s_attn"][2 * k:2 * k + 2].rearrange("a p n -> (a p) n")
                             ).then_inc(a_in, 16)
            with sp.Fori(0, KD // 2 - 1) as o:
                for s in range(2):
                    sp.wait_ge(proj, o * 6 + 3 * (s + 1))
                    sp.dma_start(W[:, s], d["w_merge"][bass.ds(o * 2 + s + 2, 1)].rearrange("o p b n -> (o p) b n")
                                 ).then_inc(w_in[s], 16)

        @block.tensor
        def _(pe):
            pe.wait_ge(a_in, 16 * CT)
            with pe.Fori(0, KD // 2) as o:
                for s in range(2):
                    pe.wait_ge(w_in[s], (o + 1) * 16)
                    for c, (a, n) in enumerate(QCH):
                        g = 3 * s + c
                        pe.wait_ge(done, o * 6 + g - 1) if g >= 2 else pe.wait_ge(done, o * 6)
                        at = 0
                        for m, (x, nk, lo) in enumerate(((H, KD, META), (H, KD, META), (YC, CT, 0), (A, CT, 0))):
                            for k in range(nk):
                                mm = pe.matmul(PS[:, g % 2, m, 0:n], W[:, s, at + k, :], x[:, k, lo + a:lo + a + n],
                                               start=(k == 0), stop=(k == nk - 1))
                            at += nk
                        mm.then_inc(proj, 1)

        @block.scalar
        def _(act):
            with act.Fori(0, KD // 2) as o:
                for g in range(6):
                    act.wait_ge(proj, o * 6 + g + 1)
                    act.wait_ge(done, o * 6 + g - 1) if g >= 2 else act.wait_ge(done, o * 6)
                    n = 352
                    act.activation(S[:, g % 2, :, :], PS[:, g % 2, 0:2, 0:n], ACT.Sigmoid).then_inc(gates, 1)

        @block.vector
        def _(dve):
            with dve.Fori(0, KD // 2) as o:
                for g in range(6):
                    a, n = QCH[g % 3]
                    dve.wait_ge(gates, o * 6 + g + 1)
                    dve.tensor_tensor(S[:, g % 2, :, :], PS[:, g % 2, 2:4, 0:n], S[:, g % 2, :, :], ALU.mult
                                      ).then_inc(step, 1)
                    dve.wait_ge(step, o * 6 + g + 1)
                    out = M[:, bass.ds(o * 2 + g // 3, 1), a:a + n].rearrange("p a n -> p (a n)")
                    dve.tensor_tensor(out, S[:, g % 2, 0, :], S[:, g % 2, 1, :], ALU.add).then_inc(done, 1)


def mix_stage(nc, X, M, d):
    with ExitStack() as ctx:
        sem = lambda n: ctx.enter_context(nc.semaphore("mx_" + n))
        W = ctx.enter_context(nc.sbuf_tensor("mx_w", [P, 2, KD, P], F32))
        PS = ctx.enter_context(nc.psum_tensor("mx_ps", [P, 6, 512], F32))
        w_in = [sem(f"w_in{s}") for s in range(2)]
        proj, done = sem("proj"), sem("done")
        block = ctx.enter_context(nc.Block())

        @block.sync
        def _(sp):
            for s in range(2):
                sp.dma_start(W[:, s], d["w_mix"][s]).then_inc(w_in[s], 16)
            with sp.Fori(0, KD // 2 - 1) as o:
                for s in range(2):
                    sp.wait_ge(proj, o * 6 + 3 * (s + 1))
                    sp.dma_start(W[:, s], d["w_mix"][bass.ds(o * 2 + s + 2, 1)].rearrange("o p b n -> (o p) b n")
                                 ).then_inc(w_in[s], 16)

        @block.tensor
        def _(pe):
            with pe.Fori(0, KD // 2) as o:
                for s in range(2):
                    pe.wait_ge(w_in[s], (o + 1) * 16)
                    if s == 0:
                        pe.wait_ge(done, o * 6)
                    for c, (a, n) in enumerate(QCH):
                        for k in range(KD):
                            mm = pe.matmul(PS[:, 3 * s + c, 0:n], W[:, s, k, :], M[:, k, a:a + n],
                                           start=(k == 0), stop=(k == KD - 1))
                        mm.then_inc(proj, 1)

        @block.vector
        def _(dve):
            with dve.Fori(0, KD // 2) as o:
                for g in range(6):
                    a, n = QCH[g % 3]
                    x = X[:, bass.ds(o * 2 + g // 3, 1), META + a:META + a + n].rearrange("p a n -> p (a n)")
                    dve.wait_ge(proj, o * 6 + g + 1)
                    dve.tensor_tensor(x, PS[:, g, 0:n], x, ALU.add).then_inc(done, 1)


def topk_stage(nc, H, VAL, IDX, d):
    with ExitStack() as ctx:
        sb = lambda n, s, dt=F32: ctx.enter_context(nc.sbuf_tensor("tk_" + n, s, dt))
        sem = lambda n: ctx.enter_context(nc.semaphore("tk_" + n))
        W = sb("w", [P, 2, KD + 1, P])
        QS = sb("q", [P, TQ])
        S = sb("s", [TT, 2, NT, NK])
        S2 = sb("s2", [TT, NT, NK])
        PAD = sb("pad", [1, 1])
        TV = sb("tv", [TT, NT, TOPK])
        TI = sb("ti", [TT, NT, TOPK], U32)
        PQ = ctx.enter_context(nc.psum_tensor("tk_pq", [P, 3, 512], F32))
        PS = ctx.enter_context(nc.psum_tensor("tk_ps", [P, 3, 512], F32))
        w_in = [sem(f"w_in{s}") for s in range(2)]
        proj, qset, score, sset, step = (sem(n) for n in ("proj", "qset", "score", "sset", "step"))
        block = ctx.enter_context(nc.Block())
        STEPS = 6

        @block.sync
        def _(sp):
            for s in range(2):
                sp.dma_start(W[:, s], d["w_peer"][s]).then_inc(w_in[s], 16)
            with sp.Fori(0, PH - 1) as h:
                for s in range(2):
                    sp.wait_ge(score, h * 2 + s + 1)
                    sp.dma_start(W[:, s], d["w_peer"][bass.ds(h * 2 + s + 2, 1)].rearrange("o p b n -> (o p) b n")
                                 ).then_inc(w_in[s], 16)

        @block.tensor
        def _(pe):
            with pe.Fori(0, PH) as h:
                for s in range(2):
                    q = h * 2 + s
                    pe.wait_ge(w_in[s], (h + 1) * 16)
                    pe.wait_ge(qset, q)
                    for c, (a, n) in enumerate(QCH):
                        for k in range(KD):
                            mm = pe.matmul(PQ[:, c, 0:n], W[:, s, k, :], H[:, k, META + a:META + a + n],
                                           start=(k == 0), stop=(k == KD - 1))
                    mm.then_inc(proj, 1)
                    pe.wait_ge(qset, q + 1)
                    pe.wait_ge(sset, q)
                    for t in range(NT):
                        mm = pe.matmul(PS[0:TT, t // 4, (t % 4) * NK:(t % 4 + 1) * NK], QS[:, t * TT:(t + 1) * TT],
                                       W[:, s, KD, :], start=True, stop=True, skip_group_check=True)
                    mm.then_inc(score, 1)

        @block.scalar
        def _(act):
            with act.Fori(0, PH) as h:
                for s in range(2):
                    q = h * 2 + s
                    act.wait_ge(proj, q + 1)
                    act.wait_ge(score, q)
                    for c, (a, n) in enumerate(QCH):
                        ins = act.activation(QS[:, a:a + n], PQ[:, c, 0:n], ACT.Copy)
                    ins.then_inc(qset, 1)
                    act.wait_ge(score, q + 1)
                    act.wait_ge(step, h * 2 * STEPS)
                    for c, (t, n) in enumerate(TILES):
                        ins = act.activation(S[:, s, t:t + n, :].rearrange("p a b -> p (a b)"),
                                             PS[0:TT, c, 0:n * NK], ACT.Copy)
                    ins.then_inc(sset, 1)

        @block.vector
        def _(dve):
            with dve.Fori(0, PH) as h:
                for s in range(2):
                    q = h * 2 + s
                    at = q * STEPS
                    val = lambda t, a: TV[:, t, a:a + 8]
                    idx = lambda t, a: TI[:, t, a:a + 8]
                    dve.wait_ge(sset, q + 1)
                    dve.wait_ge(step, at)
                    dve.memset(PAD[:], 0.0)
                    for t in range(NT):
                        ins = dve.max(val(t, 0), S[:, s, t, :])
                    ins.then_inc(step, 1)
                    dve.wait_ge(step, at + 1)
                    dve.memset(PAD[:], 0.0)
                    for t in range(NT):
                        ins = dve.max_index(idx(t, 0), val(t, 0), S[:, s, t, :])
                    ins.then_inc(step, 1)
                    for t in range(NT):
                        ins = dve.match_replace(S2[:, t, :], val(t, 0), S[:, s, t, :], -3e38)
                    ins.then_inc(step, 1)
                    dve.wait_ge(step, at + 3)
                    dve.memset(PAD[:], 0.0)
                    for t in range(NT):
                        ins = dve.max(val(t, 8), S2[:, t, :])
                    ins.then_inc(step, 1)
                    dve.wait_ge(step, at + 4)
                    dve.memset(PAD[:], 0.0)
                    for t in range(NT):
                        ins = dve.max_index(idx(t, 8), val(t, 8), S2[:, t, :])
                    ins.then_inc(step, 1)
                    dve.wait_ge(step, at + 5)
                    dve.tensor_copy(VAL[:, :, bass.ds(q, 1), :].rearrange("p t a b -> p t (a b)"), TV[:])
                    dve.tensor_copy(IDX[:, :, bass.ds(q, 1), :].rearrange("p t a b -> p t (a b)"), TI[:]
                                    ).then_inc(step, 1)


def route_stage(nc, K, VAL, IDX, d):
    with ExitStack() as ctx:
        sb = lambda n, s, dt=F32: ctx.enter_context(nc.sbuf_tensor("rt_" + n, s, dt))
        sem = lambda n: ctx.enter_context(nc.semaphore("rt_" + n))
        PP = TOPK * TOPK
        CA = sb("cand", [TT, PH, PP])
        CB = sb("cand2", [TT, PH, PP])
        B = sb("best", [TT, PH, TOPK])
        PI = sb("pos", [TT, 2, PICK], U32)
        PF = sb("posf", [TT, 2, PICK])
        PW = sb("poswhole", [TT, PICK], U32)
        IF = sb("idxf", [TT, HC, TOPK])
        EQ = sb("eq", [TT, PICK, TOPK])
        SEL = sb("sel", [TT, 3, PICK])
        PAD = sb("pad", [1, 1])
        SM = sb("sum", [TT, PH])
        TR = sb("tr", [P, 3, TT])
        TB = 8
        NBT = TT // TB
        O1 = sb("one1", [P, 2, TB, NK])
        O2 = sb("one2", [P, 2, TB, NK])
        OG = sb("one2g", [P, 2, TB, NK])
        STG = sb("stage", [P, NK, TT])
        PS = ctx.enter_context(nc.psum_tensor("rt_ps", [P, 4, 512], F32))
        PT = ctx.enter_context(nc.psum_tensor("rt_pt", [P, 512], F32))
        (expo, sel_ready, turned, tr, one1, two, one2, gm, gset, step, bstep, stored) = (
            sem(n) for n in ("expo", "sel_ready", "turned", "tr", "one1", "two", "one2", "gm", "gset", "step", "bstep",
                             "stored"))
        block = ctx.enter_context(nc.Block())
        STEPS = 12

        @block.sync
        def _(sp):
            with sp.Fori(0, NT) as t:
                sp.wait_ge(gset, (t + 1) * NBT)
                sp.dma_start(d["s_route"][bass.ds(t, 1)].rearrange("o p n -> (o p) n"),
                             STG[:].rearrange("p a b -> p (a b)")).then_inc(stored, 16)
            sp.wait_ge(stored, 16 * NT)

        @block.tensor
        def _(pe):
            with pe.Fori(0, NT) as t:
                pe.wait_ge(sel_ready, t + 1)
                pe.wait_ge(tr, t)
                for i in range(3):
                    mm = pe.transpose(PT[:, i * TT:(i + 1) * TT], SEL[:, i, :], K[0:TT, C_ID:C_ID + TT])
                mm.then_inc(turned, 1)
                with pe.Fori(0, NBT // 2) as b:
                    for s in range(2):
                        n = t * NBT + b * 2 + s
                        pe.wait_ge(one1, n + 1)
                        pe.wait_ge(one2, n + 1)
                        if s == 0:
                            pe.wait_ge(gset, n)
                        for j in range(TB):
                            mm = pe.matmul(PS[:, 2 * s + j // 4, (j % 4) * NK:(j % 4 + 1) * NK], O1[:, s, j, :],
                                           OG[:, s, j, :], start=True, stop=True, skip_group_check=True)
                        mm.then_inc(gm, 1)

        @block.scalar
        def _(act):
            with act.Fori(0, NT) as t:
                act.wait_ge(step, t * STEPS + 10)
                act.activation(SEL[:, 2, :], SEL[:, 2, :], ACT.Exp).then_inc(expo, 1)
                act.wait_ge(turned, t + 1)
                act.wait_ge(gm, t * NBT)
                act.activation(TR[:].rearrange("p a b -> p (a b)"), PT[:, 0:3 * TT], ACT.Copy).then_inc(tr, 1)
                act.wait_ge(stored, t * 16)
                with act.Fori(0, NBT // 2) as b:
                    for s in range(2):
                        n = t * NBT + b * 2 + s
                        act.wait_ge(gm, n + 1)
                        for i in range(2):
                            tok = (b * 2 + s) * TB + 4 * i
                            ins = act.activation(STG[:, :, bass.ds(tok, 4)].rearrange("p i t -> p t i"),
                                                 PS[:, 2 * s + i, :].rearrange("p (t i) -> p t i", i=NK), ACT.Copy)
                        ins.then_inc(gset, 1)

        @block.vector
        def _(dve):
            io = K[:, C_IOTA:C_IOTA + NK].unsqueeze(1).to_broadcast([P, TB, NK])
            io16 = K[0:TT, C_IOTA:C_IOTA + TOPK].unsqueeze(1).to_broadcast([TT, PICK, TOPK])
            with dve.Fori(0, NT) as t:
                at = t * STEPS
                v = VAL[:, bass.ds(t, 1)].rearrange("p a (h c) k -> p (a h) c k", c=2)
                ca = CA[:].rearrange("p h (a b) -> p h a b", b=TOPK)
                dve.tensor_tensor(ca, v[:, :, 0, :].unsqueeze(3).to_broadcast([TT, PH, TOPK, TOPK]),
                                  v[:, :, 1, :].unsqueeze(2).to_broadcast([TT, PH, TOPK, TOPK]), ALU.add
                                  ).then_inc(step, 1)
                dve.tensor_copy(IF[:], IDX[:, bass.ds(t, 1)].rearrange("p a h k -> p (a h) k")).then_inc(step, 1)
                dve.wait_ge(step, at + 2)
                dve.memset(PAD[:], 0.0)
                for h in range(PH):
                    ins = dve.max(B[:, h, 0:8], CA[:, h, :])
                ins.then_inc(step, 1)
                dve.wait_ge(step, at + 3)
                dve.memset(PAD[:], 0.0)
                for h in range(PH):
                    dve.max_index(PW[:, h * TOPK:h * TOPK + 8], B[:, h, 0:8], CA[:, h, :])
                    ins = dve.match_replace(CB[:, h, :], B[:, h, 0:8], CA[:, h, :], -3e38)
                ins.then_inc(step, 1)
                dve.wait_ge(step, at + 4)
                dve.memset(PAD[:], 0.0)
                for h in range(PH):
                    ins = dve.max(B[:, h, 8:16], CB[:, h, :])
                ins.then_inc(step, 1)
                dve.wait_ge(step, at + 5)
                dve.memset(PAD[:], 0.0)
                for h in range(PH):
                    ins = dve.max_index(PW[:, h * TOPK + 8:(h + 1) * TOPK], B[:, h, 8:16], CB[:, h, :])
                ins.then_inc(step, 1)
                dve.wait_ge(step, at + 6)
                dve.tensor_scalar(PI[:, 0, :], PW[:], 4, None, ALU.logical_shift_right).then_inc(step, 1)
                dve.tensor_scalar(PI[:, 1, :], PW[:], TOPK - 1, None, ALU.bitwise_and).then_inc(step, 1)
                dve.wait_ge(step, at + 8)
                dve.tensor_copy(PF[:], PI[:]).then_inc(step, 1)
                dve.wait_ge(turned, t)
                ifv = IF[:].rearrange("p (h c) k -> p h c k", c=2)
                for c in range(2):
                    eq = EQ[:].rearrange("p (h j) k -> p h j k", h=PH)
                    dve.wait_ge(step, at + 9) if c == 0 else dve.wait_ge(bstep, t * 6 + 3)
                    dve.tensor_tensor(EQ[:], PF[:, c, :].unsqueeze(2).to_broadcast([TT, PICK, TOPK]), io16,
                                      ALU.is_equal).then_inc(bstep, 1)
                    dve.wait_ge(bstep, (t * 2 + c) * 3 + 1)
                    dve.tensor_tensor(eq, eq, ifv[:, :, c, :].unsqueeze(2).to_broadcast([TT, PH, TOPK, TOPK]),
                                      ALU.mult).then_inc(bstep, 1)
                    dve.wait_ge(bstep, (t * 2 + c) * 3 + 2)
                    dve.tensor_reduce(SEL[:, c, :], EQ[:], AX.X, ALU.add).then_inc(bstep, 1)
                w = SEL[:, 2, :].rearrange("p (h k) -> p h k", h=PH)
                dve.tensor_tensor(w, B[:], B[:, :, 0:1].to_broadcast([TT, PH, TOPK]), ALU.subtract).then_inc(step, 1)
                dve.wait_ge(expo, t + 1)
                dve.tensor_reduce(SM[:], w, AX.X, ALU.add).then_inc(step, 1)
                dve.wait_ge(step, at + 11)
                dve.reciprocal(SM[:], SM[:]).then_inc(step, 1)
                dve.wait_ge(step, at + 12)
                dve.tensor_tensor(w, w, SM[:].unsqueeze(2).to_broadcast([TT, PH, TOPK]), ALU.mult
                                  ).then_inc(sel_ready, 1)
                with dve.Fori(0, NBT // 2) as b:
                    dve.wait_ge(tr, t + 1)
                    for s in range(2):
                        n = t * NBT + b * 2 + s
                        if s == 0:
                            dve.wait_ge(gm, t * NBT + b * 2)
                        x = lambda i: TR[:, i, bass.ds((b * 2 + s) * TB, TB)].unsqueeze(2).to_broadcast([P, TB, NK])
                        dve.tensor_tensor(O1[:, s], io, x(0), ALU.is_equal).then_inc(one1, 1)
                        dve.tensor_tensor(O2[:, s], io, x(1), ALU.is_equal).then_inc(two, 1)
                        dve.wait_ge(two, n + 1)
                        dve.tensor_tensor(OG[:, s], O2[:, s], x(2), ALU.mult).then_inc(one2, 1)


def expert_stage(nc, X, H, d):
    with ExitStack() as ctx:
        sb = lambda n, s, dt=F32: ctx.enter_context(nc.sbuf_tensor("ex_" + n, s, dt))
        sem = lambda n: ctx.enter_context(nc.semaphore("ex_" + n))
        U = sb("u", [P, 2, KD, P])
        V = sb("v", [P, 2, GRP, D])
        R = sb("r", [P, 2, NT, GRP, TT])
        W = sb("w", [P, GRP, TQ])
        G = sb("g", [P, 2, 4 * TT])
        PA = ctx.enter_context(nc.psum_tensor("ex_pa", [P, 4, 512], F32))
        PO = ctx.enter_context(nc.psum_tensor("ex_po", [P, 4, 512], F32))
        u_in = [sem(f"u_in{s}") for s in range(2)]
        v_in = [sem(f"v_in{s}") for s in range(2)]
        r_in = [sem(f"r_in{s}") for s in range(2)]
        a_mm, gelu, w_set, o_mm, o_set, stored = (
            sem(n) for n in ("a_mm", "gelu", "w_set", "o_mm", "o_set", "stored"))
        block = ctx.enter_context(nc.Block())
        NG = NK // GRP
        NC = 3 * GRP
        NO = 3 * KD
        CH = [(t * TT, n * TT) for t, n in TILES]

        @block.sync
        def _(sp):
            with sp.Fori(0, NG // 2) as o:
                for s in range(2):
                    g = o * 2 + s
                    sp.wait_ge(w_set, o * 2 * NC)
                    sp.dma_start(R[:, s].rearrange("p t g n -> p t (g n)"),
                                 d["s_route4"][:, :, bass.ds(g * (GRP * TT), GRP * TT)]).then_inc(r_in[s], 16)
                    for b in range(GRP):
                        if b == 2:
                            sp.wait_ge(o_mm, o * 2 * NO)
                            sp.dma_start(V[:, s].rearrange("p g n -> p (g n)"),
                                         d["v"][:, bass.ds(g * (GRP * D), GRP * D)]).then_inc(v_in[s], 16)
                        sp.wait_ge(a_mm, g * NC + 3 * (b - 1) if b >= 2 else g * NC)
                        sp.dma_start(U[:, b % 2], d["u"][bass.ds(g * GRP + b, 1)].rearrange("o p k n -> (o p) k n")
                                     ).then_inc(u_in[b % 2], 16)
            sp.wait_ge(o_set, NG * NO)
            sp.dma_start(d["o_y"], X[:, :, META:T]).then_inc(stored, 16)
            sp.wait_ge(stored, 16)

        @block.tensor
        def _(pe):
            with pe.Fori(0, NG // 2) as o:
                for s in range(2):
                    g = o * 2 + s
                    for b in range(GRP):
                        pe.wait_ge(u_in[b % 2], (g * (GRP // 2) + b // 2 + 1) * 16)
                        for c, (a, n) in enumerate(CH):
                            j = 3 * b + c
                            pe.wait_ge(gelu, g * NC + j - 3) if j >= 4 else pe.wait_ge(gelu, g * NC)
                            for k in range(KD):
                                mm = pe.matmul(PA[:, j % 4, 0:n], U[:, b % 2, k, :],
                                               H[:, k, META + a:META + a + n], start=(k == 0), stop=(k == KD - 1))
                            mm.then_inc(a_mm, 1)
                    pe.wait_ge(w_set, (g + 1) * NC)
                    pe.wait_ge(v_in[s], (o + 1) * 16)
                    for j in range(NO):
                        k, c = j // 3, j % 3
                        a, n = CH[c]
                        pe.wait_ge(o_set, g * NO + j - 3) if j >= 4 else pe.wait_ge(o_set, g * NO)
                        for b in range(GRP):
                            mm = pe.matmul(PO[:, j % 4, 0:n], V[:, s, b, k * P:(k + 1) * P], W[:, b, a:a + n],
                                           start=(b == 0), stop=(b == GRP - 1))
                        mm.then_inc(o_mm, 1)

        @block.scalar
        def _(act):
            with act.Fori(0, NG) as g:
                for j in range(NC):
                    a, n = CH[j % 3]
                    act.wait_ge(a_mm, g * NC + j + 1)
                    act.wait_ge(w_set, g * NC + j - 1) if j >= 2 else act.wait_ge(w_set, g * NC)
                    act.activation(G[:, j % 2, 0:n], PA[:, j % 4, 0:n], ACT.Gelu).then_inc(gelu, 1)

        @block.vector
        def _(dve):
            with dve.Fori(0, NG // 2) as o:
                for s in range(2):
                    g = o * 2 + s
                    dve.wait_ge(r_in[s], (o + 1) * 16)
                    for j in range(NC):
                        a, n = CH[j % 3]
                        t, nt = TILES[j % 3]
                        dve.wait_ge(gelu, g * NC + j + 1)
                        if j == 0:
                            dve.wait_ge(o_mm, g * NO)
                        v3 = lambda x: x.rearrange("p (t n) -> p t n", n=TT)
                        dve.tensor_tensor(v3(W[:, j // 3, a:a + n]), v3(G[:, j % 2, 0:n]),
                                          R[:, s, t:t + nt, j // 3, :], ALU.mult).then_inc(w_set, 1)
                    for j in range(NO):
                        k, c = j // 3, j % 3
                        a, n = CH[c]
                        x = X[:, k, META + a:META + a + n]
                        dve.wait_ge(o_mm, g * NO + j + 1)
                        dve.tensor_tensor(x, PO[:, j % 4, 0:n], x, ALU.add).then_inc(o_set, 1)


def build(nc, d):
    with ExitStack() as ctx:
        X = ctx.enter_context(nc.sbuf_tensor("X", [P, KD, T], F32))
        H = ctx.enter_context(nc.sbuf_tensor("H", [P, KD, T], F32))
        K = ctx.enter_context(nc.sbuf_tensor("K", [P, C_ALL], F32))
        const_in = ctx.enter_context(nc.semaphore("const_in"))
        with nc.Block() as block:
            @block.sync
            def _(sp):
                sp.dma_start(K[:], d["const"]).then_inc(const_in, 16)
                sp.wait_ge(const_in, 16)
        norm_stage(nc, "n1_", X, H, K, d["g_mix"], d["x"])
        with ExitStack() as mid:
            YC = mid.enter_context(nc.sbuf_tensor("YC", [P, CT, TQ], F32))
            conv_stage(nc, H, YC, d)
            with ExitStack() as at:
                QABS = at.enter_context(nc.sbuf_tensor("QABS", [P, KT, NSEQ, NH, DSEQ], F32))
                QRS = at.enter_context(nc.sbuf_tensor("QRS", [ROPE, NSEQ, NH, DSEQ], F32))
                CKV = at.enter_context(nc.sbuf_tensor("CKV", [P, KT, T], F32))
                KR = at.enter_context(nc.sbuf_tensor("KR", [P, T], F32))
                d["KR"] = KR
                with ExitStack() as hd:
                    CQ = hd.enter_context(nc.sbuf_tensor("CQ", [P, QT, T], F32))
                    CS = hd.enter_context(nc.sbuf_tensor("CS", [P, 2, T], F32))
                    latent_stage(nc, H, K, CQ, CKV, KR, CS, d)
                    head_stage(nc, K, CQ, CKV, KR, CS, QABS, QRS, d)
                OLAT = at.enter_context(nc.sbuf_tensor("OLAT", [P, KT, NH, NSEQ, DSEQ], F32))
                decode_stage(nc, K, CKV, QABS, QRS, OLAT, d)
            M = mid.enter_context(nc.sbuf_tensor("M", [P, KD, TQ], F32))
            merge_stage(nc, H, YC, M, d)
            mix_stage(nc, X, M, d)
        norm_stage(nc, "n2_", X, H, K, d["g_ffn"])
        with ExitStack() as pk:
            VAL = pk.enter_context(nc.sbuf_tensor("VAL", [TT, NT, HC, TOPK], F32))
            IDX = pk.enter_context(nc.sbuf_tensor("IDX", [TT, NT, HC, TOPK], U32))
            topk_stage(nc, H, VAL, IDX, d)
            route_stage(nc, K, VAL, IDX, d)
        expert_stage(nc, X, H, d)


def constants():
    K = np.zeros((P, C_ALL), np.float32)
    r = np.arange(P)
    K[:, C_ONES:C_ONES + P] = 1
    K[:, C_MEAN:C_MEAN + P] = 1 / D
    K[:, C_KV:C_KV + P] = 1 / KVL
    K[:, C_R32:C_R32 + P] = (r[:, None] // ROPE == r[None] // ROPE) / ROPE
    K[:NOPE, C_HEAD:C_HEAD + NOPE] = 1 / NOPE
    K[NOPE:HD, C_HEAD + NOPE:C_HEAD + HD] = 1 / ROPE
    K[:, C_ID:C_ID + P] = np.eye(P)
    for f in range(4):
        K[:, C_SEL + f * NS:C_SEL + (f + 1) * NS] = ((2 * f + r[:, None] // NOPE) == np.arange(NS)[None] // DSEQ) / NOPE
    K[:, C_MASK:C_MASK + P + META] = np.where(np.arange(P + META)[None] <= r[:, None] + META, 0, NEG)
    K[:NS, C_SMASK:C_SMASK + DSEQ] = np.where(np.arange(DSEQ)[None] <= np.arange(NS)[:, None] % DSEQ, 0, NEG)
    K[:, C_IOTA:C_IOTA + P] = r[None]
    K[:, C_EPS] = EPS
    pos = np.concatenate([np.arange(KEYS), np.tile(PAST + np.arange(DSEQ), NSEQ)]).astype(np.float32)
    freq = np.float32(10000.0) ** (-np.arange(0, ROPE, 2, dtype=np.float32) / np.float32(ROPE))
    ang = pos[None, :] * freq[:, None]
    c, s = np.cos(ang).astype(np.float32), np.sin(ang).astype(np.float32)
    cs = np.stack([np.tile(np.concatenate([c, c]), (4, 1)), np.tile(np.concatenate([-s, s]), (4, 1))], 1)
    return K, np.ascontiguousarray(cs)


def kernel(**inputs):
    import concourse.bacc as bacc
    from concourse.bass_utils import run_bass_kernel_spmd

    a = {k: np.asarray(v) for k, v in inputs.items()}
    K, cs = constants()
    tiles = lambda w: w.reshape(-1, P, w.shape[1]).transpose(1, 0, 2)
    blocks = lambda w: w.reshape(w.shape[0] // P, P, -1, P).transpose(2, 1, 0, 3)
    w_in = a["w_in"][0]
    edges = np.cumsum([0, CW, CW, CW, QL, KVL, ROPE, D, D])
    wB, wC, wX, wQ, wKV, wKR, wGC, wGA = (w_in[:, edges[i]:edges[i + 1]] for i in range(8))
    cols = lambda g: g.reshape(-1, P).T
    gq = np.concatenate([a["g_q_nope"][0], a["g_q_rope"][0]])
    g_head = np.zeros((P, 3), np.float32)
    g_head[:HD, 0] = gq
    g_head[:NOPE, 1] = a["g_k_nope"][0]
    uq, uk, uv = a["w_uq"][0], a["w_uk"][0], a["w_uv"][0]
    per_head = lambda w: w.reshape(-1, P, NH, w.shape[-1]).transpose(2, 1, 0, 3).reshape(NH, P, -1)
    feeds = {
        "const": K,
        "cossin": cs,
        "x": tiles(np.concatenate([a["meta_tokens"], a["x_prompt"][0], a["x_sample"].reshape(NS, D)]).T),
        "g_mix": cols(a["norm_mix"][0]),
        "g_ffn": cols(a["norm_ffn"][0]),
        "w_conv": np.stack([blocks(wB), blocks(wC), blocks(wX)], 1),
        "taps": a["conv_w"][0].reshape(3, CT, P).transpose(2, 1, 0),
        "state": a["state_conv"][0].reshape(NSEQ, 2, CT, P).transpose(3, 2, 0, 1),
        "w_lat": np.concatenate([blocks(wQ), blocks(wKV), blocks(np.tile(wKR, (1, 4)))]),
        "g_lat": np.concatenate([cols(a["g_q_lat"][0]), cols(a["g_kv_lat"][0]),
                                 np.tile(a["g_k_rope"][0], 4)[:, None]], 1),
        "g_head": g_head,
        "w_head": np.concatenate([per_head(uq), per_head(uk), per_head(uv)], 2),
        "w_ukT": uk.transpose(1, 2, 0),
        "w_uk": tiles(uk.reshape(KVL, -1)),
        "w_uv": tiles(uv.reshape(KVL, -1)),
        "pages": a["page_table"].reshape(1, -1),
        "cache": a["cache_ckv"][0],
        "krope": a["cache_krope"][0],
        "w_merge": np.concatenate([blocks(wGC), blocks(wGA), blocks(a["w_conv_out"][0]),
                                   blocks(a["w_attn_out"][0])], 2),
        "w_mix": blocks(a["w_mix_out"][0]),
        "w_peer": np.concatenate([blocks(a["w_peer_q"][0]), a["peer_sub_keys"][0].transpose(1, 0, 3, 2).reshape(
            HC, P, 1, NK)], 2),
        "u": a["peer_u"][0].reshape(NK, NK, KD, P).transpose(1, 3, 2, 0),
        "v": a["peer_v"][0].reshape(NK, NK * D),
    }
    nc = bacc.Bacc("TRN2", target_bir_lowering=False, num_devices=1)
    arrays, d = {}, {}
    for name, x in feeds.items():
        x = np.ascontiguousarray(x)
        arrays["in_" + name] = x
        d[name] = nc.dram_tensor("in_" + name, x.shape, mybir.dt.from_np(x.dtype), kind="ExternalInput").ap()
    outs = {"o_y": (P, KD, TQ), "o_ckv": (P, KT, T), "o_kr": (ROPE, T), "o_convp": (P, CT, 2),
            "o_convs": (P, CT, NSEQ, 2)}
    for name, shape in outs.items():
        d[name] = nc.dram_tensor(name, shape, F32, kind="ExternalOutput").ap()
    s_attn = nc.dram_tensor("s_attn", (NH, VH, TQ), F32)
    d["s_attn"] = s_attn.ap()
    s_route = nc.dram_tensor("s_route", (NT, P, NK * TT), F32)
    d["s_route"] = s_route.ap()
    d["s_route4"] = s_route.ap().rearrange("t p n -> p t n")
    build(nc, d)
    r = run_bass_kernel_spmd(nc, [arrays], core_ids=[0]).results[0]
    y = r["o_y"].transpose(2, 1, 0).reshape(TQ, D)
    ckv = r["o_ckv"].transpose(2, 1, 0).reshape(T, KVL)
    kr = r["o_kr"].T
    return (
        y[:SEQ].reshape(1, SEQ, D), y[SEQ:].reshape(NSEQ, DSEQ, D),
        ckv[:KEYS].reshape(1, 1, KEYS, KVL), kr[:KEYS].reshape(1, 1, KEYS, ROPE),
        r["o_convp"].transpose(2, 1, 0).reshape(1, 1, 2, CW),
        ckv[KEYS:].reshape(1, NSEQ, DSEQ, KVL), kr[KEYS:].reshape(1, NSEQ, DSEQ, ROPE),
        r["o_convs"].transpose(2, 3, 1, 0).reshape(1, NSEQ, 2, CW),
    )
```

```python
from contextlib import ExitStack

import numpy as np

import concourse.bass as bass
from concourse import mybir

F32 = mybir.dt.float32
F32R = mybir.dt.float32r
U32 = mybir.dt.uint32
I32 = mybir.dt.int32
ALU = mybir.AluOpType
ACT = mybir.ActivationFunctionType
AX = mybir.AxisListType

P = 128
D = 1024
KD = D // P
META, SEQ = 16, 1024
NSEQ, DSEQ = 8, 4
NS = NSEQ * DSEQ
T = META + SEQ + NS
KEYS = META + SEQ
TQ = SEQ + NS
CW = 512
CT = CW // P
QL, KVL, ROPE, NOPE, VH, NH = 384, 256, 32, 64, 64, 8
QT, KT = QL // P, KVL // P
HD = NOPE + ROPE
SCALE = float(HD) ** -0.5
PAST, PAGE = 1024, 128
NPG = PAST // PAGE
SK = PAST + DSEQ
NEG = -1e30
PH, NK, TOPK = 8, 128, 16
HC = PH * 2
TT = 96
NT = TQ // TT
PICK = PH * TOPK
EPS = 1e-6
CHUNKS = [(0, 360), (360, 360), (720, 352)]
QCH = [(0, 352), (352, 352), (704, 352)]
GRP = 2
TILES = [(0, 4), (4, 4), (8, 3)]

C_ONES = 0
C_MEAN = C_ONES + P
C_KV = C_MEAN + P
C_R32 = C_KV + P
C_HEAD = C_R32 + P
C_ID = C_HEAD + P
C_SEL = C_ID + P
C_MASK = C_SEL + 4 * NS
C_SMASK = C_MASK + P + META
C_IOTA = C_SMASK + DSEQ
C_EPS = C_IOTA + P
C_ALL = C_EPS + 1


def norm_stage(nc, tag, X, H, K, g_dram, x_dram=None, h_dram=None):
    with ExitStack() as ctx:
        sb = lambda n, s, d=F32: ctx.enter_context(nc.sbuf_tensor(tag + n, s, d))
        sem = lambda n: ctx.enter_context(nc.semaphore(tag + n))
        G = sb("gain", [P, KD])
        SQ = sb("sq", [P, 2, T])
        RT = sb("root", [P, T])
        SS = ctx.enter_context(nc.psum_tensor(tag + "ss", [P, 3, 512], F32))
        gain_in, sq_ready, sq_used, root_ready, inv_ready, h_ready, stored = (
            sem(n) for n in ("gain_in", "sq_ready", "sq_used", "root_ready", "inv_ready", "h_ready", "stored"))
        x_in = [sem(f"x_in{k}") for k in range(KD)] if x_dram is not None else None
        block = ctx.enter_context(nc.Block())

        @block.sync
        def _(sp):
            if x_dram is not None:
                for k in range(KD):
                    sp.dma_start(X[:, k, :], x_dram[:, k, :]).then_inc(x_in[k], 16)
            sp.dma_start(G[:], g_dram).then_inc(gain_in, 16)
            if h_dram is not None:
                sp.wait_ge(h_ready, KD)
                sp.dma_start(h_dram, H[:, :, META:T]).then_inc(stored, 16)
                sp.wait_ge(stored, 16)

        @block.scalar
        def _(act):
            for k in range(KD):
                if x_dram is not None:
                    act.wait_ge(x_in[k], 16)
                if k >= 2:
                    act.wait_ge(sq_used, k - 1)
                act.activation(SQ[:, k % 2, :], X[:, k, :], ACT.Square).then_inc(sq_ready, 1)
            act.wait_ge(sq_used, KD)
            for c, (a, n) in enumerate(CHUNKS):
                act.activation(RT[:, a:a + n], SS[:, c, 0:n], ACT.Sqrt,
                               bias=K[:, C_EPS:C_EPS + 1]).then_inc(root_ready, 1)

        @block.tensor
        def _(pe):
            for k in range(KD):
                pe.wait_ge(sq_ready, k + 1)
                for c, (a, n) in enumerate(CHUNKS):
                    mm = pe.matmul(SS[:, c, 0:n], K[:, C_MEAN:C_MEAN + P], SQ[:, k % 2, a:a + n],
                                   start=(k == 0), stop=(k == KD - 1))
                mm.then_inc(sq_used, 1)

        @block.vector
        def _(dve):
            for c, (a, n) in enumerate(CHUNKS):
                dve.wait_ge(root_ready, c + 1)
                dve.reciprocal(RT[:, a:a + n], RT[:, a:a + n]).then_inc(inv_ready, 1)
            dve.wait_ge(inv_ready, 3)
            dve.wait_ge(gain_in, 16)
            for k in range(KD):
                dve.scalar_tensor_tensor(H[:, k, :], X[:, k, :], G[:, k:k + 1], RT[:],
                                         ALU.mult, ALU.mult).then_inc(h_ready, 1)
            dve.wait_ge(h_ready, KD)


def conv_stage(nc, H, YC, d):
    with ExitStack() as ctx:
        sb = lambda n, s, dt=F32: ctx.enter_context(nc.sbuf_tensor("cv_" + n, s, dt))
        sem = lambda n: ctx.enter_context(nc.semaphore("cv_" + n))
        W = sb("w", [P, 2, 3, KD, P])
        U = sb("u", [P, T])
        US = sb("us", [P, NSEQ, 2 + DSEQ])
        BS = sb("b", [P, T])
        XS = sb("xin", [P, 2, 360])
        Y = sb("y", [P, TQ])
        CWT = sb("taps", [P, CT, 3])
        ST = sb("state", [P, CT, NSEQ, 2])
        NP_ = sb("newp", [P, CT, 2])
        NS_ = sb("news", [P, CT, NSEQ, 2])
        PS = ctx.enter_context(nc.psum_tensor("cv_ps", [P, 2, 3, 512], F32))
        w_in = [sem(f"w_in{s}") for s in range(2)]
        small_in, proj, copied, u_part, chan_done, step, stored = (
            sem(n) for n in ("small_in", "proj", "copied", "u_part", "chan_done", "step", "stored"))
        block = ctx.enter_context(nc.Block())
        STEPS = 10

        @block.sync
        def _(sp):
            sp.dma_start(CWT[:], d["taps"]).then_inc(small_in, 16)
            sp.dma_start(ST[:], d["state"]).then_inc(small_in, 16)
            for s in range(2):
                sp.dma_start(W[:, s], d["w_conv"][s].rearrange("a p k n -> p a k n")).then_inc(w_in[s], 16)
            with sp.Fori(0, CT // 2 - 1) as o:
                for s in range(2):
                    sp.wait_ge(proj, o * 6 + 3 * (s + 1))
                    sp.dma_start(W[:, s], d["w_conv"][bass.ds(o * 2 + s + 2, 1)].rearrange(
                        "o a p k n -> (o p) a k n")).then_inc(w_in[s], 16)
            sp.wait_ge(chan_done, CT)
            sp.dma_start(d["o_convp"], NP_[:]).then_inc(stored, 16)
            sp.dma_start(d["o_convs"], NS_[:]).then_inc(stored, 16)
            sp.wait_ge(stored, 32)

        @block.tensor
        def _(pe):
            with pe.Fori(0, CT // 2) as o:
                for s in range(2):
                    pe.wait_ge(w_in[s], (o + 1) * 16)
                    for c, (a, n) in enumerate(CHUNKS):
                        g = 3 * s + c
                        if g >= 2:
                            pe.wait_ge(u_part, o * 6 + g - 1)
                        else:
                            pe.wait_ge(u_part, o * 6)
                        for m in range(3):
                            for k in range(KD):
                                mm = pe.matmul(PS[:, g % 2, m, 0:n], W[:, s, m, k, :], H[:, k, a:a + n],
                                               start=(k == 0), stop=(k == KD - 1))
                        mm.then_inc(proj, 1)

        @block.scalar
        def _(act):
            with act.Fori(0, CT // 2) as o:
                for s in range(2):
                    for c, (a, n) in enumerate(CHUNKS):
                        g = 3 * s + c
                        act.wait_ge(proj, o * 6 + g + 1)
                        if c == 0:
                            act.wait_ge(chan_done, o * 2 + s)
                        if g >= 2:
                            act.wait_ge(u_part, o * 6 + g - 1)
                        else:
                            act.wait_ge(u_part, o * 6)
                        act.activation(BS[:, a:a + n], PS[:, g % 2, 0, 0:n], ACT.Copy)
                        act.activation(XS[:, g % 2, 0:n], PS[:, g % 2, 2, 0:n], ACT.Copy).then_inc(copied, 1)

        @block.vector
        def _(dve):
            dve.wait_ge(small_in, 32)
            with dve.Fori(0, CT // 2) as o:
                for s in range(2):
                    c_ = o * 2 + s
                    at = c_ * STEPS
                    for c, (a, n) in enumerate(CHUNKS):
                        dve.wait_ge(copied, o * 6 + 3 * s + c + 1)
                        dve.tensor_tensor(U[:, a:a + n], PS[:, (3 * s + c) % 2, 1, 0:n],
                                          XS[:, (3 * s + c) % 2, 0:n], ALU.mult).then_inc(u_part, 1)
                    dve.wait_ge(u_part, c_ * 3 + 3)
                    tap = lambda k: CWT[:, bass.ds(c_, 1), k:k + 1].rearrange("p a k -> p (a k)")
                    us = U[:, META + SEQ:T].rearrange("p (s q) -> p s q", q=DSEQ)
                    dve.tensor_copy(US[:, :, 2:], us).then_inc(step, 1)
                    dve.tensor_copy(US[:, :, 0:2], ST[:, bass.ds(c_, 1)].rearrange("p a s k -> p (a s) k")
                                    ).then_inc(step, 1)
                    dve.tensor_copy(NP_[:, bass.ds(c_, 1), :].rearrange("p a k -> p (a k)"),
                                    U[:, META + SEQ - 2:META + SEQ]).then_inc(step, 1)
                    dve.tensor_scalar(Y[:, 0:SEQ], U[:, META - 2:META - 2 + SEQ], tap(0), None, ALU.mult
                                      ).then_inc(step, 1)
                    dve.wait_ge(step, at + 4)
                    dve.tensor_copy(NS_[:, bass.ds(c_, 1)].rearrange("p a s k -> p (a s) k"),
                                    US[:, :, DSEQ:]).then_inc(step, 1)
                    dve.scalar_tensor_tensor(Y[:, 0:SEQ], U[:, META - 1:META - 1 + SEQ], tap(1), Y[:, 0:SEQ],
                                             ALU.mult, ALU.add).then_inc(step, 1)
                    ys = Y[:, SEQ:TQ].rearrange("p (s q) -> p s q", q=DSEQ)
                    dve.tensor_scalar(ys, US[:, :, 0:DSEQ], tap(0), None, ALU.mult).then_inc(step, 1)
                    dve.wait_ge(step, at + 7)
                    dve.scalar_tensor_tensor(Y[:, 0:SEQ], U[:, META:META + SEQ], tap(2), Y[:, 0:SEQ],
                                             ALU.mult, ALU.add).then_inc(step, 1)
                    dve.scalar_tensor_tensor(ys, US[:, :, 1:1 + DSEQ], tap(1), ys, ALU.mult, ALU.add
                                             ).then_inc(step, 1)
                    dve.wait_ge(step, at + 9)
                    dve.scalar_tensor_tensor(ys, US[:, :, 2:2 + DSEQ], tap(2), ys, ALU.mult, ALU.add
                                             ).then_inc(step, 1)
                    dve.wait_ge(step, at + 10)
                    dve.tensor_tensor(YC[:, bass.ds(c_, 1), :].rearrange("p a t -> p (a t)"), Y[:],
                                      BS[:, META:T], ALU.mult).then_inc(chan_done, 1)


def rope(dve, out, x, swapped, CS, a, n, step, at, rows=slice(0, P)):
    r = rows
    dve.stream_shuffle(swapped, x, [(i + 16) % 32 for i in range(32)]).then_inc(step, 1)
    dve.wait_ge(step, at + 1)
    dve.tensor_tensor(swapped, swapped, CS[r, 1, a:a + n], ALU.mult).then_inc(step, 1)
    dve.tensor_tensor(out, x, CS[r, 0, a:a + n], ALU.mult).then_inc(step, 1)
    dve.wait_ge(step, at + 3)
    dve.tensor_tensor(out, out, swapped, ALU.add).then_inc(step, 1)


def latent_stage(nc, H, K, CQ, CKV, KR, CS, d):
    with ExitStack() as ctx:
        sb = lambda n, s, dt=F32: ctx.enter_context(nc.sbuf_tensor("lt_" + n, s, dt))
        sem = lambda n: ctx.enter_context(nc.semaphore("lt_" + n))
        NB = QT + KT + 1
        W = sb("w", [P, 2, KD, P])
        SQ = sb("sq", [P, 2, T])
        RT = sb("root", [P, 3, T])
        G = sb("gains", [P, NB])
        SW = sb("swap", [P, T])
        PS = ctx.enter_context(nc.psum_tensor("lt_ps", [P, 3, 512], F32))
        SS = ctx.enter_context(nc.psum_tensor("lt_ss", [P, 3, 512], F32))
        w_in = [sem(f"w_in{s}") for s in range(2)]
        small_in, proj, lat, sq_ready, sq_used, root, step, stored = (
            sem(n) for n in ("small_in", "proj", "lat", "sq_ready", "sq_used", "root", "step", "stored"))
        block = ctx.enter_context(nc.Block())
        dst = [CQ[:, i, :] for i in range(QT)] + [CKV[:, i, :] for i in range(KT)] + [KR[:, :]]
        first = {0: 0, 1: 0, 2: 0, 3: 1, 4: 1, 5: 2}
        last = {2: 0, 4: 1, 5: 2}
        mean = [C_ONES, C_KV, C_R32]

        @block.sync
        def _(sp):
            sp.dma_start(G[:], d["g_lat"]).then_inc(small_in, 16)
            sp.dma_start(CS[:], d["cossin"]).then_inc(small_in, 16)
            for b in range(NB):
                if b >= 2:
                    sp.wait_ge(proj, b - 1)
                sp.dma_start(W[:, b % 2], d["w_lat"][b]).then_inc(w_in[b % 2], 16)
            sp.wait_ge(step, 13)
            sp.dma_start(d["o_ckv"], CKV[:]).then_inc(stored, 16)
            sp.dma_start(d["o_kr"], KR[0:ROPE, :]).then_inc(stored, 16)
            sp.wait_ge(stored, 32)

        @block.tensor
        def _(pe):
            def squares(b):
                pe.wait_ge(sq_ready, b + 1)
                if b in (3, 5):
                    pe.wait_ge(root, 1 + (b == 5))
                for c, (a, n) in enumerate(CHUNKS):
                    m = mean[first[b]]
                    mm = pe.matmul(SS[:, c, 0:n], K[:, m:m + P], SQ[:, b % 2, a:a + n],
                                   start=(b in (0, 3, 5)), stop=(b in last))
                mm.then_inc(sq_used, 1)

            for b in range(NB):
                pe.wait_ge(w_in[b % 2], 16 * (b // 2 + 1))
                if b:
                    pe.wait_ge(lat, b)
                for c, (a, n) in enumerate(CHUNKS):
                    for k in range(KD):
                        mm = pe.matmul(PS[:, c, 0:n], W[:, b % 2, k, :], H[:, k, a:a + n],
                                       start=(k == 0), stop=(k == KD - 1))
                mm.then_inc(proj, 1)
                if b:
                    squares(b - 1)
            squares(NB - 1)

        @block.scalar
        def _(act):
            def roots(b):
                act.wait_ge(sq_used, b + 1)
                i = last[b]
                for c, (a, n) in enumerate(CHUNKS):
                    ins = act.activation(RT[:, i, a:a + n], SS[:, c, 0:n], ACT.Sqrt, bias=K[:, C_EPS:C_EPS + 1],
                                         scale=1.0 / QL if i == 0 else 1.0)
                ins.then_inc(root, 1)

            for b in range(NB):
                act.wait_ge(proj, b + 1)
                for c, (a, n) in enumerate(CHUNKS):
                    ins = act.activation(dst[b][:, a:a + n], PS[:, c, 0:n], ACT.Copy)
                ins.then_inc(lat, 1)
                act.wait_ge(lat, b + 1)
                if b >= 2:
                    act.wait_ge(sq_used, b - 1)
                act.activation(SQ[:, b % 2, :], dst[b], ACT.Square).then_inc(sq_ready, 1)
                if b - 1 in last:
                    roots(b - 1)
            roots(NB - 1)

        @block.vector
        def _(dve):
            dve.wait_ge(small_in, 32)
            at = 0
            for i, blocks in enumerate(([0, 1, 2], [3, 4], [5])):
                dve.wait_ge(root, i + 1)
                dve.reciprocal(RT[:, i, :], RT[:, i, :]).then_inc(step, 1)
                at += 1
                dve.wait_ge(step, at)
                for b in blocks:
                    dve.scalar_tensor_tensor(dst[b], dst[b], G[:, b:b + 1], RT[:, i, :], ALU.mult, ALU.mult
                                             ).then_inc(step, 1)
                    at += 1
            dve.wait_ge(step, at)
            rope(dve, KR[:, :], KR[:, :], SW[:], CS, 0, T, step, at)
            assert at + 4 == 13
            dve.wait_ge(step, at + 4)


def head_stage(nc, K, CQ, CKV, KR, CS, QABS, QRS, d):
    with ExitStack() as ctx:
        sb = lambda n, s, dt=F32: ctx.enter_context(nc.sbuf_tensor("hd_" + n, s, dt))
        sem = lambda n: ctx.enter_context(nc.semaphore("hd_" + n))
        WQ, WK, WV = 0, QT * HD, QT * HD + KT * NOPE
        WALL = WV + KT * VH
        W = sb("w", [P, WALL])
        WUT = sb("wukT", [NOPE, KVL])
        G = sb("gains", [P, 3])
        SQ = sb("sq", [HD, 2, 360])
        RQ = sb("rq", [HD, TQ])
        RK = sb("rk", [NOPE, T])
        Q = sb("q", [HD, TQ])
        KH = sb("k", [HD, T])
        SW = sb("swap", [HD, TQ])
        QG = sb("qg", [NOPE, NS])
        V = sb("v", [P, 9, VH])
        PR = sb("p", [P, 2, KEYS])
        PT = sb("pt", [P, 10, P])
        PAD = sb("pad", [1, 1])
        MX = sb("mx", [P, 8])
        NM = sb("nm", [P, 8])
        SM = sb("sum", [P, 8])
        RI = sb("ri", [P, 8])
        O = sb("o", [P, 2, VH])
        AT = sb("at", [VH, SEQ])
        PS = ctx.enter_context(nc.psum_tensor("hd_ps", [P, 8, 512], F32))
        (w_in, small_in, qraw, kraw, sq_ready, ss, root, vraw, vset, qabs, qabs_set, qk, step, score, negmax,
         probs, inv, turned, pt_act, pt_dve, pv, oset, ot, oT, stored) = (
            sem(n) for n in ("w_in", "small_in", "qraw", "kraw", "sq_ready", "ss", "root", "vraw", "vset", "qabs",
                             "qabs_set", "qk", "step", "score", "negmax", "probs", "inv", "turned", "pt_act", "pt_dve",
                             "pv", "oset", "ot", "oT", "stored"))
        block = ctx.enter_context(nc.Block())
        NQ = SEQ // P
        nkeys = lambda i: META + P * (i + 1)
        blocks = lambda i: i + 2
        groups = lambda i: (blocks(i) + 3) // 4
        before = lambda i: sum(groups(j) for j in range(i))
        GR = before(NQ)
        even = lambda n: (n + 1) // 2
        odd = lambda n: n // 2
        assert GR % 2 == 0
        STEPS = 8 + 2 * NQ

        @block.sync
        def _(sp):
            sp.dma_start(G[:], d["g_head"]).then_inc(small_in, 16)
            with sp.Fori(0, NH) as h:
                sp.wait_ge(qabs, h)
                sp.dma_start(W[:], d["w_head"][bass.ds(h, 1)].rearrange("o p n -> (o p) n")).then_inc(w_in, 16)
                sp.dma_start(WUT[:], d["w_ukT"][bass.ds(h, 1)].rearrange("o p n -> (o p) n")).then_inc(w_in, 16)
                sp.wait_ge(oT, (h + 1) * NQ)
                sp.dma_start(d["s_attn"][bass.ds(h, 1), :, 0:SEQ].rearrange("o p n -> (o p) n"), AT[:]
                             ).then_inc(stored, 16)
            sp.wait_ge(stored, 16 * NH)

        @block.tensor
        def _(pe):
            with pe.Fori(0, NH) as h:
                pe.wait_ge(w_in, (h + 1) * 32)
                pe.wait_ge(probs, h * NQ)
                pe.wait_ge(oT, h * NQ)
                for c, (a, n) in enumerate(QCH):
                    for k in range(QT):
                        mm = pe.matmul(PS[0:HD, c, 0:n], W[:, WQ + k * HD:WQ + (k + 1) * HD],
                                       CQ[:, k, META + a:META + a + n], start=(k == 0), stop=(k == QT - 1))
                    mm.then_inc(qraw, 1)
                for c, (a, n) in enumerate(CHUNKS):
                    for k in range(KT):
                        mm = pe.matmul(PS[0:NOPE, 3 + c, 0:n], W[:, WK + k * NOPE:WK + (k + 1) * NOPE],
                                       CKV[:, k, a:a + n], start=(k == 0), stop=(k == KT - 1))
                    mm.then_inc(kraw, 1)
                for i in range(6):
                    n = QCH[i][1] if i < 3 else CHUNKS[i - 3][1]
                    R = HD if i < 3 else NOPE
                    pe.wait_ge(sq_ready, h * 6 + i + 1)
                    if i >= 2:
                        pe.wait_ge(root, h * 6 + i - 1)
                    pe.matmul(PS[0:HD, 6 + i % 2, 0:n], K[0:R, C_HEAD:C_HEAD + HD], SQ[0:R, i % 2, 0:n],
                              start=True, stop=True).then_inc(ss, 1)
                pe.wait_ge(root, h * 6 + 6)
                for j in range(9):
                    m = P if j < 8 else META
                    out = PS[0:m, 6, j * VH:(j + 1) * VH] if j < 8 else PS[0:m, 7, 0:VH]
                    for k in range(KT):
                        mm = pe.matmul(out, CKV[:, k, j * P:j * P + m], W[:, WV + k * VH:WV + (k + 1) * VH],
                                       start=(k == 0), stop=(k == KT - 1), skip_group_check=True)
                mm.then_inc(vraw, 1)
                pe.wait_ge(vset, h + 1)
                pe.wait_ge(qk, h + 1)
                for k in range(KT):
                    mm = pe.matmul(PS[:, 7, k * NS:(k + 1) * NS], WUT[:, k * P:(k + 1) * P], QG[:],
                                   start=True, stop=True, skip_group_check=True)
                mm.then_inc(qabs, 1)

                def back(i):
                    pe.wait_ge(w_in, 32)
                    pe.wait_ge(probs, h * NQ + i + 1)
                    if i == 0:
                        pe.wait_ge(qabs_set, h + 1)
                    for g in range(groups(i)):
                        G_ = before(i) + g
                        pe.wait_ge(w_in, 32)
                        if G_:
                            if G_ % 2:
                                pe.wait_ge(pt_act, h * (GR // 2) + even(G_))
                            else:
                                pe.wait_ge(pt_dve, h * (GR // 2) + odd(G_))
                        for j in range(4 * g, min(4 * g + 4, blocks(i))):
                            m = P if j < blocks(i) - 1 else META
                            mm = pe.transpose(PS[0:m, 6, (j % 4) * P:(j % 4 + 1) * P],
                                              PR[:, i % 2, j * P:j * P + m], K[:, C_ID:C_ID + P])
                        mm.then_inc(turned, 1)
                    n = before(i + 1)
                    pe.wait_ge(pt_act, h * (GR // 2) + even(n))
                    if odd(n):
                        pe.wait_ge(pt_dve, h * (GR // 2) + odd(n))
                    if i:
                        pe.wait_ge(oT, h * NQ + i)
                    for j in range(blocks(i)):
                        m = P if j < blocks(i) - 1 else META
                        mm = pe.matmul(PS[:, 7, 0:VH], PT[0:m, j, :], V[0:m, j, :],
                                       start=(j == 0), stop=(j == blocks(i) - 1))
                    mm.then_inc(pv, 1)
                    pe.wait_ge(w_in, 32)
                    pe.wait_ge(oset, h * NQ + i + 1)
                    pe.transpose(PS[0:VH, 7, P:2 * P], O[:, i % 2, :], K[:, C_ID:C_ID + P]).then_inc(ot, 1)

                for i in range(NQ + 1):
                    if i < NQ:
                        if i >= 2:
                            pe.wait_ge(probs, h * NQ + i - 1)
                        for c in range(-(-nkeys(i) // 512)):
                            n = min(512, nkeys(i) - 512 * c)
                            mm = pe.matmul(PS[:, 3 * (i % 2) + c, 0:n], Q[:, i * P:(i + 1) * P],
                                           KH[:, 512 * c:512 * c + n], start=True, stop=True)
                        mm.then_inc(score, 1)
                    if i:
                        back(i - 1)

        def roots(act, h, i):
            a, n = QCH[i] if i < 3 else CHUNKS[i - 3]
            M, R = (HD, RQ) if i < 3 else (NOPE, RK)
            act.wait_ge(ss, h * 6 + i + 1)
            if i == 0:
                act.wait_ge(qk, h)
            act.activation(R[:, a:a + n], PS[0:M, 6 + i % 2, 0:n], ACT.Sqrt, bias=K[0:M, C_EPS:C_EPS + 1]
                           ).then_inc(root, 1)

        def copy_turned(eng, i, g, G_, copy):
            j0, j1 = 4 * g, min(4 * g + 4, blocks(i))
            full = min(j1, blocks(i) - 1)
            if full > j0:
                ins = copy(PT[:, j0:full, :], PS[:, 6, 0:(full - j0) * P].rearrange("p (a b) -> p a b", b=P))
            if full < j1:
                ins = copy(PT[0:META, full, :], PS[0:META, 6, (full % 4) * P:(full % 4 + 1) * P])
            return ins

        @block.scalar
        def _(act):
            with act.Fori(0, NH) as h:
                for i in range(6):
                    n = QCH[i][1] if i < 3 else CHUNKS[i - 3][1]
                    M = HD if i < 3 else NOPE
                    act.wait_ge(qraw if i < 3 else kraw, h * 3 + i % 3 + 1)
                    if i >= 2:
                        act.wait_ge(ss, h * 6 + i - 1)
                    act.activation(SQ[0:M, i % 2, 0:n], PS[0:M, i, 0:n], ACT.Square).then_inc(sq_ready, 1)
                    if i:
                        roots(act, h, i - 1)
                roots(act, h, 5)
                act.wait_ge(vraw, h + 1)
                act.activation(V[:, 0:8, :].rearrange("p a b -> p (a b)"), PS[:, 6, :], ACT.Copy)
                act.activation(V[0:META, 8, :], PS[0:META, 7, 0:VH], ACT.Copy).then_inc(vset, 1)

                def back(i):
                    for g in range(groups(i)):
                        G_ = before(i) + g
                        if G_ % 2:
                            continue
                        act.wait_ge(turned, h * GR + G_ + 1)
                        copy_turned(act, i, g, G_, lambda o, x: act.activation(o, x, ACT.Copy)).then_inc(pt_act, 1)
                    act.wait_ge(ot, h * NQ + i + 1)
                    if i == 0:
                        act.wait_ge(stored, h * 16)
                    act.activation(AT[:, i * P:(i + 1) * P], PS[0:VH, 7, P:2 * P], ACT.Copy).then_inc(oT, 1)

                for i in range(NQ + 1):
                    if i < NQ:
                        act.wait_ge(negmax, h * NQ + i + 1)
                        if i >= 2:
                            act.wait_ge(pv, h * NQ + i - 1)
                        ps = PS[:, 3 * (i % 2):3 * (i % 2) + 3, :].rearrange("p a b -> p (a b)")
                        act.activation(PR[:, i % 2, 0:nkeys(i)], ps[:, 0:nkeys(i)], ACT.Exp,
                                       bias=NM[:, i:i + 1], scale=SCALE, accum_out=SM[:, i:i + 1]).then_inc(probs, 1)
                    if i:
                        back(i - 1)

        @block.vector
        def _(dve):
            dve.wait_ge(small_in, 16)
            dve.tensor_copy(KH[NOPE:HD, :], KR[NOPE:HD, :]).then_inc(small_in, 1)
            dve.wait_ge(small_in, 17)
            with dve.Fori(0, NH) as h:
                at = h * STEPS
                dve.wait_ge(root, h * 6 + 6)
                dve.reciprocal(RQ[:], RQ[:]).then_inc(step, 1)
                dve.reciprocal(RK[:], RK[:]).then_inc(step, 1)
                dve.wait_ge(step, at + 2)
                for c, (a, n) in enumerate(QCH):
                    ins = dve.scalar_tensor_tensor(Q[:, a:a + n], PS[0:HD, c, 0:n], G[0:HD, 0:1], RQ[:, a:a + n],
                                                   ALU.mult, ALU.mult)
                ins.then_inc(step, 1)
                for c, (a, n) in enumerate(CHUNKS):
                    ins = dve.scalar_tensor_tensor(KH[0:NOPE, a:a + n], PS[0:NOPE, 3 + c, 0:n], G[0:NOPE, 1:2],
                                                   RK[:, a:a + n], ALU.mult, ALU.mult)
                ins.then_inc(step, 1)
                dve.wait_ge(step, at + 4)
                dve.memset(PAD[:], 0.0)
                r = slice(NOPE, HD)
                rope(dve, Q[r, :], Q[r, :], SW[r, :], CS, META, TQ, step, at + 4, r)
                dve.wait_ge(step, at + 8)
                dve.tensor_scalar(QG[:], Q[0:NOPE, SEQ:TQ], G[0:NOPE, 1:2], None, ALU.mult)
                dve.tensor_copy(QRS[:, :, bass.ds(h, 1), :].rearrange("p s h q -> p s (h q)"),
                                Q[r, SEQ:TQ].rearrange("p (s q) -> p s q", q=DSEQ)).then_inc(qk, 1)
                dve.wait_ge(qabs, h + 1)
                for k in range(KT):
                    ins = dve.tensor_copy(QABS[:, k, :, bass.ds(h, 1), :].rearrange("p s h q -> p s (h q)"),
                                          PS[:, 7, k * NS:(k + 1) * NS].rearrange("p (s q) -> p s q", q=DSEQ))
                ins.then_inc(qabs_set, 1)

                def front(i):
                    b = at + 8 + 2 * i
                    ps = PS[:, 3 * (i % 2):3 * (i % 2) + 3, :].rearrange("p a b -> p (a b)")
                    n = nkeys(i)
                    dve.wait_ge(score, h * NQ + i + 1)
                    m = ps[:, n - P - META:n]
                    dve.tensor_tensor(m, m, K[:, C_MASK:C_MASK + P + META], ALU.add).then_inc(step, 1)
                    dve.wait_ge(step, b + 1)
                    dve.tensor_reduce(MX[:, i:i + 1], ps[:, 0:n], AX.X, ALU.max).then_inc(step, 1)
                    dve.wait_ge(step, b + 2)
                    dve.tensor_scalar(NM[:, i:i + 1], MX[:, i:i + 1], -SCALE, None, ALU.mult).then_inc(negmax, 1)

                def back(i):
                    dve.wait_ge(probs, h * NQ + i + 1)
                    dve.reciprocal(RI[:, i:i + 1], SM[:, i:i + 1]).then_inc(inv, 1)
                    for g in range(groups(i)):
                        G_ = before(i) + g
                        if G_ % 2 == 0:
                            continue
                        dve.wait_ge(turned, h * GR + G_ + 1)
                        copy_turned(dve, i, g, G_, lambda o, x: dve.tensor_copy(o, x)).then_inc(pt_dve, 1)
                    dve.wait_ge(pv, h * NQ + i + 1)
                    dve.wait_ge(inv, h * NQ + i + 1)
                    dve.tensor_scalar(O[:, i % 2, :], PS[:, 7, 0:VH], RI[:, i:i + 1], None, ALU.mult
                                      ).then_inc(oset, 1)

                for i in range(NQ + 1):
                    if i < NQ:
                        front(i)
                    if i:
                        back(i - 1)


def decode_stage(nc, K, CKV, KR, QABS, QRS, d):
    with ExitStack() as ctx:
        sb = lambda n, s, dt=F32: ctx.enter_context(nc.sbuf_tensor("dc_" + n, s, dt))
        sem = lambda n: ctx.enter_context(nc.semaphore("dc_" + n))
        PTB = sb("pages", [1, NSEQ * NPG], I32)
        C = sb("c", [P, 2, NPG, KVL])
        R = sb("r", [P, 2, NPG, ROPE])
        CT_ = sb("cT", [P, KT, SK])
        RT_ = sb("rT", [ROPE, SK])
        WK = sb("wuk", [P, KT, NH * NOPE])
        WV = sb("wuv", [P, KT, NH * VH])
        QA = sb("qa", [P, KT, NS])
        QR = sb("qr", [ROPE, NS])
        SQ = sb("sq", [P, 2, 512])
        RS = sb("rs", [NS, SK])
        L = sb("l", [NS, SK])
        PR = sb("p", [NS, SK])
        PT = sb("pt", [P, NPG + 1, NS])
        CN = sb("cn", [DSEQ, KVL])
        ST = sb("st", [NS, 4])
        AS = sb("as", [VH, NH, NS])
        OLAT = sb("olat", [P, KT, NH, NSEQ, DSEQ])
        PS = ctx.enter_context(nc.psum_tensor("dc_ps", [P, 8, 512], F32))
        page_in = [sem(f"page_in{s}") for s in range(2)]
        (tbl_in, w_in, newk, turned, ct, kraw, sq, ss, root, sc, step, expo, probs, pturn, pt, ol, olset, av, stored) = (
            sem(n) for n in ("tbl_in", "w_in", "newk", "turned", "ct", "kraw", "sq", "ss", "root", "sc", "step",
                             "expo", "probs", "pturn", "pt", "ol", "olset", "av", "stored"))
        block = ctx.enter_context(nc.Block())
        CK = [(0, 512), (512, 512), (PAST, DSEQ)]
        TB = 6
        STEPS = 13
        NF = NH * NOPE // P

        @block.sync
        def _(sp):
            sp.dma_start(PTB[:], d["pages"]).then_inc(tbl_in, 16)
            sp.dma_start(WK[:], d["w_uk"]).then_inc(w_in, 16)
            sp.dma_start(WV[:], d["w_uv"]).then_inc(w_in, 16)
            sp.wait_ge(tbl_in, 16)
            with sp.Fori(0, NSEQ // 2) as o:
                for s in range(2):
                    sp.wait_ge(ol, 2 * o)
                    for j in range(NPG):
                        page = sp.value_load(PTB[0:1, bass.ds((o * 2 + s) * NPG + j, 1)], min_val=0,
                                             max_val=d["cache"].shape[0] - 1)
                        sp.dma_start(C[:, s, j, :], d["cache"][bass.ds(page, 1)].rearrange("o p n -> (o p) n")
                                     ).then_inc(page_in[s], 16)
                        sp.dma_start(R[:, s, j, :], d["krope"][bass.ds(page, 1)].rearrange("o p n -> (o p) n")
                                     ).then_inc(page_in[s], 16)
            sp.wait_ge(av, 2)
            sp.dma_start(d["s_attn"][:, :, SEQ:TQ].rearrange("h p n -> p h n"), AS[:]).then_inc(stored, 16)
            sp.wait_ge(stored, 16)

        @block.tensor
        def _(pe):
            pe.wait_ge(w_in, 32)
            I_ = K[:, C_ID:C_ID + P]
            with pe.Fori(0, NSEQ // 2) as o:
                for s in range(2):
                    q = o * 2 + s
                    pe.wait_ge(w_in, 32)
                    pe.wait_ge(page_in[s], (o + 1) * NPG * 32)
                    for b in range(TB):
                        pe.wait_ge(w_in, 32)
                        if b >= 2:
                            pe.wait_ge(ct, q * TB + b - 1)
                        if b < 4:
                            k, half = b // 2, b % 2
                            for j in range(4):
                                mm = pe.transpose(PS[:, b % 2, j * P:(j + 1) * P],
                                                  C[:, s, half * 4 + j, k * P:(k + 1) * P], I_)
                        else:
                            for j in range(4):
                                mm = pe.transpose(PS[0:ROPE, b % 2, j * P:(j + 1) * P],
                                                  R[:, s, (b - 4) * 4 + j, :], I_)
                        mm.then_inc(turned, 1)
                    pe.wait_ge(ct, q * TB + TB)
                    pe.wait_ge(newk, q + 1)
                    for c, (a, n) in enumerate(CK):
                        if c:
                            pe.wait_ge(step, q * STEPS + 3 * c)
                        for k in range(KT):
                            pe.matmul(PS[0:NS, 5, 0:n], QA[:, k, :], CT_[:, k, a:a + n],
                                      start=(k == 0), stop=(k == KT - 1))
                        pe.matmul(PS[0:NS, 6, 0:n], QR[:], RT_[:, a:a + n], start=True, stop=True).then_inc(sc, 1)
                        for f in range(NF + 1):
                            if f < NF:
                                g = NF * c + f
                                if g >= 2:
                                    pe.wait_ge(sq, q * 3 * NF + g - 1)
                                for k in range(KT):
                                    mm = pe.matmul(PS[:, g % 2, 0:n], WK[:, k, f * P:(f + 1) * P],
                                                   CT_[:, k, a:a + n], start=(k == 0), stop=(k == KT - 1))
                                mm.then_inc(kraw, 1)
                            if f:
                                g = NF * c + f - 1
                                pe.wait_ge(sq, q * 3 * NF + g + 1)
                                if c and f == 1:
                                    pe.wait_ge(root, q * 3 + c)
                                mm = pe.matmul(PS[0:NS, 4, 0:n], K[:, C_SEL + (f - 1) * NS:C_SEL + f * NS],
                                               SQ[:, g % 2, 0:n], start=(f == 1), stop=(f == NF))
                                mm.then_inc(ss, 1)
                    for k in range(KT):
                        mm = pe.transpose(PS[0:DSEQ, 2, k * P:(k + 1) * P], CT_[:, k, PAST:SK], I_)
                    pe.wait_ge(w_in, 32)
                    pe.wait_ge(probs, q + 1)
                    for j in range(NPG):
                        pe.transpose(PS[:, 3, j * NS:(j + 1) * NS], PR[:, j * P:(j + 1) * P], K[0:NS, C_ID:C_ID + NS])
                    pe.transpose(PS[0:DSEQ, 3, NPG * NS:(NPG + 1) * NS], PR[:, PAST:SK], K[0:NS, C_ID:C_ID + NS]
                                 ).then_inc(pturn, 1)
                    pe.wait_ge(pt, q + 1)
                    pe.wait_ge(olset, q)
                    for k in range(KT):
                        for j in range(NPG + 1):
                            if j < NPG:
                                lhs, rhs = C[:, s, j, k * P:(k + 1) * P], PT[:, j, :]
                            else:
                                lhs, rhs = CN[:, k * P:(k + 1) * P], PT[0:DSEQ, j, :]
                            mm = pe.matmul(PS[:, 7, k * NS:(k + 1) * NS], lhs, rhs,
                                           start=(j == 0), stop=(j == NPG), skip_group_check=True)
                    mm.then_inc(ol, 1)
            pe.wait_ge(olset, NSEQ)
            for h in range(NH):
                for k in range(KT):
                    mm = pe.matmul(PS[0:VH, 0, h * NS:(h + 1) * NS], WV[:, k, h * VH:(h + 1) * VH],
                                   OLAT[:, k, h].rearrange("p s q -> p (s q)"), start=(k == 0), stop=(k == KT - 1),
                                   skip_group_check=True)
            mm.then_inc(av, 1)

        @block.scalar
        def _(act):
            with act.Fori(0, NSEQ // 2) as o:
                for s in range(2):
                    q = o * 2 + s
                    act.wait_ge(pt, q)
                    for b in range(TB):
                        act.wait_ge(turned, q * TB + b + 1)
                        if b < 4:
                            out = CT_[:, b // 2, (b % 2) * 512:(b % 2 + 1) * 512]
                            act.activation(out, PS[:, b % 2, :], ACT.Copy).then_inc(ct, 1)
                        else:
                            out = RT_[:, (b - 4) * 512:(b - 3) * 512]
                            act.activation(out, PS[0:ROPE, b % 2, :], ACT.Copy).then_inc(ct, 1)
                    for c, (a, n) in enumerate(CK):
                        for f in range(NF):
                            g = NF * c + f
                            act.wait_ge(kraw, q * 3 * NF + g + 1)
                            if g >= 2:
                                act.wait_ge(ss, q * 3 * NF + g - 1)
                            act.activation(SQ[:, g % 2, 0:n], PS[:, g % 2, 0:n], ACT.Square).then_inc(sq, 1)
                        act.wait_ge(ss, q * 3 * NF + NF * (c + 1))
                        act.activation(RS[:, a:a + n], PS[0:NS, 4, 0:n], ACT.Sqrt, bias=K[0:NS, C_EPS:C_EPS + 1]
                                       ).then_inc(root, 1)
                    act.wait_ge(step, q * STEPS + 12)
                    act.activation(PR[:], L[:], ACT.Exp, bias=ST[:, 1:2], scale=SCALE, accum_out=ST[:, 2:3]
                                   ).then_inc(expo, 1)
                    act.wait_ge(ol, q + 1)
                    for k in range(KT):
                        ins = act.activation(OLAT[:, k, :, bass.ds(q, 1), :].rearrange("p h s q -> p h (s q)"),
                                             PS[:, 7, k * NS:(k + 1) * NS].rearrange("p (h q) -> p h q", q=DSEQ),
                                             ACT.Copy)
                    ins.then_inc(olset, 1)
            act.wait_ge(av, 1)
            act.activation(AS[:].rearrange("p h n -> p (h n)"), PS[0:VH, 0, 0:NH * NS], ACT.Copy).then_inc(av, 1)

        @block.vector
        def _(dve):
            with dve.Fori(0, NSEQ // 2) as o:
                for s in range(2):
                    q = o * 2 + s
                    at = q * STEPS
                    dve.wait_ge(ol, q)
                    a = META + SEQ + q * DSEQ
                    dve.tensor_copy(CT_[:, :, PAST:SK], CKV[:, :, bass.ds(a, DSEQ)])
                    dve.tensor_copy(RT_[:, PAST:SK], KR[0:ROPE, bass.ds(a, DSEQ)])
                    dve.tensor_copy(QA[:], QABS[:, :, bass.ds(q, 1)].rearrange("p k s h q -> p k (s h q)"))
                    dve.tensor_copy(QR[:], QRS[:, bass.ds(q, 1)].rearrange("p s h q -> p (s h q)")).then_inc(newk, 1)
                    for c, (a, n) in enumerate(CK):
                        dve.wait_ge(root, q * 3 + c + 1)
                        dve.reciprocal(RS[:, a:a + n], RS[:, a:a + n]).then_inc(step, 1)
                        dve.wait_ge(step, at + 3 * c + 1)
                        dve.wait_ge(sc, q * 3 + c + 1)
                        dve.tensor_tensor(L[:, a:a + n], PS[0:NS, 5, 0:n], RS[:, a:a + n], ALU.mult).then_inc(step, 1)
                        dve.wait_ge(step, at + 3 * c + 2)
                        dve.tensor_tensor(L[:, a:a + n], PS[0:NS, 6, 0:n], L[:, a:a + n], ALU.add).then_inc(step, 1)
                    dve.wait_ge(step, at + 9)
                    m = L[:, PAST:SK]
                    dve.tensor_tensor(m, m, K[0:NS, C_SMASK:C_SMASK + DSEQ], ALU.add).then_inc(step, 1)
                    dve.wait_ge(step, at + 10)
                    dve.tensor_reduce(ST[:, 0:1], L[:], AX.X, ALU.max).then_inc(step, 1)
                    dve.wait_ge(step, at + 11)
                    dve.tensor_scalar(ST[:, 1:2], ST[:, 0:1], -SCALE, None, ALU.mult).then_inc(step, 1)
                    dve.wait_ge(expo, q + 1)
                    dve.reciprocal(ST[:, 3:4], ST[:, 2:3]).then_inc(step, 1)
                    dve.wait_ge(step, at + 13)
                    dve.tensor_scalar(PR[:], PR[:], ST[:, 3:4], None, ALU.mult).then_inc(probs, 1)
                    dve.wait_ge(pturn, q + 1)
                    dve.tensor_copy(CN[:], PS[0:DSEQ, 2, 0:KVL])
                    dve.tensor_copy(PT[:, 0:NPG, :].rearrange("p a b -> p (a b)"), PS[:, 3, 0:NPG * NS])
                    dve.tensor_copy(PT[0:DSEQ, NPG, :], PS[0:DSEQ, 3, NPG * NS:(NPG + 1) * NS]).then_inc(pt, 1)


def merge_stage(nc, H, YC, M, d):
    with ExitStack() as ctx:
        sb = lambda n, s, dt=F32: ctx.enter_context(nc.sbuf_tensor("mg_" + n, s, dt))
        sem = lambda n: ctx.enter_context(nc.semaphore("mg_" + n))
        NB = 2 * KD + 2 * CT
        W = sb("w", [P, 2, NB, P])
        A = sb("a", [P, CT, TQ])
        S = sb("s", [P, 2, 2, 352])
        PS = ctx.enter_context(nc.psum_tensor("mg_ps", [P, 2, 4, 512], F32))
        w_in = [sem(f"w_in{s}") for s in range(2)]
        a_in, proj, gates, step, done = (sem(n) for n in ("a_in", "proj", "gates", "step", "done"))
        block = ctx.enter_context(nc.Block())

        @block.sync
        def _(sp):
            for s in range(2):
                sp.dma_start(W[:, s], d["w_merge"][s]).then_inc(w_in[s], 16)
            for k in range(CT):
                sp.dma_start(A[:, k, :], d["s_attn"][2 * k:2 * k + 2].rearrange("a p n -> (a p) n")
                             ).then_inc(a_in, 16)
            with sp.Fori(0, KD // 2 - 1) as o:
                for s in range(2):
                    sp.wait_ge(proj, o * 6 + 3 * (s + 1))
                    sp.dma_start(W[:, s], d["w_merge"][bass.ds(o * 2 + s + 2, 1)].rearrange("o p b n -> (o p) b n")
                                 ).then_inc(w_in[s], 16)

        @block.tensor
        def _(pe):
            pe.wait_ge(a_in, 16 * CT)
            with pe.Fori(0, KD // 2) as o:
                for s in range(2):
                    pe.wait_ge(w_in[s], (o + 1) * 16)
                    for c, (a, n) in enumerate(QCH):
                        g = 3 * s + c
                        pe.wait_ge(done, o * 6 + g - 1) if g >= 2 else pe.wait_ge(done, o * 6)
                        at = 0
                        for m, (x, nk, lo) in enumerate(((H, KD, META), (H, KD, META), (YC, CT, 0), (A, CT, 0))):
                            for k in range(nk):
                                mm = pe.matmul(PS[:, g % 2, m, 0:n], W[:, s, at + k, :], x[:, k, lo + a:lo + a + n],
                                               start=(k == 0), stop=(k == nk - 1))
                            at += nk
                        mm.then_inc(proj, 1)

        @block.scalar
        def _(act):
            with act.Fori(0, KD // 2) as o:
                for g in range(6):
                    act.wait_ge(proj, o * 6 + g + 1)
                    act.wait_ge(done, o * 6 + g - 1) if g >= 2 else act.wait_ge(done, o * 6)
                    n = 352
                    act.activation(S[:, g % 2, :, :], PS[:, g % 2, 0:2, 0:n], ACT.Sigmoid).then_inc(gates, 1)

        @block.vector
        def _(dve):
            with dve.Fori(0, KD // 2) as o:
                for g in range(6):
                    a, n = QCH[g % 3]
                    dve.wait_ge(gates, o * 6 + g + 1)
                    dve.tensor_tensor(S[:, g % 2, :, :], PS[:, g % 2, 2:4, 0:n], S[:, g % 2, :, :], ALU.mult
                                      ).then_inc(step, 1)
                    dve.wait_ge(step, o * 6 + g + 1)
                    out = M[:, bass.ds(o * 2 + g // 3, 1), a:a + n].rearrange("p a n -> p (a n)")
                    dve.tensor_tensor(out, S[:, g % 2, 0, :], S[:, g % 2, 1, :], ALU.add).then_inc(done, 1)


def mix_stage(nc, X, M, d):
    with ExitStack() as ctx:
        sem = lambda n: ctx.enter_context(nc.semaphore("mx_" + n))
        W = ctx.enter_context(nc.sbuf_tensor("mx_w", [P, 2, KD, P], F32))
        PS = ctx.enter_context(nc.psum_tensor("mx_ps", [P, 6, 512], F32))
        w_in = [sem(f"w_in{s}") for s in range(2)]
        proj, done = sem("proj"), sem("done")
        block = ctx.enter_context(nc.Block())

        @block.sync
        def _(sp):
            for s in range(2):
                sp.dma_start(W[:, s], d["w_mix"][s]).then_inc(w_in[s], 16)
            with sp.Fori(0, KD // 2 - 1) as o:
                for s in range(2):
                    sp.wait_ge(proj, o * 6 + 3 * (s + 1))
                    sp.dma_start(W[:, s], d["w_mix"][bass.ds(o * 2 + s + 2, 1)].rearrange("o p b n -> (o p) b n")
                                 ).then_inc(w_in[s], 16)

        @block.tensor
        def _(pe):
            with pe.Fori(0, KD // 2) as o:
                for s in range(2):
                    pe.wait_ge(w_in[s], (o + 1) * 16)
                    if s == 0:
                        pe.wait_ge(done, o * 6)
                    for c, (a, n) in enumerate(QCH):
                        for k in range(KD):
                            mm = pe.matmul(PS[:, 3 * s + c, 0:n], W[:, s, k, :], M[:, k, a:a + n],
                                           start=(k == 0), stop=(k == KD - 1))
                        mm.then_inc(proj, 1)

        @block.vector
        def _(dve):
            with dve.Fori(0, KD // 2) as o:
                for g in range(6):
                    a, n = QCH[g % 3]
                    x = X[:, bass.ds(o * 2 + g // 3, 1), META + a:META + a + n].rearrange("p a n -> p (a n)")
                    dve.wait_ge(proj, o * 6 + g + 1)
                    dve.tensor_tensor(x, PS[:, g, 0:n], x, ALU.add).then_inc(done, 1)


def topk_stage(nc, K, H, SEL, d):
    with ExitStack() as ctx:
        sb = lambda n, s, dt=F32: ctx.enter_context(nc.sbuf_tensor("tk_" + n, s, dt))
        sem = lambda n: ctx.enter_context(nc.semaphore("tk_" + n))
        W = sb("w", [P, 2, KD + 1, P])
        QS = sb("q", [P, TQ])
        S = sb("s", [TT, 2, NT, NK])
        S2 = sb("s2", [TT, NT, NK])
        TV = sb("tv", [TT, 2, NT, TOPK])
        TI = sb("ti", [TT, 2, NT, TOPK], U32)
        IF = sb("if", [TT, 2, NT, TOPK])
        CA = sb("cand", [TT, NT, TOPK * TOPK])
        CB = sb("cand2", [TT, NT, TOPK * TOPK])
        B = sb("best", [TT, NT, TOPK])
        BW = sb("weight", [TT, NT, TOPK])
        SM = sb("sum", [TT, NT])
        PW = sb("place", [TT, NT, TOPK], U32)
        PI = sb("ranks", [TT, 2, NT, TOPK], U32)
        PF = sb("ranksf", [TT, 2, NT * TOPK])
        EQ = sb("eq", [TT, 2, NT * TOPK, TOPK])
        PAD = sb("pad", [1, 1])
        PQ = ctx.enter_context(nc.psum_tensor("tk_pq", [P, 3, 512], F32))
        PS = ctx.enter_context(nc.psum_tensor("tk_ps", [P, 3, 512], F32))
        w_in = [sem(f"w_in{s}") for s in range(2)]
        (proj, qset, score, sset, half, pair, eq, picked, expo, done) = (
            sem(n) for n in ("proj", "qset", "score", "sset", "half", "pair", "eq", "picked", "expo", "done"))
        block = ctx.enter_context(nc.Block())
        known = lambda x: isinstance(x, int)
        HALF, PAIR = 5, 10

        @block.sync
        def _(sp):
            for s in range(2):
                sp.dma_start(W[:, s], d["w_peer"][s]).then_inc(w_in[s], 16)
            with sp.Fori(0, PH - 1) as h:
                for s in range(2):
                    sp.wait_ge(score, h * 2 + s + 2)
                    sp.dma_start(W[:, s], d["w_peer"][bass.ds(h * 2 + s + 2, 1)].rearrange("o p b n -> (o p) b n")
                                 ).then_inc(w_in[s], 16)

        @block.tensor
        def _(pe):
            pe.sem_inc(score, 1)
            with pe.Fori(0, PH) as h:
                for s in range(2):
                    q = h * 2 + s
                    pe.wait_ge(w_in[s], h * 16 + 16)
                    pe.wait_ge(qset, q + 1)
                    for c, (a, n) in enumerate(QCH):
                        for k in range(KD):
                            mm = pe.matmul(PQ[:, c, 0:n], W[:, s, k, :], H[:, k, META + a:META + a + n],
                                           start=(k == 0), stop=(k == KD - 1))
                    mm.then_inc(proj, 1)
                    pe.wait_ge(qset, q + 2)
                    pe.wait_ge(sset, q + 1)
                    for t in range(NT):
                        mm = pe.matmul(PS[0:TT, t // 4, (t % 4) * NK:(t % 4 + 1) * NK], QS[:, t * TT:(t + 1) * TT],
                                       W[:, s, KD, :], start=True, stop=True, skip_group_check=True)
                    mm.then_inc(score, 1)

        @block.scalar
        def _(act):
            act.sem_inc(qset, 1)
            act.sem_inc(sset, 1)
            with act.Fori(0, PH) as h:
                for s in range(2):
                    q = h * 2 + s
                    act.wait_ge(proj, q + 1)
                    act.wait_ge(score, q + 1)
                    for c, (a, n) in enumerate(QCH):
                        ins = act.activation(QS[:, a:a + n], PQ[:, c, 0:n], ACT.Copy)
                    ins.then_inc(qset, 1)
                    act.wait_ge(score, q + 2)
                    act.wait_ge(half, q * HALF + 3)
                    for c, (t, n) in enumerate(TILES):
                        ins = act.activation(S[:, s, t:t + n, :].rearrange("p a b -> p (a b)"),
                                             PS[0:TT, c, 0:n * NK], ACT.Copy)
                    ins.then_inc(sset, 1)
                act.wait_ge(pair, h * PAIR + PAIR)
                act.activation(BW[:], BW[:], ACT.Exp).then_inc(expo, 1)

        @block.gpsimd
        def _(pool):
            with pool.Fori(0, PH) as h:
                for c in range(2):
                    pool.wait_ge(eq, h * 2 + c + 1)
                    e = EQ[:, c].rearrange("p (t j) k -> p t j k", t=NT)
                    pool.tensor_tensor(e, e, IF[:, c].unsqueeze(2).to_broadcast([TT, NT, TOPK, TOPK]), ALU.mult
                                       ).then_inc(picked, 1)

        @block.vector
        def _(dve):
            def search(h, s):
                q = h * 2 + s
                at = (q + 2) * HALF
                dve.wait_ge(half, at)
                dve.wait_ge(sset, q + 2)
                dve.memset(PAD[:], 0.0)
                for t in range(NT):
                    ins = dve.max(TV[:, s, t, 0:8], S[:, s, t, :])
                ins.then_inc(half, 1)
                dve.wait_ge(half, at + 1)
                dve.memset(PAD[:], 0.0)
                for t in range(NT):
                    ins = dve.max_index(TI[:, s, t, 0:8], TV[:, s, t, 0:8], S[:, s, t, :])
                ins.then_inc(half, 1)
                for t in range(NT):
                    ins = dve.match_replace(S2[:, t, :], TV[:, s, t, 0:8], S[:, s, t, :], -3e38)
                ins.then_inc(half, 1)
                dve.wait_ge(half, at + 3)
                dve.memset(PAD[:], 0.0)
                for t in range(NT):
                    ins = dve.max(TV[:, s, t, 8:16], S2[:, t, :])
                ins.then_inc(half, 1)
                dve.wait_ge(half, at + 4)
                dve.memset(PAD[:], 0.0)
                for t in range(NT):
                    ins = dve.max_index(TI[:, s, t, 8:16], TV[:, s, t, 8:16], S2[:, t, :])
                ins.then_inc(half, 1)

            def pairs(h):
                at = h * PAIR
                dve.wait_ge(half, h * (2 * HALF) + 4 * HALF)
                ca = CA[:].rearrange("p t (a b) -> p t a b", b=TOPK)
                full = [TT, NT, TOPK, TOPK]
                dve.tensor_tensor(ca, TV[:, 0].unsqueeze(3).to_broadcast(full), TV[:, 1].unsqueeze(2).to_broadcast(full),
                                  ALU.add).then_inc(pair, 1)
                dve.tensor_copy(IF[:], TI[:]).then_inc(pair, 1)
                dve.wait_ge(pair, at + 2)
                dve.memset(PAD[:], 0.0)
                for t in range(NT):
                    ins = dve.max(B[:, t, 0:8], CA[:, t, :])
                ins.then_inc(pair, 1)
                dve.wait_ge(pair, at + 3)
                dve.memset(PAD[:], 0.0)
                for t in range(NT):
                    dve.max_index(PW[:, t, 0:8], B[:, t, 0:8], CA[:, t, :])
                    ins = dve.match_replace(CB[:, t, :], B[:, t, 0:8], CA[:, t, :], -3e38)
                ins.then_inc(pair, 1)
                dve.wait_ge(pair, at + 4)
                dve.memset(PAD[:], 0.0)
                for t in range(NT):
                    ins = dve.max(B[:, t, 8:16], CB[:, t, :])
                ins.then_inc(pair, 1)
                dve.wait_ge(pair, at + 5)
                dve.memset(PAD[:], 0.0)
                for t in range(NT):
                    ins = dve.max_index(PW[:, t, 8:16], B[:, t, 8:16], CB[:, t, :])
                ins.then_inc(pair, 1)
                dve.wait_ge(pair, at + 6)
                dve.tensor_scalar(PI[:, 0], PW[:], 4, None, ALU.logical_shift_right).then_inc(pair, 1)
                dve.tensor_scalar(PI[:, 1], PW[:], TOPK - 1, None, ALU.bitwise_and).then_inc(pair, 1)
                dve.wait_ge(pair, at + 8)
                dve.tensor_copy(PF[:], PI[:].rearrange("p c t j -> p c (t j)")).then_inc(pair, 1)
                dve.wait_ge(pair, at + 9)
                io16 = K[0:TT, C_IOTA:C_IOTA + TOPK].unsqueeze(1).to_broadcast([TT, NT * TOPK, TOPK])
                for c in range(2):
                    dve.tensor_tensor(EQ[:, c], PF[:, c, :].unsqueeze(2).to_broadcast([TT, NT * TOPK, TOPK]), io16,
                                      ALU.is_equal).then_inc(eq, 1)
                dve.tensor_tensor(BW[:], B[:], B[:, :, 0:1].to_broadcast([TT, NT, TOPK]), ALU.subtract
                                  ).then_inc(pair, 1)

            def finish(h):
                out = lambda i: SEL[:, :, i, bass.ds(h, 1), :].rearrange("p t a k -> p t (a k)")
                dve.wait_ge(expo, h + 1)
                dve.tensor_reduce(SM[:], BW[:], AX.X, ALU.add).then_inc(done, 1)
                dve.wait_ge(done, h * 2 + 1)
                dve.reciprocal(SM[:], SM[:]).then_inc(done, 1)
                for c in range(2):
                    dve.wait_ge(picked, h * 2 + c + 1)
                    dve.tensor_reduce(out(c), EQ[:, c].rearrange("p (t j) k -> p t j k", t=NT), AX.X, ALU.add)
                dve.wait_ge(done, h * 2 + 2)
                dve.tensor_tensor(out(2), BW[:], SM[:].unsqueeze(2).to_broadcast([TT, NT, TOPK]), ALU.mult)

            dve.sem_inc(half, 2 * HALF)
            search(0, 0)
            with dve.Fori(0, PH - 1) as h:
                search(h, 1)
                pairs(h)
                search(h + 1, 0)
                finish(h)
            search(PH - 1, 1)
            pairs(PH - 1)
            finish(PH - 1)


def route_stage(nc, K, SEL, d):
    with ExitStack() as ctx:
        sb = lambda n, s, dt=F32: ctx.enter_context(nc.sbuf_tensor("rt_" + n, s, dt))
        sem = lambda n: ctx.enter_context(nc.semaphore("rt_" + n))
        TR = sb("tr", [P, 3, TQ])
        TB = 8
        NBT = TT // TB
        O1 = sb("one1", [P, 2, TB, NK])
        O2 = sb("one2", [P, 2, TB, NK])
        OG = sb("one2g", [P, 2, TB, NK])
        STG = sb("stage", [P, 2, NK, TT])
        PS = ctx.enter_context(nc.psum_tensor("rt_ps", [P, 4, 512], F32))
        PT = ctx.enter_context(nc.psum_tensor("rt_pt", [P, 3, 512], F32))
        stored = [sem(f"stored{s}") for s in range(2)]
        turned, tr, one1, two, one2, gm, gset = (
            sem(n) for n in ("turned", "tr", "one1", "two", "one2", "gm", "gset"))
        block = ctx.enter_context(nc.Block())

        def tiles(eng, tile):
            with eng.Fori(0, NT // 2) as o:
                tile(o * 2, 0, o)
                tile(o * 2 + 1, 1, o)
            for t in range(NT // 2 * 2, NT):
                tile(t, t % 2, t // 2)

        @block.sync
        def _(sp):
            for s in range(2):
                sp.sem_inc(stored[s], 16)

            def tile(t, s, o):
                sp.wait_ge(gset, t * NBT + NBT + 2)
                dst = d["s_route"][t] if isinstance(t, int) else \
                    d["s_route"][bass.ds(t, 1)].rearrange("o p n -> (o p) n")
                sp.dma_start(dst, STG[:, s].rearrange("p a b -> p (a b)")).then_inc(stored[s], 16)

            tiles(sp, tile)
            sp.wait_ge(stored[0], 16 * (NT - NT // 2 + 1))
            sp.wait_ge(stored[1], 16 * (NT // 2 + 1))

        @block.tensor
        def _(pe):
            pe.sem_inc(gm, 2)
            for i in range(3):
                for c, (t0, n) in enumerate(TILES):
                    if 3 * i + c >= 3:
                        pe.wait_ge(tr, 3 * i + c - 2)
                    for t in range(t0, t0 + n):
                        mm = pe.transpose(PT[:, c, (t - t0) * TT:(t - t0 + 1) * TT],
                                          SEL[:, t, i].rearrange("p h k -> p (h k)"), K[0:TT, C_ID:C_ID + TT])
                    mm.then_inc(turned, 1)

            def tile(t, slot, o):
                with pe.Fori(0, NBT // 2) as b:
                    for s in range(2):
                        n = t * NBT + b * 2 + s
                        pe.wait_ge(one1, n + 1)
                        pe.wait_ge(one2, n + 1)
                        pe.wait_ge(gset, n + 1)
                        for j in range(TB):
                            mm = pe.matmul(PS[:, 2 * s + j // 4, (j % 4) * NK:(j % 4 + 1) * NK], O1[:, s, j, :],
                                           OG[:, s, j, :], start=True, stop=True, skip_group_check=True)
                        mm.then_inc(gm, 1)

            tiles(pe, tile)

        @block.scalar
        def _(act):
            act.sem_inc(gset, 2)
            for i in range(3):
                for c, (t0, n) in enumerate(TILES):
                    act.wait_ge(turned, 3 * i + c + 1)
                    act.activation(TR[:, i, t0 * TT:(t0 + n) * TT], PT[:, c, 0:n * TT], ACT.Copy).then_inc(tr, 1)

            def tile(t, slot, o):
                act.wait_ge(stored[slot], o * 16 + 16)
                with act.Fori(0, NBT // 2) as b:
                    for s in range(2):
                        n = t * NBT + b * 2 + s
                        act.wait_ge(gm, n + 3)
                        for i in range(2):
                            tok = (b * 2 + s) * TB + 4 * i
                            ins = act.activation(STG[:, slot, :, bass.ds(tok, 4)].rearrange("p i t -> p t i"),
                                                 PS[:, 2 * s + i, :].rearrange("p (t i) -> p t i", i=NK), ACT.Copy)
                        ins.then_inc(gset, 1)

            tiles(act, tile)

        picks = lambda i, t, b, s: TR[:, i, bass.ds(t * TT + (b * 2 + s) * TB, TB)].unsqueeze(2).to_broadcast([P, TB, NK])

        @block.gpsimd
        def _(pool):
            def tile(t, slot, o):
                with pool.Fori(0, NBT // 2) as b:
                    for s in range(2):
                        n = t * NBT + b * 2 + s
                        pool.wait_ge(two, n + 1)
                        pool.tensor_tensor(OG[:, s], O2[:, s], picks(2, t, b, s), ALU.mult).then_inc(one2, 1)

            tiles(pool, tile)

        @block.vector
        def _(dve):
            io = K[:, C_IOTA:C_IOTA + NK].unsqueeze(1).to_broadcast([P, TB, NK])

            def tile(t, slot, o):
                with dve.Fori(0, NBT // 2) as b:
                    for s in range(2):
                        n = t * NBT + b * 2 + s
                        dve.wait_ge(gm, n + 1)
                        dve.tensor_tensor(O2[:, s], io, picks(1, t, b, s), ALU.is_equal).then_inc(two, 1)
                        dve.tensor_tensor(O1[:, s], io, picks(0, t, b, s), ALU.is_equal).then_inc(one1, 1)

            dve.wait_ge(tr, 9)
            tiles(dve, tile)


def split_stage(nc, HH, HL, d):
    with ExitStack() as ctx:
        S = ctx.enter_context(nc.sbuf_tensor("sp_s", [P, 3, TQ], F32))
        s_in = [ctx.enter_context(nc.semaphore(f"sp_in{i}")) for i in range(3)]
        high, low = (ctx.enter_context(nc.semaphore("sp_" + n)) for n in ("high", "low"))
        block = ctx.enter_context(nc.Block())

        @block.sync
        def _(sp):
            for k in range(KD):
                if k >= 3:
                    sp.wait_ge(low, k - 2)
                sp.dma_start(S[:, k % 3, :], d["s_h"][:, k, :]).then_inc(s_in[k % 3], 16)

        @block.scalar
        def _(act):
            for k in range(KD):
                act.wait_ge(s_in[k % 3], 16 * (k // 3 + 1))
                act.activation(HH[:, k, :], S[:, k % 3, :], ACT.Copy).then_inc(high, 1)

        @block.vector
        def _(dve):
            for k in range(KD):
                dve.wait_ge(high, k + 1)
                dve.tensor_tensor(HL[:, k, :], S[:, k % 3, :], HH[:, k, :].bitcast(F32), ALU.subtract
                                  ).then_inc(low, 1)
            dve.wait_ge(low, KD)


def expert_stage(nc, X, HH, HL, d):
    with ExitStack() as ctx:
        sb = lambda n, s, dt=F32: ctx.enter_context(nc.sbuf_tensor("ex_" + n, s, dt))
        sem = lambda n: ctx.enter_context(nc.semaphore("ex_" + n))
        UR = sb("ur", [P, 2, KD * P])
        VR = sb("vr", [P, D])
        UH = sb("uh", [P, 2, KD * P], F32R)
        UL = sb("ul", [P, 2, KD * P], F32R)
        VHI = sb("vh", [P, 2, GRP, D], F32R)
        VLO = sb("vl", [P, 2, GRP, D], F32R)
        R = sb("r", [P, NT, GRP, TT])
        WH = sb("wh", [P, 2, GRP, TQ], F32R)
        WL = sb("wl", [P, 2, GRP, TQ], F32R)
        G = sb("g", [P, 2, 4 * TT])
        WR = sb("wr", [P, 4 * TT])
        PA = ctx.enter_context(nc.psum_tensor("ex_pa", [P, 3, 512], F32))
        PO = ctx.enter_context(nc.psum_tensor("ex_po", [P, 4, 512], F32))
        u_in = [sem(f"u_in{s}") for s in range(2)]
        v_in, r_in, u_high, u_set, v_high, v_set, a_mm, gelu, w_mul, w_high, w_set, o_mm, o_free, stored = (
            sem(n) for n in ("v_in", "r_in", "u_high", "u_set", "v_high", "v_set", "a_mm", "gelu", "w_mul",
                             "w_high", "w_set", "o_mm", "o_free", "stored"))
        block = ctx.enter_context(nc.Block())
        NG = NK // GRP
        NC = 3 * GRP
        NO = 3 * KD
        CH = [(t * TT, n * TT) for t, n in TILES]
        known = lambda x: isinstance(x, int)

        def schedule(eng, first, second):
            first(0, 0)
            with eng.Fori(0, NG // 2 - 1) as o:
                first(o * 2 + 1, 1)
                second(o * 2, 0)
                first(o * 2 + 2, 0)
                second(o * 2 + 1, 1)
            first(NG - 1, 1)
            second(NG - 2, 0)
            second(NG - 1, 1)

        @block.sync
        def _(sp):
            def load_u(n, slot):
                src = d["u"][n] if known(n) else d["u"][bass.ds(n, 1)].rearrange("o p m -> (o p) m")
                sp.dma_start(UR[:, slot, :], src).then_inc(u_in[slot], 16)

            def load_v(n):
                sp.dma_start(VR[:], d["v"][:, bass.ds(n * D, D)]).then_inc(v_in, 16)

            def load_r(g):
                sp.dma_start(R[:].rearrange("p t g n -> p t (g n)"),
                             d["s_route4"][:, :, bass.ds(g * (GRP * TT), GRP * TT)]).then_inc(r_in, 16)

            def first(g, s):
                for b in range(GRP):
                    m = g * GRP + b
                    if not known(m) or m + 2 < NK:
                        sp.wait_ge(u_set, m + 1)
                        load_u(m + 2, b)
                    if not known(m) or m + 1 < NK:
                        sp.wait_ge(v_set, m + 1)
                        load_v(m + 1)
                if not known(g) or g + 1 < NG:
                    sp.wait_ge(w_mul, (g + 1) * NC)
                    load_r(g + 1)

            load_u(0, 0)
            load_r(0)
            load_u(1, 1)
            load_v(0)
            schedule(sp, first, lambda g, s: None)
            sp.wait_ge(o_free, NG * NO + 4)
            sp.dma_start(d["o_y"], X[:, :, META:T]).then_inc(stored, 16)
            sp.wait_ge(stored, 16)

        @block.tensor
        def _(pe):
            def first(g, s):
                for b in range(GRP):
                    pe.wait_ge(u_set, g * GRP + b + 1)
                    for c, (a, n) in enumerate(CH):
                        j = 3 * b + c
                        if not known(g) or g * NC + j >= 3:
                            pe.wait_ge(gelu, g * NC + j - 2)
                        for k in range(KD):
                            u = slice(k * P, (k + 1) * P)
                            for i, (l, r) in enumerate(((UH, HH), (UH, HL), (UL, HH))):
                                mm = pe.matmul(PA[:, c, 0:n], l[:, b, u], r[:, k, a:a + n],
                                               start=(k == 0 and i == 0), stop=(k == KD - 1 and i == 2))
                        mm.then_inc(a_mm, 1)

            def second(g, s):
                pe.wait_ge(w_set, (g + 1) * NC)
                pe.wait_ge(v_set, (g + 1) * GRP)
                for j in range(NO):
                    k, (a, n) = j // 3, CH[j % 3]
                    pe.wait_ge(o_free, g * NO + j + 1)
                    for b in range(GRP):
                        for i, (l, r) in enumerate(((VHI, WH), (VHI, WL), (VLO, WH))):
                            mm = pe.matmul(PO[:, j % 4, 0:n], l[:, s, b, k * P:(k + 1) * P], r[:, s, b, a:a + n],
                                           start=(b == 0 and i == 0), stop=(b == GRP - 1 and i == 2))
                    mm.then_inc(o_mm, 1)

            schedule(pe, first, second)

        @block.scalar
        def _(act):
            def high_u(n, slot):
                act.wait_ge(u_in[slot], (n // 2 + 1) * 16 if known(n) else (n - slot) * 8 + 16)
                if not known(n) or n >= 2:
                    act.wait_ge(a_mm, n * 3 - 3)
                act.activation(UH[:, slot, :], UR[:, slot, :], ACT.Copy).then_inc(u_high, 1)

            def first(g, s):
                for b in range(GRP):
                    m = g * GRP + b
                    if not known(m) or m + 1 < NK:
                        high_u(m + 1, 1 - b)
                    for c, (a, n) in enumerate(CH):
                        j = 3 * b + c
                        act.wait_ge(a_mm, g * NC + j + 1)
                        if not known(g) or g * NC + j >= 2:
                            act.wait_ge(w_mul, g * NC + j - 1)
                        act.activation(G[:, j % 2, 0:n], PA[:, c, 0:n], ACT.Gelu).then_inc(gelu, 1)
                        if c == 0:
                            act.wait_ge(v_in, m * 16 + 16)
                            if not known(g) or g >= 2:
                                act.wait_ge(o_mm, g * NO - NO)
                            act.activation(VHI[:, s, b, :], VR[:], ACT.Copy).then_inc(v_high, 1)

            high_u(0, 0)
            schedule(act, first, lambda g, s: None)

        @block.vector
        def _(dve):
            def low_u(n, slot):
                dve.wait_ge(u_high, n + 1)
                dve.tensor_tensor(UL[:, slot, :], UR[:, slot, :], UH[:, slot, :].bitcast(F32), ALU.subtract
                                  ).then_inc(u_set, 1)

            def first(g, s):
                for b in range(GRP):
                    m = g * GRP + b
                    if not known(m) or m + 1 < NK:
                        low_u(m + 1, 1 - b)
                    if b == 0:
                        dve.wait_ge(r_in, g * 16 + 16)
                        if not known(g) or g >= 2:
                            dve.wait_ge(o_mm, g * NO - NO)
                    for c, (a, n) in enumerate(CH):
                        j = g * NC + 3 * b + c
                        t, nt = TILES[c]
                        v3 = lambda x: x.rearrange("p (t n) -> p t n", n=TT)
                        dve.wait_ge(gelu, j + 1)
                        if not known(j) or j >= 1:
                            dve.wait_ge(w_set, j)
                        dve.tensor_tensor(v3(WR[:, 0:n]), v3(G[:, (3 * b + c) % 2, 0:n]), R[:, t:t + nt, b, :],
                                          ALU.mult).then_inc(w_mul, 1)
                        dve.wait_ge(w_mul, j + 1)
                        dve.tensor_copy(WH[:, s, b, a:a + n], WR[:, 0:n]).then_inc(w_high, 1)
                        dve.wait_ge(w_high, j + 1)
                        dve.tensor_tensor(WL[:, s, b, a:a + n], WR[:, 0:n], WH[:, s, b, a:a + n].bitcast(F32),
                                          ALU.subtract).then_inc(w_set, 1)
                        if c == 0:
                            dve.wait_ge(v_high, m + 1)
                            dve.tensor_tensor(VLO[:, s, b, :], VR[:], VHI[:, s, b, :].bitcast(F32), ALU.subtract
                                              ).then_inc(v_set, 1)

            def second(g, s):
                for j in range(NO):
                    k, (a, n) = j // 3, CH[j % 3]
                    x = X[:, k, META + a:META + a + n]
                    dve.wait_ge(o_mm, g * NO + j + 1)
                    dve.tensor_tensor(x, PO[:, j % 4, 0:n], x, ALU.add).then_inc(o_free, 1)

            dve.sem_inc(o_free, 4)
            low_u(0, 0)
            schedule(dve, first, second)


def build(nc, d):
    with ExitStack() as ctx:
        X = ctx.enter_context(nc.sbuf_tensor("X", [P, KD, T], F32))
        with ExitStack() as trunk:
            K = trunk.enter_context(nc.sbuf_tensor("K", [P, C_ALL], F32))
            SEL = trunk.enter_context(nc.sbuf_tensor("SEL", [TT, NT, 3, PH, TOPK], F32))
            const_in = trunk.enter_context(nc.semaphore("const_in"))
            with nc.Block() as block:
                @block.sync
                def _(sp):
                    sp.dma_start(K[:], d["const"]).then_inc(const_in, 16)
                    sp.wait_ge(const_in, 16)
            with ExitStack() as normed:
                H = normed.enter_context(nc.sbuf_tensor("H", [P, KD, T], F32))
                norm_stage(nc, "n1_", X, H, K, d["g_mix"], d["x"])
                with ExitStack() as mid:
                    YC = mid.enter_context(nc.sbuf_tensor("YC", [P, CT, TQ], F32))
                    conv_stage(nc, H, YC, d)
                    attention(nc, H, K, d)
                    M = mid.enter_context(nc.sbuf_tensor("M", [P, KD, TQ], F32))
                    merge_stage(nc, H, YC, M, d)
                    mix_stage(nc, X, M, d)
                norm_stage(nc, "n2_", X, H, K, d["g_ffn"], h_dram=d["s_h"])
                topk_stage(nc, K, H, SEL, d)
            route_stage(nc, K, SEL, d)
        HH = ctx.enter_context(nc.sbuf_tensor("HH", [P, KD, TQ], F32R))
        HL = ctx.enter_context(nc.sbuf_tensor("HL", [P, KD, TQ], F32R))
        split_stage(nc, HH, HL, d)
        expert_stage(nc, X, HH, HL, d)


def attention(nc, H, K, d):
    with ExitStack() as at:
        QABS = at.enter_context(nc.sbuf_tensor("QABS", [P, KT, NSEQ, NH, DSEQ], F32))
        QRS = at.enter_context(nc.sbuf_tensor("QRS", [ROPE, NSEQ, NH, DSEQ], F32))
        CKV = at.enter_context(nc.sbuf_tensor("CKV", [P, KT, T], F32))
        KR = at.enter_context(nc.sbuf_tensor("KR", [P, T], F32))
        with ExitStack() as hd:
            CQ = hd.enter_context(nc.sbuf_tensor("CQ", [P, QT, T], F32))
            CS = hd.enter_context(nc.sbuf_tensor("CS", [P, 2, T], F32))
            latent_stage(nc, H, K, CQ, CKV, KR, CS, d)
            head_stage(nc, K, CQ, CKV, KR, CS, QABS, QRS, d)
        decode_stage(nc, K, CKV, KR, QABS, QRS, d)


def constants():
    K = np.zeros((P, C_ALL), np.float32)
    r = np.arange(P)
    K[:, C_ONES:C_ONES + P] = 1
    K[:, C_MEAN:C_MEAN + P] = 1 / D
    K[:, C_KV:C_KV + P] = 1 / KVL
    K[:, C_R32:C_R32 + P] = (r[:, None] // ROPE == r[None] // ROPE) / ROPE
    K[:NOPE, C_HEAD:C_HEAD + NOPE] = 1 / NOPE
    K[NOPE:HD, C_HEAD + NOPE:C_HEAD + HD] = 1 / ROPE
    K[:, C_ID:C_ID + P] = np.eye(P)
    for f in range(4):
        K[:, C_SEL + f * NS:C_SEL + (f + 1) * NS] = ((2 * f + r[:, None] // NOPE) == np.arange(NS)[None] // DSEQ) / NOPE
    K[:, C_MASK:C_MASK + P + META] = np.where(np.arange(P + META)[None] <= r[:, None] + META, 0, NEG)
    K[:NS, C_SMASK:C_SMASK + DSEQ] = np.where(np.arange(DSEQ)[None] <= np.arange(NS)[:, None] % DSEQ, 0, NEG)
    K[:, C_IOTA:C_IOTA + P] = r[None]
    K[:, C_EPS] = EPS
    pos = np.concatenate([np.arange(KEYS), np.tile(PAST + np.arange(DSEQ), NSEQ)]).astype(np.float32)
    freq = np.float32(10000.0) ** (-np.arange(0, ROPE, 2, dtype=np.float32) / np.float32(ROPE))
    ang = pos[None, :] * freq[:, None]
    c, s = np.cos(ang).astype(np.float32), np.sin(ang).astype(np.float32)
    cs = np.stack([np.tile(np.concatenate([c, c]), (4, 1)), np.tile(np.concatenate([-s, s]), (4, 1))], 1)
    return K, np.ascontiguousarray(cs)


def kernel(**inputs):
    import concourse.bacc as bacc
    from concourse.bass_utils import run_bass_kernel_spmd

    a = {k: np.asarray(v) for k, v in inputs.items()}
    K, cs = constants()
    tiles = lambda w: w.reshape(-1, P, w.shape[1]).transpose(1, 0, 2)
    blocks = lambda w: w.reshape(w.shape[0] // P, P, -1, P).transpose(2, 1, 0, 3)
    w_in = a["w_in"][0]
    edges = np.cumsum([0, CW, CW, CW, QL, KVL, ROPE, D, D])
    wB, wC, wX, wQ, wKV, wKR, wGC, wGA = (w_in[:, edges[i]:edges[i + 1]] for i in range(8))
    cols = lambda g: g.reshape(-1, P).T
    gq = np.concatenate([a["g_q_nope"][0], a["g_q_rope"][0]])
    g_head = np.zeros((P, 3), np.float32)
    g_head[:HD, 0] = gq
    g_head[:NOPE, 1] = a["g_k_nope"][0]
    uq, uk, uv = a["w_uq"][0], a["w_uk"][0], a["w_uv"][0]
    per_head = lambda w: w.reshape(-1, P, NH, w.shape[-1]).transpose(2, 1, 0, 3).reshape(NH, P, -1)
    feeds = {
        "const": K,
        "cossin": cs,
        "x": tiles(np.concatenate([a["meta_tokens"], a["x_prompt"][0], a["x_sample"].reshape(NS, D)]).T),
        "g_mix": cols(a["norm_mix"][0]),
        "g_ffn": cols(a["norm_ffn"][0]),
        "w_conv": np.stack([blocks(wB), blocks(wC), blocks(wX)], 1),
        "taps": a["conv_w"][0].reshape(3, CT, P).transpose(2, 1, 0),
        "state": a["state_conv"][0].reshape(NSEQ, 2, CT, P).transpose(3, 2, 0, 1),
        "w_lat": np.concatenate([blocks(wQ), blocks(wKV), blocks(np.tile(wKR, (1, 4)))]),
        "g_lat": np.concatenate([cols(a["g_q_lat"][0]), cols(a["g_kv_lat"][0]),
                                 np.tile(a["g_k_rope"][0], 4)[:, None]], 1),
        "g_head": g_head,
        "w_head": np.concatenate([per_head(uq), per_head(uk), per_head(uv)], 2),
        "w_ukT": uk.transpose(1, 2, 0),
        "w_uk": tiles(uk.reshape(KVL, -1)),
        "w_uv": tiles(uv.reshape(KVL, -1)),
        "pages": a["page_table"].reshape(1, -1),
        "cache": a["cache_ckv"][0],
        "krope": a["cache_krope"][0],
        "w_merge": np.concatenate([blocks(wGC), blocks(wGA), blocks(a["w_conv_out"][0]),
                                   blocks(a["w_attn_out"][0])], 2),
        "w_mix": blocks(a["w_mix_out"][0]),
        "w_peer": np.concatenate([blocks(a["w_peer_q"][0]), a["peer_sub_keys"][0].transpose(1, 0, 3, 2).reshape(
            HC, P, 1, NK)], 2),
        "u": a["peer_u"][0].reshape(NK, NK, KD, P).transpose(1, 3, 2, 0).reshape(NK, P, KD * P),
        "v": a["peer_v"][0].reshape(NK, NK * D),
    }
    nc = bacc.Bacc("TRN2", target_bir_lowering=False, num_devices=1)
    arrays, d = {}, {}
    for name, x in feeds.items():
        x = np.ascontiguousarray(x)
        arrays["in_" + name] = x
        d[name] = nc.dram_tensor("in_" + name, x.shape, mybir.dt.from_np(x.dtype), kind="ExternalInput").ap()
    outs = {"o_y": (P, KD, TQ), "o_ckv": (P, KT, T), "o_kr": (ROPE, T), "o_convp": (P, CT, 2),
            "o_convs": (P, CT, NSEQ, 2)}
    for name, shape in outs.items():
        d[name] = nc.dram_tensor(name, shape, F32, kind="ExternalOutput").ap()
    s_attn = nc.dram_tensor("s_attn", (NH, VH, TQ), F32)
    d["s_attn"] = s_attn.ap()
    d["s_h"] = nc.dram_tensor("s_h", (P, KD, TQ), F32).ap()
    s_route = nc.dram_tensor("s_route", (NT, P, NK * TT), F32)
    d["s_route"] = s_route.ap()
    d["s_route4"] = s_route.ap().rearrange("t p n -> p t n")
    build(nc, d)
    r = run_bass_kernel_spmd(nc, [arrays], core_ids=[0]).results[0]
    y = r["o_y"].transpose(2, 1, 0).reshape(TQ, D)
    ckv = r["o_ckv"].transpose(2, 1, 0).reshape(T, KVL)
    kr = r["o_kr"].T
    return (
        y[:SEQ].reshape(1, SEQ, D), y[SEQ:].reshape(NSEQ, DSEQ, D),
        ckv[:KEYS].reshape(1, 1, KEYS, KVL), kr[:KEYS].reshape(1, 1, KEYS, ROPE),
        r["o_convp"].transpose(2, 1, 0).reshape(1, 1, 2, CW),
        ckv[KEYS:].reshape(1, NSEQ, DSEQ, KVL), kr[KEYS:].reshape(1, NSEQ, DSEQ, ROPE),
        r["o_convs"].transpose(2, 3, 1, 0).reshape(1, NSEQ, 2, CW),
    )
```

```python
from contextlib import ExitStack

import numpy as np

import concourse.bass as bass
from concourse import mybir

F32 = mybir.dt.float32
F32R = mybir.dt.float32r
BF16 = mybir.dt.bfloat16
U32 = mybir.dt.uint32
I32 = mybir.dt.int32
ALU = mybir.AluOpType
ACT = mybir.ActivationFunctionType
AX = mybir.AxisListType

P = 128
D = 1024
KD = D // P
META, SEQ = 16, 1024
NSEQ, DSEQ = 8, 4
NS = NSEQ * DSEQ
T = META + SEQ + NS
KEYS = META + SEQ
TQ = SEQ + NS
CW = 512
CT = CW // P
QL, KVL, ROPE, NOPE, VH, NH = 384, 256, 32, 64, 64, 8
QT, KT = QL // P, KVL // P
HD = NOPE + ROPE
SCALE = float(HD) ** -0.5
PAST, PAGE = 1024, 128
NPG = PAST // PAGE
SK = PAST + DSEQ
NEG = -1e30
PH, NK, TOPK = 8, 128, 16
HC = PH * 2
TT = 96
NT = TQ // TT
PICK = PH * TOPK
EPS = 1e-6
CHUNKS = [(0, 360), (360, 360), (720, 352)]
QCH = [(0, 352), (352, 352), (704, 352)]
GRP = 2
NP = -(-TQ // P)
LAST = TQ - (NP - 1) * P
BANKS = [(0, 4), (4, 4), (8, NP - 8)]
TILES = [(0, 4), (4, 4), (8, NT - 8)]

C_ONES = 0
C_MEAN = C_ONES + P
C_KV = C_MEAN + P
C_R32 = C_KV + P
C_ID = C_R32 + P
C_SEL = C_ID + P
C_MASK = C_SEL + 4 * NS
C_SMASK = C_MASK + P + META
C_IOTA = C_SMASK + DSEQ
C_EPS = C_IOTA + P
NJ, ROWS = 6, 9
C_SUM = C_EPS + 1
C_ALL = C_SUM + NJ * ROWS


class Ahead:

    def __init__(self, nc, ctx, name, shape, sources):
        self.tile = ctx.enter_context(nc.sbuf_tensor(name, shape, F32))
        self.arrived = [ctx.enter_context(nc.semaphore(f"{name}_in{s}")) for s in range(2)]
        self.sources = sources

    def load(self, sp):
        for s in range(2):
            sp.dma_start(self.tile[:, s], self.sources[s]).then_inc(self.arrived[s], 16)


def norm_stage(nc, tag, X, H, K, g_dram, ahead, x_dram=None, h_dram=None):
    with ExitStack() as ctx:
        sb = lambda n, s, d=F32: ctx.enter_context(nc.sbuf_tensor(tag + n, s, d))
        sem = lambda n: ctx.enter_context(nc.semaphore(tag + n))
        G = sb("gain", [P, KD])
        SQ = sb("sq", [P, 2, T])
        RT = sb("root", [P, T])
        SS = ctx.enter_context(nc.psum_tensor(tag + "ss", [P, 3, 512], F32))
        gain_in, sq_ready, sq_used, root_ready, inv_ready, h_ready, stored = (
            sem(n) for n in ("gain_in", "sq_ready", "sq_used", "root_ready", "inv_ready", "h_ready", "stored"))
        x_in = [sem(f"x_in{k}") for k in range(KD // 2)] if x_dram is not None else None
        block = ctx.enter_context(nc.Block())

        @block.sync
        def _(sp):
            if x_dram is not None:
                for k in range(KD):
                    sp.dma_start(X[:, k, :], x_dram[:, k, :]).then_inc(x_in[k // 2], 16)
            sp.dma_start(G[:], g_dram).then_inc(gain_in, 16)
            ahead.load(sp)
            if h_dram is not None:
                sp.wait_ge(h_ready, KD)
                sp.dma_start(h_dram, H[:, :, META:T]).then_inc(stored, 16)
                sp.wait_ge(stored, 16)

        @block.scalar
        def _(act):
            for k in range(KD):
                if x_dram is not None:
                    act.wait_ge(x_in[k // 2], 32)
                if k >= 2:
                    act.wait_ge(sq_used, k - 1)
                act.activation(SQ[:, k % 2, :], X[:, k, :], ACT.Square).then_inc(sq_ready, 1)
            act.wait_ge(sq_used, KD)
            for c, (a, n) in enumerate(CHUNKS):
                act.activation(RT[:, a:a + n], SS[:, c, 0:n], ACT.Sqrt,
                               bias=K[:, C_EPS:C_EPS + 1]).then_inc(root_ready, 1)

        @block.tensor
        def _(pe):
            for k in range(KD):
                pe.wait_ge(sq_ready, k + 1)
                for c, (a, n) in enumerate(CHUNKS):
                    mm = pe.matmul(SS[:, c, 0:n], K[:, C_MEAN:C_MEAN + P], SQ[:, k % 2, a:a + n],
                                   start=(k == 0), stop=(k == KD - 1))
                mm.then_inc(sq_used, 1)

        @block.vector
        def _(dve):
            for c, (a, n) in enumerate(CHUNKS):
                dve.wait_ge(root_ready, c + 1)
                dve.reciprocal(RT[:, a:a + n], RT[:, a:a + n]).then_inc(inv_ready, 1)
            dve.wait_ge(inv_ready, 3)
            dve.wait_ge(gain_in, 16)
            for k in range(KD):
                dve.scalar_tensor_tensor(H[:, k, :], X[:, k, :], G[:, k:k + 1], RT[:],
                                         ALU.mult, ALU.mult).then_inc(h_ready, 1)
            dve.wait_ge(h_ready, KD)


def conv_stage(nc, H, YC, weights, ahead, d):
    with ExitStack() as ctx:
        sb = lambda n, s, dt=F32: ctx.enter_context(nc.sbuf_tensor("cv_" + n, s, dt))
        sem = lambda n: ctx.enter_context(nc.semaphore("cv_" + n))
        W, w_in = weights.tile, weights.arrived
        U = sb("u", [P, T])
        US = sb("us", [P, NSEQ, 2 + DSEQ])
        BS = sb("b", [P, T])
        XS = sb("xin", [P, 2, 360])
        Y = sb("y", [P, TQ])
        CWT = sb("taps", [P, CT, 3])
        ST = sb("state", [P, CT, NSEQ, 2])
        NP_ = sb("newp", [P, CT, 2])
        NS_ = sb("news", [P, CT, NSEQ, 2])
        PS = ctx.enter_context(nc.psum_tensor("cv_ps", [P, 2, 3, 512], F32))
        small_in, proj, copied, u_part, chan_done, step, stored = (
            sem(n) for n in ("small_in", "proj", "copied", "u_part", "chan_done", "step", "stored"))
        block = ctx.enter_context(nc.Block())
        STEPS = 10

        @block.sync
        def _(sp):
            sp.dma_start(CWT[:], d["taps"]).then_inc(small_in, 16)
            sp.dma_start(ST[:], d["state"]).then_inc(small_in, 16)
            ahead.load(sp)
            with sp.Fori(0, CT // 2 - 1) as o:
                for s in range(2):
                    sp.wait_ge(proj, o * 6 + 3 * (s + 1))
                    sp.dma_start(W[:, s], d["w_conv"][bass.ds(o * 2 + s + 2, 1)].rearrange(
                        "o a p k n -> (o p) a k n")).then_inc(w_in[s], 16)
            sp.wait_ge(chan_done, CT)
            sp.dma_start(d["o_convp"], NP_[:]).then_inc(stored, 16)
            sp.dma_start(d["o_convs"], NS_[:]).then_inc(stored, 16)
            sp.wait_ge(stored, 32)

        @block.tensor
        def _(pe):
            with pe.Fori(0, CT // 2) as o:
                for s in range(2):
                    pe.wait_ge(w_in[s], (o + 1) * 16)
                    for c, (a, n) in enumerate(CHUNKS):
                        g = 3 * s + c
                        if g >= 2:
                            pe.wait_ge(u_part, o * 6 + g - 1)
                        else:
                            pe.wait_ge(u_part, o * 6)
                        for m in range(3):
                            for k in range(KD):
                                mm = pe.matmul(PS[:, g % 2, m, 0:n], W[:, s, m, k, :], H[:, k, a:a + n],
                                               start=(k == 0), stop=(k == KD - 1))
                        mm.then_inc(proj, 1)

        @block.scalar
        def _(act):
            with act.Fori(0, CT // 2) as o:
                for s in range(2):
                    for c, (a, n) in enumerate(CHUNKS):
                        g = 3 * s + c
                        act.wait_ge(proj, o * 6 + g + 1)
                        if c == 0:
                            act.wait_ge(chan_done, o * 2 + s)
                        if g >= 2:
                            act.wait_ge(u_part, o * 6 + g - 1)
                        else:
                            act.wait_ge(u_part, o * 6)
                        act.activation(BS[:, a:a + n], PS[:, g % 2, 0, 0:n], ACT.Copy)
                        act.activation(XS[:, g % 2, 0:n], PS[:, g % 2, 2, 0:n], ACT.Copy).then_inc(copied, 1)

        @block.vector
        def _(dve):
            dve.wait_ge(small_in, 32)
            with dve.Fori(0, CT // 2) as o:
                for s in range(2):
                    c_ = o * 2 + s
                    at = c_ * STEPS
                    for c, (a, n) in enumerate(CHUNKS):
                        dve.wait_ge(copied, o * 6 + 3 * s + c + 1)
                        dve.tensor_tensor(U[:, a:a + n], PS[:, (3 * s + c) % 2, 1, 0:n],
                                          XS[:, (3 * s + c) % 2, 0:n], ALU.mult).then_inc(u_part, 1)
                    dve.wait_ge(u_part, c_ * 3 + 3)
                    tap = lambda k: CWT[:, bass.ds(c_, 1), k:k + 1].rearrange("p a k -> p (a k)")
                    us = U[:, META + SEQ:T].rearrange("p (s q) -> p s q", q=DSEQ)
                    dve.tensor_copy(US[:, :, 2:], us).then_inc(step, 1)
                    dve.tensor_copy(US[:, :, 0:2], ST[:, bass.ds(c_, 1)].rearrange("p a s k -> p (a s) k")
                                    ).then_inc(step, 1)
                    dve.tensor_copy(NP_[:, bass.ds(c_, 1), :].rearrange("p a k -> p (a k)"),
                                    U[:, META + SEQ - 2:META + SEQ]).then_inc(step, 1)
                    dve.tensor_scalar(Y[:, 0:SEQ], U[:, META - 2:META - 2 + SEQ], tap(0), None, ALU.mult
                                      ).then_inc(step, 1)
                    dve.wait_ge(step, at + 4)
                    dve.tensor_copy(NS_[:, bass.ds(c_, 1)].rearrange("p a s k -> p (a s) k"),
                                    US[:, :, DSEQ:]).then_inc(step, 1)
                    dve.scalar_tensor_tensor(Y[:, 0:SEQ], U[:, META - 1:META - 1 + SEQ], tap(1), Y[:, 0:SEQ],
                                             ALU.mult, ALU.add).then_inc(step, 1)
                    ys = Y[:, SEQ:TQ].rearrange("p (s q) -> p s q", q=DSEQ)
                    dve.tensor_scalar(ys, US[:, :, 0:DSEQ], tap(0), None, ALU.mult).then_inc(step, 1)
                    dve.wait_ge(step, at + 7)
                    dve.scalar_tensor_tensor(Y[:, 0:SEQ], U[:, META:META + SEQ], tap(2), Y[:, 0:SEQ],
                                             ALU.mult, ALU.add).then_inc(step, 1)
                    dve.scalar_tensor_tensor(ys, US[:, :, 1:1 + DSEQ], tap(1), ys, ALU.mult, ALU.add
                                             ).then_inc(step, 1)
                    dve.wait_ge(step, at + 9)
                    dve.scalar_tensor_tensor(ys, US[:, :, 2:2 + DSEQ], tap(2), ys, ALU.mult, ALU.add
                                             ).then_inc(step, 1)
                    dve.wait_ge(step, at + 10)
                    dve.tensor_tensor(YC[:, bass.ds(c_, 1), :].rearrange("p a t -> p (a t)"), Y[:],
                                      BS[:, META:T], ALU.mult).then_inc(chan_done, 1)


def rope(dve, out, x, swapped, CS, a, n, step, at, rows=slice(0, P)):
    r = rows
    dve.stream_shuffle(swapped, x, [(i + 16) % 32 for i in range(32)]).then_inc(step, 1)
    dve.wait_ge(step, at + 1)
    dve.tensor_tensor(swapped, swapped, CS[r, 1, a:a + n], ALU.mult).then_inc(step, 1)
    dve.tensor_tensor(out, x, CS[r, 0, a:a + n], ALU.mult).then_inc(step, 1)
    dve.wait_ge(step, at + 3)
    dve.tensor_tensor(out, out, swapped, ALU.add).then_inc(step, 1)


def latent_stage(nc, H, K, CQ, CKV, KR, CS, weights, ahead, d):
    with ExitStack() as ctx:
        sb = lambda n, s, dt=F32: ctx.enter_context(nc.sbuf_tensor("lt_" + n, s, dt))
        sem = lambda n: ctx.enter_context(nc.semaphore("lt_" + n))
        NB = QT + KT + 1
        W, w_in = weights.tile, weights.arrived
        SQ = sb("sq", [P, 2, T])
        RT = sb("root", [P, 3, T])
        G = sb("gains", [P, NB])
        SW = sb("swap", [P, T])
        PS = ctx.enter_context(nc.psum_tensor("lt_ps", [P, 3, 512], F32))
        SS = ctx.enter_context(nc.psum_tensor("lt_ss", [P, 3, 512], F32))
        small_in, proj, lat, sq_ready, sq_used, root, step, stored = (
            sem(n) for n in ("small_in", "proj", "lat", "sq_ready", "sq_used", "root", "step", "stored"))
        block = ctx.enter_context(nc.Block())
        dst = [CQ[:, i, :] for i in range(QT)] + [CKV[:, i, :] for i in range(KT)] + [KR[:, :]]
        first = {0: 0, 1: 0, 2: 0, 3: 1, 4: 1, 5: 2}
        last = {2: 0, 4: 1, 5: 2}
        mean = [C_ONES, C_KV, C_R32]

        @block.sync
        def _(sp):
            sp.dma_start(G[:], d["g_lat"]).then_inc(small_in, 16)
            sp.dma_start(CS[:], d["cossin"]).then_inc(small_in, 16)
            ahead.load(sp)
            for b in range(2, NB):
                sp.wait_ge(proj, b - 1)
                sp.dma_start(W[:, b % 2], d["w_lat"][b]).then_inc(w_in[b % 2], 16)
            sp.wait_ge(step, 13)
            sp.dma_start(d["o_ckv"], CKV[:]).then_inc(stored, 16)
            sp.dma_start(d["o_kr"], KR[0:ROPE, :]).then_inc(stored, 16)
            sp.wait_ge(stored, 32)

        @block.tensor
        def _(pe):
            def squares(b):
                pe.wait_ge(sq_ready, b + 1)
                if b in (3, 5):
                    pe.wait_ge(root, 1 + (b == 5))
                for c, (a, n) in enumerate(CHUNKS):
                    m = mean[first[b]]
                    mm = pe.matmul(SS[:, c, 0:n], K[:, m:m + P], SQ[:, b % 2, a:a + n],
                                   start=(b in (0, 3, 5)), stop=(b in last))
                mm.then_inc(sq_used, 1)

            for b in range(NB):
                pe.wait_ge(w_in[b % 2], 16 * (b // 2 + 1))
                if b:
                    pe.wait_ge(lat, b)
                for c, (a, n) in enumerate(CHUNKS):
                    for k in range(KD):
                        mm = pe.matmul(PS[:, c, 0:n], W[:, b % 2, k, :], H[:, k, a:a + n],
                                       start=(k == 0), stop=(k == KD - 1))
                mm.then_inc(proj, 1)
                if b:
                    squares(b - 1)
            squares(NB - 1)

        @block.scalar
        def _(act):
            def roots(b):
                act.wait_ge(sq_used, b + 1)
                i = last[b]
                for c, (a, n) in enumerate(CHUNKS):
                    ins = act.activation(RT[:, i, a:a + n], SS[:, c, 0:n], ACT.Sqrt, bias=K[:, C_EPS:C_EPS + 1],
                                         scale=1.0 / QL if i == 0 else 1.0)
                ins.then_inc(root, 1)

            for b in range(NB):
                act.wait_ge(proj, b + 1)
                for c, (a, n) in enumerate(CHUNKS):
                    ins = act.activation(dst[b][:, a:a + n], PS[:, c, 0:n], ACT.Copy)
                ins.then_inc(lat, 1)
                act.wait_ge(lat, b + 1)
                if b >= 2:
                    act.wait_ge(sq_used, b - 1)
                act.activation(SQ[:, b % 2, :], dst[b], ACT.Square).then_inc(sq_ready, 1)
                if b - 1 in last:
                    roots(b - 1)
            roots(NB - 1)

        @block.vector
        def _(dve):
            dve.wait_ge(small_in, 32)
            at = 0
            for i, blocks in enumerate(([0, 1, 2], [3, 4], [5])):
                dve.wait_ge(root, i + 1)
                dve.reciprocal(RT[:, i, :], RT[:, i, :]).then_inc(step, 1)
                at += 1
                dve.wait_ge(step, at)
                for b in blocks:
                    dve.scalar_tensor_tensor(dst[b], dst[b], G[:, b:b + 1], RT[:, i, :], ALU.mult, ALU.mult
                                             ).then_inc(step, 1)
                    at += 1
            dve.wait_ge(step, at)
            rope(dve, KR[:, :], KR[:, :], SW[:], CS, 0, T, step, at)
            assert at + 4 == 13
            dve.wait_ge(step, at + 4)


def known(x):
    return isinstance(x, int)


def query_stage(nc, K, CQ, CKV, KR, CS, QABS, QRS, weights, d):
    with ExitStack() as ctx:
        sb = lambda n, s, dt=F32: ctx.enter_context(nc.sbuf_tensor("qr_" + n, s, dt))
        sem = lambda n: ctx.enter_context(nc.semaphore("qr_" + n))
        WQ, WK = 0, QT * HD
        W, w_in = weights.tile, weights.arrived
        WUT = sb("wukT", [NOPE, NH, KVL])
        G = sb("gains", [P, 2])
        S = sb("spread", [ROWS, NJ * HD])
        RAW = sb("raw", [HD, 2, NJ, 360])
        SQ = sb("sq", [HD, NJ, 360])
        RI = sb("root", [ROWS, 2, 360])
        Q = sb("q", [HD, 2, TQ])
        KH = sb("k", [NOPE, 2, T])
        SW = sb("swap", [HD, 360])
        QG = sb("qg", [NOPE, NH, NS])
        PAD = sb("pad", [1, 1])
        PS = ctx.enter_context(nc.psum_tensor("qr_ps", [P, 8, 512], F32))
        SUMS, SPREAD, ABS = 3, 5, 7
        stored = [sem(f"stored{s}") for s in range(2)]
        small_in, spread_in, raw, sq, ss, root, inv, spread, normed, step, ready, qabs = (
            sem(n) for n in ("small_in", "spread_in", "raw", "sq", "ss", "root", "inv", "spread", "normed", "step", "ready", "qabs"))
        block = ctx.enter_context(nc.Block())
        JOBS = [(False, a, n) for a, n in CHUNKS] + [(True, a, n) for a, n in QCH]
        BEHIND = ((), (), (0,), (1,), (2, 3), (4, 5))

        def heads(eng, front, back):
            def one(h, s):
                front(h, s, lambda j: back(h - 1, 1 - s, j))

            front(0, 0, lambda j: None)
            one(1, 1)
            with eng.Fori(1, NH // 2) as o:
                one(o * 2, 0)
                one(o * 2 + 1, 1)
            for j in range(NJ):
                back(NH - 1, 1, j)

        @block.sync
        def _(sp):
            sp.dma_start(G[:], d["g_head"]).then_inc(small_in, 16)
            sp.dma_start(S[:], d["spread"]).then_inc(spread_in, 16)
            sp.dma_start(WUT[:], d["w_ukT"]).then_inc(small_in, 16)
            for s in range(2):
                sp.sem_inc(stored[s], 32)

            def store(h, s):
                sp.wait_ge(ready, h + 1)
                sp.dma_start(d["s_q"][bass.ds(h, 1)].rearrange("o p n -> (o p) n"), Q[:, s, 0:SEQ]
                             ).then_inc(stored[s], 16)
                sp.dma_start(d["s_k"][bass.ds(h, 1)].rearrange("o p n -> (o p) n"), KH[:, s, 0:KEYS]
                             ).then_inc(stored[s], 16)

            with sp.Fori(0, NH // 2 - 1) as o:
                for s in range(2):
                    h = o * 2 + s
                    sp.wait_ge(raw, h * NJ + NJ)
                    sp.dma_start(W[:, s], d["w_head"][bass.ds(h + 2, 1)].rearrange("o p n -> (o p) n")
                                 ).then_inc(w_in[s], 16)
                    store(h, s)
            for h in range(NH - 2, NH):
                store(h, h % 2)
            for s in range(2):
                sp.wait_ge(stored[s], 32 * (NH // 2 + 1))

        @block.tensor
        def _(pe):
            def sums(h, s, j):
                n = JOBS[j][2]
                pe.wait_ge(sq, h * NJ + j + 1)
                if known(h) and h == j == 0:
                    pe.wait_ge(step, 1)
                if j == 0 and (not known(h) or h >= 2):
                    pe.wait_ge(root, h - 1)
                at = C_SUM + j * ROWS
                pe.matmul(PS[0:ROWS, SUMS + s, 0:n], K[0:HD, at:at + ROWS], SQ[:, j, 0:n],
                          start=(j == 0), stop=(j == NJ - 1)).then_inc(ss, 1)

            def front(h, s, behind):
                pe.wait_ge(w_in[s], (h - s) * 8 + 16)
                for j, (query, a, n) in enumerate(JOBS):
                    if not known(h) or h * NJ + j >= 3:
                        pe.wait_ge(sq, h * NJ + j - 2)
                    M, w, nk, x, lo = (HD, WQ, QT, CQ, META) if query else (NOPE, WK, KT, CKV, 0)
                    for k in range(nk):
                        mm = pe.matmul(PS[0:M, j % 3, 0:n], W[:, s, w + k * M:w + (k + 1) * M],
                                       x[:, k, lo + a:lo + a + n], start=(k == 0), stop=(k == nk - 1))
                    mm.then_inc(raw, 1)
                    if j:
                        sums(h, s, j - 1)
                    for i in BEHIND[j]:
                        behind(i)
                sums(h, s, NJ - 1)

            def back(h, s, j):
                query, a, n = JOBS[j]
                M = HD if query else NOPE
                if known(h) and h == j == 0:
                    pe.wait_ge(spread_in, 16)
                if j == 0:
                    pe.wait_ge(inv, h + 1)
                if not known(h) or h * NJ + j >= 2:
                    pe.wait_ge(normed, h * NJ + j - 1)
                pe.matmul(PS[0:M, SPREAD + j % 2, 0:n], S[:, j * HD:j * HD + M], RI[:, s, 0:n],
                          start=True, stop=True).then_inc(spread, 1)

            heads(pe, front, back)
            pe.wait_ge(ready, NH)
            pe.wait_ge(small_in, 32)
            for h in range(NH):
                for k in range(KT):
                    mm = pe.matmul(PS[:, ABS, (h * KT + k) * NS:(h * KT + k + 1) * NS], WUT[:, h, k * P:(k + 1) * P],
                                   QG[:, h, :], start=True, stop=True, skip_group_check=True)
            mm.then_inc(qabs, 1)

        @block.scalar
        def _(act):
            def front(h, s, behind):
                if not known(h) or h >= 2:
                    act.wait_ge(normed, (h - 1) * NJ)
                for j, (query, a, n) in enumerate(JOBS):
                    M = HD if query else NOPE
                    act.wait_ge(raw, h * NJ + j + 1)
                    if not known(h) or h >= 1:
                        act.wait_ge(ss, (h - 1) * NJ + j + 1)
                    act.activation(RAW[0:M, s, j, 0:n], PS[0:M, j % 3, 0:n], ACT.Copy)
                    act.activation(SQ[0:M, j, 0:n], PS[0:M, j % 3, 0:n], ACT.Square).then_inc(sq, 1)
                if not known(h) or h >= 2:
                    act.wait_ge(spread, (h - 1) * NJ)
                act.wait_ge(ss, h * NJ + NJ)
                act.activation(RI[:, s, :], PS[0:ROWS, SUMS + s, 0:360], ACT.Sqrt,
                               bias=K[0:ROWS, C_EPS:C_EPS + 1]).then_inc(root, 1)

            heads(act, front, lambda h, s, j: None)

        @block.vector
        def _(dve):
            STEPS = 4 * 3
            r = slice(NOPE, HD)

            def head(h, s, o):
                dve.wait_ge(root, h + 1)
                dve.reciprocal(RI[:, s, :], RI[:, s, :]).then_inc(inv, 1)
                dve.wait_ge(stored[s], o * 32 + 32)
                for j, (query, a, n) in enumerate(JOBS):
                    M, out, g = (HD, Q, 0) if query else (NOPE, KH, 1)
                    dve.wait_ge(spread, h * NJ + j + 1)
                    dve.scalar_tensor_tensor(out[0:M, s, a:a + n], RAW[0:M, s, j, 0:n], G[0:M, g:g + 1],
                                             PS[0:M, SPREAD + j % 2, 0:n], ALU.mult, ALU.mult).then_inc(normed, 1)
                    if query:
                        dve.wait_ge(normed, h * NJ + j + 1)
                        dve.memset(PAD[:], 0.0)
                        rope(dve, Q[r, s, a:a + n], Q[r, s, a:a + n], SW[r, 0:n], CS, META + a, n, step,
                             1 + h * STEPS + 4 * (j - 3), r)
                dve.wait_ge(step, 1 + h * STEPS + STEPS)
                dve.tensor_scalar(QG[:, bass.ds(h, 1), :].rearrange("p a n -> p (a n)"), Q[0:NOPE, s, SEQ:TQ],
                                  G[0:NOPE, 1:2], None, ALU.mult)
                dve.tensor_copy(QRS[:, :, bass.ds(h, 1), :].rearrange("p s h q -> p s (h q)"),
                                Q[r, s, SEQ:TQ].rearrange("p (s q) -> p s q", q=DSEQ))
                dve.wait_ge(normed, h * NJ + NJ)
                dve.memset(PAD[:], 0.0).then_inc(ready, 1)

            dve.memset(SQ[r, 0:3, :], 0.0).then_inc(step, 1)
            dve.wait_ge(small_in, 32)
            with dve.Fori(0, NH // 2) as o:
                head(o * 2, 0, o)
                head(o * 2 + 1, 1, o)
            dve.wait_ge(qabs, 1)
            for k in range(KT):
                dve.tensor_copy(QABS[:, k].rearrange("p s h q -> p h s q"),
                                PS[:, ABS, :].rearrange("p (h k s q) -> p k h s q", k=KT, q=DSEQ, s=NSEQ)[:, k])


def prompt_stage(nc, K, CKV, KR, ahead, d):
    with ExitStack() as ctx:
        sb = lambda n, s, dt=F32: ctx.enter_context(nc.sbuf_tensor("pr_" + n, s, dt))
        sem = lambda n: ctx.enter_context(nc.semaphore("pr_" + n))
        Q = sb("q", [HD, 2, SEQ])
        KH = sb("k", [HD, 2, KEYS])
        WV = sb("wv", [P, KT, NH * VH])
        V = sb("v", [P, 2, 9, VH])
        PR = sb("p", [P, 2, KEYS])
        PT = sb("pt", [P, 9, P])
        MX = sb("mx", [P, 8])
        NM = sb("nm", [P, 8])
        SM = sb("sum", [P, 8])
        RI = sb("ri", [P, 8])
        O = sb("o", [P, 2, 8, VH])
        AT = sb("at", [P, NH // 2, P])
        PS = ctx.enter_context(nc.psum_tensor("pr_ps", [P, 8, 512], F32))
        BASE, SIDE, TURN, OUT = (0, 2), 4, 5, 7
        qk_in = [sem(f"qk_in{s}") for s in range(2)]
        (w_in, rope_in, side, side_set, step, score, negmax, probs, inv, turned, pt_act, pt_dve, pv, oset, stored) = (
            sem(n) for n in ("w_in", "rope_in", "side", "side_set", "step", "score", "negmax", "probs", "inv",
                             "turned", "pt_act", "pt_dve", "pv", "oset", "stored"))
        block = ctx.enter_context(nc.Block())
        NQ = SEQ // P
        nkeys = lambda i: META + P * (i + 1)
        blocks = lambda i: i + 2
        groups = lambda i: (blocks(i) + 3) // 4
        before = lambda i: sum(groups(j) for j in range(i))
        GR = before(NQ)
        even = lambda n: (n + 1) // 2
        odd = lambda n: n // 2
        assert GR % 2 == 0 and nkeys(NQ - 2) <= 2 * 512
        PARTS = (range(4), range(4, 9))
        more = lambda h: not known(h) or h + 1 < NH
        later = lambda h: not known(h) or h > 0

        def heads(eng, body):
            body(0, 0)
            with eng.Fori(0, NH // 2 - 1) as o:
                body(o * 2 + 1, 1)
                body(o * 2 + 2, 0)
            body(NH - 1, 1)

        def two_ahead(h, s, i, f):
            if i + 2 < NQ:
                f(h, s, i + 2)
            elif more(h):
                f(h + 1, 1 - s, i + 2 - NQ)

        def side_jobs(h, s, i, values, output):
            if i == 0 and later(h):
                output(h - 1, 1 - s, h * 3 + 2)
            if 1 <= i < 3 and more(h):
                values(h + 1, 1 - s, i - 1, h * 3 + i + 2)

        @block.sync
        def _(sp):
            def load(h, s):
                if not known(h) or h >= 2:
                    sp.wait_ge(score, (h - 1) * NQ)
                hd = bass.ds(h, 1)
                sp.dma_start(Q[:, s, :], d["s_q"][hd].rearrange("o p n -> (o p) n")).then_inc(qk_in[s], 16)
                sp.dma_start(KH[0:NOPE, s, :], d["s_k"][hd].rearrange("o p n -> (o p) n")).then_inc(qk_in[s], 16)

            def store(h, job):
                sp.wait_ge(side_set, job)
                dst = d["s_attn"][bass.ds(h, 1), :, 0:SEQ].rearrange("o p (c e n) -> e (o p) c n", e=2, n=P)
                for e in range(2):
                    sp.dma_start(dst[e], AT[e * VH:(e + 1) * VH]).then_inc(stored, 16)

            def body(h, s):
                if more(h):
                    load(h + 1, 1 - s)
                if later(h):
                    store(h - 1, h * 3 + 2)

            load(0, 0)
            sp.dma_start(WV[:], d["w_uv"]).then_inc(w_in, 16)
            ahead.load(sp)
            heads(sp, body)
            store(NH - 1, NH * 3)
            sp.wait_ge(stored, 32 * NH)

        @block.tensor
        def _(pe):
            def scores(h, s, i):
                if i == 0:
                    pe.wait_ge(qk_in[s], (h - s) * 16 + 32)
                if i == NQ - 1:
                    pe.wait_ge(side_set, h * 3 + (4 if more(h) else 2))
                for c in range(-(-nkeys(i) // 512)):
                    n = min(512, nkeys(i) - 512 * c)
                    mm = pe.matmul(PS[:, BASE[i % 2] + c, 0:n], Q[:, s, i * P:(i + 1) * P],
                                   KH[:, s, 512 * c:512 * c + n], start=True, stop=True)
                mm.then_inc(score, 1)

            def values(h, s, part, job):
                if not known(job) or job > 1:
                    pe.wait_ge(side_set, job - 1)
                for j in PARTS[part]:
                    m = P if j < 8 else META
                    for k in range(KT):
                        mm = pe.matmul(PS[0:m, SIDE, (j - PARTS[part][0]) * VH:(j - PARTS[part][0] + 1) * VH], CKV[:, k, j * P:j * P + m],
                                       WV[:, k, bass.ds(h * VH, VH)], start=(k == 0), stop=(k == KT - 1),
                                       skip_group_check=True)
                mm.then_inc(side, 1)

            def output(h, s, job):
                pe.wait_ge(side_set, job - 1)
                pe.wait_ge(oset, h * NQ + NQ)
                for j in range(NQ // 2):
                    mm = pe.transpose(PS[:, SIDE, j * P:(j + 1) * P],
                                      O[:, s, 2 * j:2 * j + 2, :].rearrange("p a b -> p (a b)"), K[:, C_ID:C_ID + P])
                mm.then_inc(side, 1)

            def turn(h, s, i):
                pe.wait_ge(w_in, 16)
                pe.wait_ge(probs, h * NQ + i + 1)
                for g in range(groups(i)):
                    G_ = before(i) + g
                    if g:
                        pe.wait_ge(w_in, 16)
                    if later(h) or G_ >= 2:
                        pe.wait_ge(pt_dve if G_ % 2 else pt_act, h * (GR // 2) + G_ // 2)
                    for j in range(4 * g, min(4 * g + 4, blocks(i))):
                        m = P if j < blocks(i) - 1 else META
                        mm = pe.transpose(PS[0:m, TURN + G_ % 2, (j % 4) * P:(j % 4 + 1) * P],
                                          PR[:, i % 2, j * P:j * P + m], K[:, C_ID:C_ID + P])
                    mm.then_inc(turned, 1)

            def product(h, s, i):
                n = before(i + 1)
                pe.wait_ge(pt_act, h * (GR // 2) + even(n))
                if later(h) or odd(n) > 0:
                    pe.wait_ge(pt_dve, h * (GR // 2) + odd(n))
                if later(h) or i > 0:
                    pe.wait_ge(oset, h * NQ + i)
                elif i == 0:
                    pe.wait_ge(side_set, 2)
                for j in range(blocks(i)):
                    m = P if j < blocks(i) - 1 else META
                    mm = pe.matmul(PS[:, OUT, 0:VH], PT[0:m, j, :], V[0:m, s, j, :],
                                   start=(j == 0), stop=(j == blocks(i) - 1))
                mm.then_inc(pv, 1)

            def body(h, s):
                for i in range(NQ):
                    turn(h, s, i)
                    two_ahead(h, s, i, scores)
                    product(h, s, i)
                    side_jobs(h, s, i, values, output)

            pe.wait_ge(w_in, 16)
            pe.wait_ge(rope_in, 2)
            values(0, 0, 0, 1)
            scores(0, 0, 0)
            scores(0, 0, 1)
            values(0, 0, 1, 2)
            heads(pe, body)
            output(NH - 1, 1, NH * 3)

        def copy_turned(i, g, copy):
            j0, j1 = 4 * g, min(4 * g + 4, blocks(i))
            full = min(j1, blocks(i) - 1)
            bank = TURN + (before(i) + g) % 2
            if full > j0:
                ins = copy(PT[:, j0:full, :], PS[:, bank, 0:(full - j0) * P].rearrange("p (a b) -> p a b", b=P))
            if full < j1:
                ins = copy(PT[0:META, full, :], PS[0:META, bank, (full % 4) * P:(full % 4 + 1) * P])
            return ins

        def score_row(i):
            b = BASE[i % 2]
            return PS[:, b:b + 2 + i % 2, :].rearrange("p a b -> p (a b)")[:, 0:nkeys(i)]

        @block.scalar
        def _(act):
            def exps(h, s, i):
                act.wait_ge(negmax, h * NQ + i + 1)
                if later(h) or i >= 2:
                    act.wait_ge(turned, (h * GR + before(i - 2) + groups(i - 2)) if i >= 2 else
                                h * GR - (GR - before(NQ - 2 + i) - groups(NQ - 2 + i)))
                act.activation(PR[:, i % 2, 0:nkeys(i)], score_row(i), ACT.Exp,
                               bias=NM[:, i:i + 1], scale=SCALE, accum_out=SM[:, i:i + 1]).then_inc(probs, 1)

            def values(h, s, part, job):
                act.wait_ge(side, job)
                ins = act.activation(V[:, s, 4 * part:4 * part + 4, :].rearrange("p a b -> p (a b)"),
                                     PS[:, SIDE, 0:4 * VH], ACT.Copy)
                if part:
                    ins = act.activation(V[0:META, s, 8, :], PS[0:META, SIDE, 4 * VH:5 * VH], ACT.Copy)
                ins.then_inc(side_set, 1)

            def output(h, s, job):
                if later(h):
                    act.wait_ge(stored, h * 32)
                act.wait_ge(side, job)
                act.activation(AT[:].rearrange("p a b -> p (a b)"), PS[:, SIDE, :], ACT.Copy).then_inc(side_set, 1)

            def body(h, s):
                for i in range(NQ):
                    for g in range(groups(i)):
                        G_ = before(i) + g
                        if G_ % 2 == 0:
                            act.wait_ge(turned, h * GR + G_ + 1)
                            copy_turned(i, g, lambda o, x: act.activation(o, x, ACT.Copy)).then_inc(pt_act, 1)
                    two_ahead(h, s, i, exps)
                    side_jobs(h, s, i, values, output)

            values(0, 0, 0, 1)
            exps(0, 0, 0)
            values(0, 0, 1, 2)
            exps(0, 0, 1)
            heads(act, body)
            output(NH - 1, 1, NH * 3)

        @block.vector
        def _(dve):
            def maxima(h, s, i):
                b = h * 2 * NQ + 2 * i
                row = score_row(i)
                dve.wait_ge(score, h * NQ + i + 1)
                m = row[:, nkeys(i) - P - META:nkeys(i)]
                dve.tensor_tensor(m, m, K[:, C_MASK:C_MASK + P + META], ALU.add).then_inc(step, 1)
                dve.wait_ge(step, b + 1)
                dve.tensor_reduce(MX[:, i:i + 1], row, AX.X, ALU.max).then_inc(step, 1)
                dve.wait_ge(step, b + 2)
                dve.tensor_scalar(NM[:, i:i + 1], MX[:, i:i + 1], -SCALE, None, ALU.mult).then_inc(negmax, 1)

            def body(h, s):
                for i in range(NQ):
                    for g in range(groups(i)):
                        G_ = before(i) + g
                        if G_ % 2:
                            dve.wait_ge(turned, h * GR + G_ + 1)
                            copy_turned(i, g, lambda o, x: dve.tensor_copy(o, x)).then_inc(pt_dve, 1)
                    dve.wait_ge(probs, h * NQ + i + 1)
                    dve.reciprocal(RI[:, i:i + 1], SM[:, i:i + 1]).then_inc(inv, 1)
                    two_ahead(h, s, i, maxima)
                    dve.wait_ge(pv, h * NQ + i + 1)
                    dve.wait_ge(inv, h * NQ + i + 1)
                    dve.tensor_scalar(O[:, s, i, :], PS[:, OUT, 0:VH], RI[:, i:i + 1], None, ALU.mult
                                      ).then_inc(oset, 1)

            for s in range(2):
                dve.tensor_copy(KH[NOPE:HD, s, :], KR[NOPE:HD, 0:KEYS]).then_inc(rope_in, 1)
            maxima(0, 0, 0)
            maxima(0, 0, 1)
            heads(dve, body)


class Cached:

    def __init__(self, nc, ctx, d):
        sb = lambda n, s, dt=F32: ctx.enter_context(nc.sbuf_tensor("ch_" + n, s, dt))
        sem = lambda n: ctx.enter_context(nc.semaphore("ch_" + n))
        self.d = d
        self.PTB = sb("pages", [1, NSEQ * NPG], I32)
        self.C = sb("c", [P, 2, NPG, KVL])
        self.R = sb("r", [P, 2, NPG, ROPE])
        self.WK = sb("wuk", [P, KT, NH * NOPE])
        self.tbl_in, self.w_in = sem("tbl_in"), sem("w_in")
        self.page_in = [sem(f"page_in{s}") for s in range(2)]

    def load_sequence(self, sp, q, s):
        for j in range(NPG):
            page = sp.value_load(self.PTB[0:1, bass.ds(q * NPG + j, 1)], min_val=0,
                                 max_val=self.d["cache"].shape[0] - 1)
            sp.dma_start(self.C[:, s, j, :], self.d["cache"][bass.ds(page, 1)].rearrange("o p n -> (o p) n")
                         ).then_inc(self.page_in[s], 16)
            sp.dma_start(self.R[:, s, j, :], self.d["krope"][bass.ds(page, 1)].rearrange("o p n -> (o p) n")
                         ).then_inc(self.page_in[s], 16)

    def load(self, sp):
        sp.dma_start(self.PTB[:], self.d["pages"]).then_inc(self.tbl_in, 16)
        sp.wait_ge(self.tbl_in, 16)
        self.load_sequence(sp, 0, 0)
        sp.dma_start(self.WK[:], self.d["w_uk"]).then_inc(self.w_in, 16)
        self.load_sequence(sp, 1, 1)


def decode_stage(nc, K, CKV, KR, QABS, QRS, cached, ahead, d):
    with ExitStack() as ctx:
        sb = lambda n, s, dt=F32: ctx.enter_context(nc.sbuf_tensor("dc_" + n, s, dt))
        sem = lambda n: ctx.enter_context(nc.semaphore("dc_" + n))
        C, R, WK, page_in, w_in = cached.C, cached.R, cached.WK, cached.page_in, cached.w_in
        CT_ = sb("cT", [P, KT, SK])
        RT_ = sb("rT", [ROPE, SK])
        WV = sb("wuv", [P, KT, NH * VH])
        QA = sb("qa", [P, KT, NS])
        QR = sb("qr", [ROPE, NS])
        SQ = sb("sq", [P, 2, 512])
        RS = sb("rs", [NS, SK])
        L = sb("l", [NS, SK])
        PR = sb("p", [NS, SK])
        PT = sb("pt", [P, NPG + 1, NS])
        CN = sb("cn", [DSEQ, KVL])
        ST = sb("st", [NS, 4])
        AS = sb("as", [VH, NH, NS])
        OLAT = sb("olat", [P, KT, NH, NSEQ, DSEQ])
        PS = ctx.enter_context(nc.psum_tensor("dc_ps", [P, 8, 512], F32))
        (wv_in, newk, turned, ct, kraw, sq, ss, root, sc, step, expo, inv, probs, pturn, pt, cn, cnset, ol,
         olset, av, stored) = (
            sem(n) for n in ("wv_in", "newk", "turned", "ct", "kraw", "sq", "ss", "root", "sc", "step",
                             "expo", "inv", "probs", "pturn", "pt", "cn", "cnset", "ol", "olset", "av", "stored"))
        block = ctx.enter_context(nc.Block())
        CK = [(0, 344), (344, 344), (688, SK - 688)]
        NC = len(CK)
        TB = 6
        STEPS = 3 * NC + 3
        NF = NH * NOPE // P

        def sequences(eng, front, back):
            def one(q, s):
                front(q, s, lambda part: back(q - 1, 1 - s, part))

            front(0, 0, lambda part: None)
            one(1, 1)
            with eng.Fori(1, NSEQ // 2 - 1) as o:
                one(o * 2, 0)
                one(o * 2 + 1, 1)
            one(NSEQ - 2, 0)
            one(NSEQ - 1, 1)
            for part in range(2):
                back(NSEQ - 1, 1, part)

        @block.sync
        def _(sp):
            sp.dma_start(WV[:], d["w_uv"]).then_inc(wv_in, 16)
            ahead.load(sp)
            with sp.Fori(1, NSEQ // 2) as o:
                for s in range(2):
                    sp.wait_ge(ol, o * 2 + s - 1)
                    cached.load_sequence(sp, o * 2 + s, s)
            sp.wait_ge(av, 2)
            sp.dma_start(d["s_attn"][:, :, SEQ:TQ].rearrange("h p n -> p h n"), AS[:]).then_inc(stored, 16)
            sp.wait_ge(stored, 16)

        @block.tensor
        def _(pe):
            I_ = K[:, C_ID:C_ID + P]

            def scores(q, c, a, n):
                if not known(q) or q or c:
                    pe.wait_ge(step, q * STEPS + 3 * c if c else q * STEPS - 3)
                for k in range(KT):
                    pe.matmul(PS[0:NS, 5, 0:n], QA[:, k, :], CT_[:, k, a:a + n], start=(k == 0), stop=(k == KT - 1))
                pe.matmul(PS[0:NS, 6, 0:n], QR[:], RT_[:, a:a + n], start=True, stop=True).then_inc(sc, 1)

            def back(q, s, part):
                if part == 0:
                    pe.wait_ge(w_in, 16)
                    pe.wait_ge(probs, q + 1)
                    for j in range(NPG):
                        pe.transpose(PS[:, 3, j * NS:(j + 1) * NS], PR[:, j * P:(j + 1) * P], K[0:NS, C_ID:C_ID + NS])
                    pe.transpose(PS[0:DSEQ, 3, NPG * NS:(NPG + 1) * NS], PR[:, PAST:SK], K[0:NS, C_ID:C_ID + NS]
                                 ).then_inc(pturn, 1)
                if part == 1:
                    pe.wait_ge(pt, q + 1)
                    pe.wait_ge(cnset, q + 1)
                    if not known(q) or q:
                        pe.wait_ge(olset, q)
                    for k in range(KT):
                        for j in range(NPG + 1):
                            if j < NPG:
                                lhs, rhs = C[:, s, j, k * P:(k + 1) * P], PT[:, j, :]
                            else:
                                lhs, rhs = CN[:, k * P:(k + 1) * P], PT[0:DSEQ, j, :]
                            mm = pe.matmul(PS[:, 7, k * NS:(k + 1) * NS], lhs, rhs,
                                           start=(j == 0), stop=(j == NPG), skip_group_check=True)
                    mm.then_inc(ol, 1)

            def front(q, s, behind):
                pe.wait_ge(w_in, 16)
                pe.wait_ge(page_in[s], (q - s + 2) * NPG * 16)
                for b in range(TB):
                    if b >= 2:
                        pe.wait_ge(w_in, 16)
                        pe.wait_ge(ct, q * TB + b - 1)
                    if b < 4:
                        k, half = b // 2, b % 2
                        for j in range(4):
                            mm = pe.transpose(PS[:, b % 2, j * P:(j + 1) * P],
                                              C[:, s, half * 4 + j, k * P:(k + 1) * P], I_)
                    else:
                        for j in range(4):
                            mm = pe.transpose(PS[0:ROPE, b % 2, j * P:(j + 1) * P],
                                              R[:, s, (b - 4) * 4 + j, :], I_)
                    mm.then_inc(turned, 1)
                pe.wait_ge(ct, q * TB + TB)
                pe.wait_ge(newk, q + 1)
                for c, (a, n) in enumerate(CK):
                    for f in range(NF + 1):
                        if c == 0 and f == NF - 1:
                            behind(0)
                        if c == 1 and f == 1:
                            behind(1)
                        if f < NF:
                            g = NF * c + f
                            if g >= 2:
                                pe.wait_ge(sq, q * NC * NF + g - 1)
                            for k in range(KT):
                                mm = pe.matmul(PS[:, g % 2, 0:n], WK[:, k, f * P:(f + 1) * P],
                                               CT_[:, k, a:a + n], start=(k == 0), stop=(k == KT - 1))
                            mm.then_inc(kraw, 1)
                        if f == 2:
                            scores(q, c, a, n)
                        if f:
                            g = NF * c + f - 1
                            pe.wait_ge(sq, q * NC * NF + g + 1)
                            if f == 1 and (c or not known(q) or q):
                                pe.wait_ge(root, q * NC + c)
                            mm = pe.matmul(PS[0:NS, 4, 0:n], K[:, C_SEL + (f - 1) * NS:C_SEL + f * NS],
                                           SQ[:, g % 2, 0:n], start=(f == 1), stop=(f == NF))
                            mm.then_inc(ss, 1)
                    if c == 1:
                        pe.wait_ge(w_in, 16)
                        if not known(q) or q:
                            pe.wait_ge(cnset, q)
                        for k in range(KT):
                            mm = pe.transpose(PS[0:DSEQ, 2, k * P:(k + 1) * P], CT_[:, k, PAST:SK], I_)
                        mm.then_inc(cn, 1)

            pe.wait_ge(w_in, 16)
            sequences(pe, front, back)
            pe.wait_ge(wv_in, 16)
            pe.wait_ge(olset, NSEQ)
            for h in range(NH):
                for k in range(KT):
                    mm = pe.matmul(PS[0:VH, 0, h * NS:(h + 1) * NS], WV[:, k, h * VH:(h + 1) * VH],
                                   OLAT[:, k, h].rearrange("p s q -> p (s q)"), start=(k == 0), stop=(k == KT - 1),
                                   skip_group_check=True)
            mm.then_inc(av, 1)

        @block.scalar
        def _(act):
            def front(q, s, behind):
                for b in range(TB):
                    act.wait_ge(turned, q * TB + b + 1)
                    if b < 4:
                        out = CT_[:, b // 2, (b % 2) * 512:(b % 2 + 1) * 512]
                        act.activation(out, PS[:, b % 2, :], ACT.Copy).then_inc(ct, 1)
                    else:
                        out = RT_[:, (b - 4) * 512:(b - 3) * 512]
                        act.activation(out, PS[0:ROPE, b % 2, :], ACT.Copy).then_inc(ct, 1)
                behind(0)
                for c, (a, n) in enumerate(CK):
                    for f in range(NF):
                        if c == 1 and f == 2:
                            behind(1)
                        g = NF * c + f
                        act.wait_ge(kraw, q * NC * NF + g + 1)
                        if g >= 2:
                            act.wait_ge(ss, q * NC * NF + g - 1)
                        act.activation(SQ[:, g % 2, 0:n], PS[:, g % 2, 0:n], ACT.Square).then_inc(sq, 1)
                    act.wait_ge(ss, q * NC * NF + NF * (c + 1))
                    act.activation(RS[:, a:a + n], PS[0:NS, 4, 0:n], ACT.Sqrt, bias=K[0:NS, C_EPS:C_EPS + 1]
                                   ).then_inc(root, 1)

            def back(q, s, part):
                if part == 0:
                    act.wait_ge(step, q * STEPS + STEPS)
                    if not known(q) or q:
                        act.wait_ge(pturn, q)
                    act.activation(PR[:], L[:], ACT.Exp, bias=ST[:, 1:2], scale=SCALE, accum_out=ST[:, 2:3]
                                   ).then_inc(expo, 1)
                if part == 1:
                    act.wait_ge(ol, q + 1)
                    for k in range(KT):
                        ins = act.activation(OLAT[:, k, :, bass.ds(q, 1), :].rearrange("p h s q -> p h (s q)"),
                                             PS[:, 7, k * NS:(k + 1) * NS].rearrange("p (h q) -> p h q", q=DSEQ),
                                             ACT.Copy)
                    ins.then_inc(olset, 1)

            sequences(act, front, back)
            act.wait_ge(av, 1)
            act.activation(AS[:].rearrange("p h n -> p (h n)"), PS[0:VH, 0, 0:NH * NS], ACT.Copy).then_inc(av, 1)

        @block.vector
        def _(dve):
            def new_keys(q):
                a = META + SEQ + q * DSEQ
                if not known(q) or q:
                    dve.wait_ge(sc, q * NC)
                    dve.wait_ge(cn, q)
                    dve.wait_ge(kraw, q * NC * NF)
                dve.tensor_copy(CT_[:, :, PAST:SK], CKV[:, :, bass.ds(a, DSEQ)])
                dve.tensor_copy(RT_[:, PAST:SK], KR[0:ROPE, bass.ds(a, DSEQ)])
                dve.tensor_copy(QA[:], QABS[:, :, bass.ds(q, 1)].rearrange("p k s h q -> p k (s h q)"))
                dve.tensor_copy(QR[:], QRS[:, bass.ds(q, 1)].rearrange("p s h q -> p (s h q)")).then_inc(newk, 1)

            def front(q, s, behind):
                at = q * STEPS
                behind(0)
                behind(1)
                for c, (a, n) in enumerate(CK):
                    dve.wait_ge(root, q * NC + c + 1)
                    if c == NC - 1 and (not known(q) or q + 1 < NSEQ):
                        new_keys(q + 1)
                    dve.reciprocal(RS[:, a:a + n], RS[:, a:a + n]).then_inc(step, 1)
                    dve.wait_ge(step, at + 3 * c + 1)
                    dve.wait_ge(sc, q * NC + c + 1)
                    dve.tensor_tensor(L[:, a:a + n], PS[0:NS, 5, 0:n], RS[:, a:a + n], ALU.mult).then_inc(step, 1)
                    dve.wait_ge(step, at + 3 * c + 2)
                    dve.tensor_tensor(L[:, a:a + n], PS[0:NS, 6, 0:n], L[:, a:a + n], ALU.add).then_inc(step, 1)
                    if c == 2:
                        dve.wait_ge(cn, q + 1)
                        if not known(q) or q:
                            dve.wait_ge(ol, q)
                        dve.tensor_copy(CN[:], PS[0:DSEQ, 2, 0:KVL]).then_inc(cnset, 1)
                at = at + 3 * NC
                dve.wait_ge(step, at)
                m = L[:, PAST:SK]
                dve.tensor_tensor(m, m, K[0:NS, C_SMASK:C_SMASK + DSEQ], ALU.add).then_inc(step, 1)
                dve.wait_ge(step, at + 1)
                dve.tensor_reduce(ST[:, 0:1], L[:], AX.X, ALU.max).then_inc(step, 1)
                dve.wait_ge(step, at + 2)
                dve.tensor_scalar(ST[:, 1:2], ST[:, 0:1], -SCALE, None, ALU.mult).then_inc(step, 1)

            def back(q, s, part):
                if part == 0:
                    dve.wait_ge(expo, q + 1)
                    dve.reciprocal(ST[:, 3:4], ST[:, 2:3]).then_inc(inv, 1)
                    dve.wait_ge(inv, q + 1)
                    dve.tensor_scalar(PR[:], PR[:], ST[:, 3:4], None, ALU.mult).then_inc(probs, 1)
                if part == 1:
                    if not known(q) or q:
                        dve.wait_ge(ol, q)
                    dve.wait_ge(pturn, q + 1)
                    dve.tensor_copy(PT[:, 0:NPG, :].rearrange("p a b -> p (a b)"), PS[:, 3, 0:NPG * NS])
                    dve.tensor_copy(PT[0:DSEQ, NPG, :], PS[0:DSEQ, 3, NPG * NS:(NPG + 1) * NS]).then_inc(pt, 1)

            new_keys(0)
            sequences(dve, front, back)


def merge_stage(nc, H, YC, M, weights, ahead, d):
    with ExitStack() as ctx:
        sb = lambda n, s, dt=F32: ctx.enter_context(nc.sbuf_tensor("mg_" + n, s, dt))
        sem = lambda n: ctx.enter_context(nc.semaphore("mg_" + n))
        W, w_in = weights.tile, weights.arrived
        A = sb("a", [P, CT, TQ])
        S = sb("s", [P, 2, 2, 352])
        PS = ctx.enter_context(nc.psum_tensor("mg_ps", [P, 2, 4, 512], F32))
        a_in, proj, gates, step, done = (sem(n) for n in ("a_in", "proj", "gates", "step", "done"))
        block = ctx.enter_context(nc.Block())

        @block.sync
        def _(sp):
            for k in range(CT):
                sp.dma_start(A[:, k, :], d["s_attn"][2 * k:2 * k + 2].rearrange("a p n -> (a p) n")
                             ).then_inc(a_in, 16)
            ahead.load(sp)
            with sp.Fori(0, KD // 2 - 1) as o:
                for s in range(2):
                    sp.wait_ge(proj, o * 6 + 3 * (s + 1))
                    sp.dma_start(W[:, s], d["w_merge"][bass.ds(o * 2 + s + 2, 1)].rearrange("o p b n -> (o p) b n")
                                 ).then_inc(w_in[s], 16)

        @block.tensor
        def _(pe):
            pe.wait_ge(a_in, 16 * CT)
            with pe.Fori(0, KD // 2) as o:
                for s in range(2):
                    pe.wait_ge(w_in[s], (o + 1) * 16)
                    for c, (a, n) in enumerate(QCH):
                        g = 3 * s + c
                        pe.wait_ge(done, o * 6 + g - 1) if g >= 2 else pe.wait_ge(done, o * 6)
                        at = 0
                        for m, (x, nk, lo) in enumerate(((H, KD, META), (H, KD, META), (YC, CT, 0), (A, CT, 0))):
                            for k in range(nk):
                                mm = pe.matmul(PS[:, g % 2, m, 0:n], W[:, s, at + k, :], x[:, k, lo + a:lo + a + n],
                                               start=(k == 0), stop=(k == nk - 1))
                            at += nk
                        mm.then_inc(proj, 1)

        @block.scalar
        def _(act):
            with act.Fori(0, KD // 2) as o:
                for g in range(6):
                    act.wait_ge(proj, o * 6 + g + 1)
                    act.wait_ge(done, o * 6 + g - 1) if g >= 2 else act.wait_ge(done, o * 6)
                    n = 352
                    act.activation(S[:, g % 2, :, :], PS[:, g % 2, 0:2, 0:n], ACT.Sigmoid).then_inc(gates, 1)

        @block.vector
        def _(dve):
            with dve.Fori(0, KD // 2) as o:
                for g in range(6):
                    a, n = QCH[g % 3]
                    dve.wait_ge(gates, o * 6 + g + 1)
                    dve.tensor_tensor(S[:, g % 2, :, :], PS[:, g % 2, 2:4, 0:n], S[:, g % 2, :, :], ALU.mult
                                      ).then_inc(step, 1)
                    dve.wait_ge(step, o * 6 + g + 1)
                    out = M[:, bass.ds(o * 2 + g // 3, 1), a:a + n].rearrange("p a n -> p (a n)")
                    dve.tensor_tensor(out, S[:, g % 2, 0, :], S[:, g % 2, 1, :], ALU.add).then_inc(done, 1)


def mix_stage(nc, X, M, weights, d):
    with ExitStack() as ctx:
        sem = lambda n: ctx.enter_context(nc.semaphore("mx_" + n))
        W, w_in = weights.tile, weights.arrived
        PS = ctx.enter_context(nc.psum_tensor("mx_ps", [P, 6, 512], F32))
        proj, done = sem("proj"), sem("done")
        block = ctx.enter_context(nc.Block())

        @block.sync
        def _(sp):
            with sp.Fori(0, KD // 2 - 1) as o:
                for s in range(2):
                    sp.wait_ge(proj, o * 6 + 3 * (s + 1))
                    sp.dma_start(W[:, s], d["w_mix"][bass.ds(o * 2 + s + 2, 1)].rearrange("o p b n -> (o p) b n")
                                 ).then_inc(w_in[s], 16)

        @block.tensor
        def _(pe):
            with pe.Fori(0, KD // 2) as o:
                for s in range(2):
                    pe.wait_ge(w_in[s], (o + 1) * 16)
                    if s == 0:
                        pe.wait_ge(done, o * 6)
                    for c, (a, n) in enumerate(QCH):
                        for k in range(KD):
                            mm = pe.matmul(PS[:, 3 * s + c, 0:n], W[:, s, k, :], M[:, k, a:a + n],
                                           start=(k == 0), stop=(k == KD - 1))
                        mm.then_inc(proj, 1)

        @block.vector
        def _(dve):
            with dve.Fori(0, KD // 2) as o:
                for g in range(6):
                    a, n = QCH[g % 3]
                    x = X[:, bass.ds(o * 2 + g // 3, 1), META + a:META + a + n].rearrange("p a n -> p (a n)")
                    dve.wait_ge(proj, o * 6 + g + 1)
                    dve.tensor_tensor(x, PS[:, g, 0:n], x, ALU.add).then_inc(done, 1)


def topk_stage(nc, K, H, SEL, weights, d):
    with ExitStack() as ctx:
        sb = lambda n, s, dt=F32: ctx.enter_context(nc.sbuf_tensor("tk_" + n, s, dt))
        sem = lambda n: ctx.enter_context(nc.semaphore("tk_" + n))
        W, w_in = weights.tile, weights.arrived
        QS = sb("q", [P, TQ])
        S = sb("s", [P, 2, NP, NK])
        S2 = sb("s2", [P, NP, NK])
        TV = sb("tv", [P, 2, 2, NP, TOPK])
        TI = sb("ti", [P, 2, 2, NP, TOPK], U32)
        IF = sb("if", [P, 2, NP, TOPK])
        CA = sb("cand", [P, NP, TOPK * TOPK])
        CB = sb("cand2", [P, NP, TOPK * TOPK])
        B = sb("best", [P, NP, TOPK])
        BW = sb("weight", [P, NP, TOPK])
        SM = sb("sum", [P, NP])
        PW = sb("place", [P, NP, TOPK], U32)
        PI = sb("ranks", [P, 2, NP, TOPK], U32)
        PF = sb("ranksf", [P, 2, NP * TOPK])
        EQ = sb("eq", [P, 2, NP * TOPK, TOPK])
        PAD = sb("pad", [1, 1])
        PQ = ctx.enter_context(nc.psum_tensor("tk_pq", [P, 3, 512], F32))
        PS = ctx.enter_context(nc.psum_tensor("tk_ps", [P, 3, 512], F32))
        (proj, qset, score, sset, cleared, half, cand, ifset, pair, eq, picked, expo, done) = (
            sem(n) for n in ("proj", "qset", "score", "sset", "cleared", "half", "cand", "ifset", "pair", "eq",
                             "picked", "expo", "done"))
        block = ctx.enter_context(nc.Block())
        known = lambda x: isinstance(x, int)
        HALF, PAIR = 5, 8

        @block.sync
        def _(sp):
            with sp.Fori(0, PH - 1) as h:
                for s in range(2):
                    sp.wait_ge(score, h * 2 + s + 2)
                    sp.dma_start(W[:, s], d["w_peer"][bass.ds(h * 2 + s + 2, 1)].rearrange("o p b n -> (o p) b n")
                                 ).then_inc(w_in[s], 16)

        @block.tensor
        def _(pe):
            pe.sem_inc(score, 1)
            with pe.Fori(0, PH) as h:
                for s in range(2):
                    q = h * 2 + s
                    pe.wait_ge(w_in[s], h * 16 + 16)
                    pe.wait_ge(qset, q + 1)
                    for c, (a, n) in enumerate(QCH):
                        for k in range(KD):
                            mm = pe.matmul(PQ[:, c, 0:n], W[:, s, k, :], H[:, k, META + a:META + a + n],
                                           start=(k == 0), stop=(k == KD - 1))
                    mm.then_inc(proj, 1)
                    pe.wait_ge(qset, q + 2)
                    pe.wait_ge(sset, q + 1)
                    for t in range(NP):
                        m = P if t < NP - 1 else LAST
                        mm = pe.matmul(PS[0:m, t // 4, (t % 4) * NK:(t % 4 + 1) * NK], QS[:, t * P:t * P + m],
                                       W[:, s, KD, :], start=True, stop=True, skip_group_check=True)
                    mm.then_inc(score, 1)

        @block.scalar
        def _(act):
            def copies(q, s):
                act.wait_ge(proj, q + 1)
                act.wait_ge(score, q + 1)
                for c, (a, n) in enumerate(QCH):
                    ins = act.activation(QS[:, a:a + n], PQ[:, c, 0:n], ACT.Copy)
                ins.then_inc(qset, 1)
                act.wait_ge(score, q + 2)
                act.wait_ge(half, q * HALF + 3)
                for c, (t, n) in enumerate(BANKS):
                    m = P if t + n < NP else LAST
                    ins = act.activation(S[0:m, s, t:t + n, :].rearrange("p a b -> p (a b)"),
                                         PS[0:m, c, 0:n * NK], ACT.Copy)
                ins.then_inc(sset, 1)

            def indices(h, slot):
                act.wait_ge(half, (h * 2 + 4) * HALF)
                if not known(h) or h:
                    act.wait_ge(picked, h * 2)
                act.activation(IF[:].rearrange("p c t k -> p (c t k)"),
                               TI[:, slot].rearrange("p c t k -> p (c t k)"), ACT.Copy).then_inc(ifset, 1)

            def exps(h):
                act.wait_ge(pair, h * PAIR + PAIR)
                act.activation(BW[:], BW[:], ACT.Exp).then_inc(expo, 1)

            act.sem_inc(qset, 1)
            act.sem_inc(sset, 1)
            act.wait_ge(cleared, 1)
            for q in range(3):
                copies(q, q % 2)

            def head(h, slot):
                indices(h, slot)
                copies(h * 2 + 3, 1)
                exps(h)
                copies(h * 2 + 4, 0)

            head(0, 0)
            head(1, 1)
            with act.Fori(1, PH // 2 - 1) as o:
                head(o * 2, 0)
                head(o * 2 + 1, 1)
            indices(PH - 2, 0)
            copies(PH * 2 - 1, 1)
            exps(PH - 2)
            indices(PH - 1, 1)
            exps(PH - 1)

        @block.gpsimd
        def _(pool):
            full = [P, NP, TOPK, TOPK]

            def sums(h, slot):
                pool.wait_ge(half, (h * 2 + 4) * HALF)
                if not known(h) or h:
                    pool.wait_ge(pair, h * PAIR)
                pool.tensor_tensor(CA[:].rearrange("p t (a b) -> p t a b", b=TOPK),
                                   TV[:, slot, 0].unsqueeze(3).to_broadcast(full),
                                   TV[:, slot, 1].unsqueeze(2).to_broadcast(full), ALU.add).then_inc(cand, 1)

            def marks(h):
                pool.wait_ge(ifset, h + 1)
                for c in range(2):
                    pool.wait_ge(eq, h * 2 + c + 1)
                    e = EQ[:, c].rearrange("p (t j) k -> p t j k", t=NP)
                    pool.tensor_tensor(e, e, IF[:, c].unsqueeze(2).to_broadcast(full), ALU.mult).then_inc(picked, 1)

            sums(0, 0)
            marks(0)
            sums(1, 1)
            marks(1)
            with pool.Fori(1, PH // 2) as o:
                for s in range(2):
                    sums(o * 2 + s, s)
                    marks(o * 2 + s)

        @block.vector
        def _(dve):
            def search(q, slot, s):
                at = (q + 2) * HALF
                dve.wait_ge(half, at)
                dve.wait_ge(sset, q + 2)
                dve.memset(PAD[:], 0.0)
                for t in range(NP):
                    ins = dve.max(TV[:, slot, s, t, 0:8], S[:, s, t, :])
                ins.then_inc(half, 1)
                dve.wait_ge(half, at + 1)
                dve.memset(PAD[:], 0.0)
                for t in range(NP):
                    ins = dve.max_index(TI[:, slot, s, t, 0:8], TV[:, slot, s, t, 0:8], S[:, s, t, :])
                ins.then_inc(half, 1)
                for t in range(NP):
                    ins = dve.match_replace(S2[:, t, :], TV[:, slot, s, t, 0:8], S[:, s, t, :], -3e38)
                ins.then_inc(half, 1)
                dve.wait_ge(half, at + 3)
                dve.memset(PAD[:], 0.0)
                for t in range(NP):
                    ins = dve.max(TV[:, slot, s, t, 8:16], S2[:, t, :])
                ins.then_inc(half, 1)
                dve.wait_ge(half, at + 4)
                dve.memset(PAD[:], 0.0)
                for t in range(NP):
                    ins = dve.max_index(TI[:, slot, s, t, 8:16], TV[:, slot, s, t, 8:16], S2[:, t, :])
                ins.then_inc(half, 1)

            def pairs(h):
                at = h * PAIR
                dve.wait_ge(half, (h * 2 + (4 if known(h) and h == PH - 1 else 5)) * HALF)
                dve.wait_ge(cand, h + 1)
                dve.memset(PAD[:], 0.0)
                for t in range(NP):
                    ins = dve.max(B[:, t, 0:8], CA[:, t, :])
                ins.then_inc(pair, 1)
                dve.wait_ge(pair, at + 1)
                dve.memset(PAD[:], 0.0)
                for t in range(NP):
                    dve.max_index(PW[:, t, 0:8], B[:, t, 0:8], CA[:, t, :])
                    ins = dve.match_replace(CB[:, t, :], B[:, t, 0:8], CA[:, t, :], -3e38)
                ins.then_inc(pair, 1)
                dve.wait_ge(pair, at + 2)
                dve.memset(PAD[:], 0.0)
                for t in range(NP):
                    ins = dve.max(B[:, t, 8:16], CB[:, t, :])
                ins.then_inc(pair, 1)
                dve.wait_ge(pair, at + 3)
                dve.memset(PAD[:], 0.0)
                for t in range(NP):
                    ins = dve.max_index(PW[:, t, 8:16], B[:, t, 8:16], CB[:, t, :])
                ins.then_inc(pair, 1)
                dve.wait_ge(pair, at + 4)
                dve.tensor_scalar(PI[:, 0], PW[:], 4, None, ALU.logical_shift_right).then_inc(pair, 1)
                dve.tensor_scalar(PI[:, 1], PW[:], TOPK - 1, None, ALU.bitwise_and).then_inc(pair, 1)
                dve.tensor_tensor(BW[:], B[:], B[:, :, 0:1].to_broadcast([P, NP, TOPK]), ALU.subtract
                                  ).then_inc(pair, 1)
                dve.wait_ge(pair, at + 7)
                dve.tensor_copy(PF[:], PI[:].rearrange("p c t j -> p c (t j)")).then_inc(pair, 1)
                dve.wait_ge(pair, at + 8)
                if not known(h) or h:
                    dve.wait_ge(done, h * 4)
                io16 = K[:, C_IOTA:C_IOTA + TOPK].unsqueeze(1).to_broadcast([P, NP * TOPK, TOPK])
                for c in range(2):
                    dve.tensor_tensor(EQ[:, c], PF[:, c, :].unsqueeze(2).to_broadcast([P, NP * TOPK, TOPK]), io16,
                                      ALU.is_equal).then_inc(eq, 1)

            def finish(h):
                out = lambda i: SEL[:, :, i, bass.ds(h, 1), :].rearrange("p t a k -> p t (a k)")
                dve.wait_ge(expo, h + 1)
                dve.tensor_reduce(SM[:], BW[:], AX.X, ALU.add).then_inc(done, 1)
                dve.wait_ge(done, h * 4 + 1)
                dve.reciprocal(SM[:], SM[:]).then_inc(done, 1)
                dve.wait_ge(done, h * 4 + 2)
                dve.tensor_tensor(out(2), BW[:], SM[:].unsqueeze(2).to_broadcast([P, NP, TOPK]), ALU.mult)
                for c in range(2):
                    dve.wait_ge(picked, h * 2 + c + 1)
                    dve.tensor_reduce(out(c), EQ[:, c].rearrange("p (t j) k -> p t j k", t=NP), AX.X, ALU.add
                                      ).then_inc(done, 1)

            def head(h, slot):
                pairs(h)
                search(h * 2 + 3, 1 - slot, 1)
                dve.wait_ge(ifset, h + 1)
                search(h * 2 + 4, slot, 0)
                finish(h)

            dve.memset(S[:, :, NP - 1, :], 0.0).then_inc(cleared, 1)
            dve.sem_inc(half, 2 * HALF)
            search(0, 0, 0)
            search(1, 0, 1)
            search(2, 1, 0)
            with dve.Fori(0, PH // 2 - 1) as o:
                head(o * 2, 0)
                head(o * 2 + 1, 1)
            pairs(PH - 2)
            search(PH * 2 - 1, 1, 1)
            finish(PH - 2)
            pairs(PH - 1)
            finish(PH - 1)


def route_stage(nc, K, SEL, d):
    with ExitStack() as ctx:
        sb = lambda n, s, dt=F32: ctx.enter_context(nc.sbuf_tensor("rt_" + n, s, dt))
        sem = lambda n: ctx.enter_context(nc.semaphore("rt_" + n))
        TR = sb("tr", [P, TQ])
        TI = sb("ti", [P, 2, TQ], BF16)
        TB = 8
        TP = 5
        NBT = TT // TB
        UN = 4
        IO = sb("iota", [P, NK, TB], BF16)
        M1 = sb("mark1", [P, 2, NK, TB], BF16)
        M2 = sb("mark2", [P, 2, NK, TB], BF16)
        O1 = sb("one1", [P, 2, TB, NK])
        OG = sb("one2g", [P, 2, TB, NK])
        STG = sb("stage", [P, 2, NK, TT])
        PS = ctx.enter_context(nc.psum_tensor("rt_ps", [P, 4, 512], F32))
        PT = ctx.enter_context(nc.psum_tensor("rt_pt", [P, 3, 512], F32))
        stored = [sem(f"stored{s}") for s in range(2)]
        turned, tr, ranks, mark1, mark2, one1, one2, one2v, gm, gset = (
            sem(n) for n in ("turned", "tr", "ranks", "mark1", "mark2", "one1", "one2", "one2v", "gm", "gset"))
        block = ctx.enter_context(nc.Block())

        def tiles(eng, tile):
            with eng.Fori(0, NT // 2) as o:
                tile(o * 2, 0, o)
                tile(o * 2 + 1, 1, o)
            for t in range(NT // 2 * 2, NT):
                tile(t, t % 2, t // 2)

        @block.sync
        def _(sp):
            for s in range(2):
                sp.sem_inc(stored[s], 16)

            def tile(t, s, o):
                sp.wait_ge(gset, t * NBT + NBT + 2)
                dst = d["s_route"][t] if isinstance(t, int) else \
                    d["s_route"][bass.ds(t, 1)].rearrange("o p n -> (o p) n")
                sp.dma_start(dst, STG[:, s].rearrange("p a b -> p (a b)")).then_inc(stored[s], 16)

            tiles(sp, tile)
            sp.wait_ge(stored[0], 16 * (NT - NT // 2 + 1))
            sp.wait_ge(stored[1], 16 * (NT // 2 + 1))

        @block.tensor
        def _(pe):
            pe.sem_inc(gm, 2)
            for i in range(3):
                for c, (t0, n) in enumerate(BANKS):
                    if 3 * i + c >= 3:
                        pe.wait_ge(tr, 3 * i + c - 2)
                    for t in range(t0, t0 + n):
                        m = P if t < NP - 1 else LAST
                        mm = pe.transpose(PT[:, c, (t - t0) * P:(t - t0) * P + m],
                                          SEL[0:m, t, i].rearrange("p h k -> p (h k)"), K[0:m, C_ID:C_ID + m])
                    mm.then_inc(turned, 1)

            def tile(t, slot, o):
                with pe.Fori(0, NBT // UN) as b:
                    for i in range(UN):
                        n, s = t * NBT + b * UN + i, i % 2
                        pe.wait_ge(one1, n + 3)
                        pe.wait_ge(one2, n + 3)
                        pe.wait_ge(one2v, n + 1)
                        pe.wait_ge(gset, n + 1)
                        for j in range(TB):
                            mm = pe.matmul(PS[:, 2 * s + j // 4, (j % 4) * NK:(j % 4 + 1) * NK], O1[:, s, j, :],
                                           OG[:, s, j, :], start=True, stop=True, skip_group_check=True)
                        mm.then_inc(gm, 1)

            tiles(pe, tile)

        @block.scalar
        def _(act):
            act.sem_inc(gset, 2)
            act.sem_inc(one1, 2)
            for i in range(3):
                for c, (t0, n) in enumerate(BANKS):
                    act.wait_ge(turned, 3 * i + c + 1)
                    m = min(n * P, TQ - t0 * P)
                    out = TI[:, i] if i < 2 else TR[:]
                    act.activation(out[:, t0 * P:t0 * P + m], PT[:, c, 0:m], ACT.Copy).then_inc(tr, 1)

            def widen(n, s):
                act.wait_ge(mark1, n + 1)
                act.wait_ge(gm, n + 1)
                act.activation(O1[:, s], M1[:, s].rearrange("p i t -> p t i"), ACT.Copy).then_inc(one1, 1)

            def keep(slot, n, b, i):
                act.wait_ge(gm, n + 3)
                for c in range(2):
                    tok = (b * UN + i) * TB + 4 * c
                    ins = act.activation(STG[:, slot, :, bass.ds(tok, 4)].rearrange("p i t -> p t i"),
                                         PS[:, 2 * (i % 2) + c, :].rearrange("p (t i) -> p t i", i=NK), ACT.Copy)
                ins.then_inc(gset, 1)

            def tile(t, slot, o):
                act.wait_ge(stored[slot], o * 16 + 16)
                whole = NBT // UN - (known(t) and t == NT - 1)
                with act.Fori(0, whole) as b:
                    for i in range(UN):
                        n, s = t * NBT + b * UN + i, i % 2
                        widen(n + 1, 1 - s)
                        keep(slot, n, b, i)
                if whole < NBT // UN:
                    for i in range(UN):
                        n = (NT - 1) * NBT + whole * UN + i
                        if i + 1 < UN:
                            widen(n + 1, (i + 1) % 2)
                        keep(slot, n, whole, i)

            widen(0, 0)
            tiles(act, tile)

        def weigh(eng, t, b, i, first, last):
            s = i % 2
            w = TR[:, bass.ds(t * TT + (b * UN + i) * TB + first, last - first)].unsqueeze(2)
            return eng.tensor_tensor(OG[:, s, first:last], M2[:, s, :, first:last].rearrange("p i t -> p t i"),
                                     w.to_broadcast([P, last - first, NK]), ALU.mult)

        @block.gpsimd
        def _(pool):
            def tile(t, slot, o):
                with pool.Fori(0, NBT // UN) as b:
                    for i in range(UN):
                        n, s = t * NBT + b * UN + i, i % 2
                        pool.wait_ge(mark2, n + 1)
                        pool.wait_ge(gm, n + 1)
                        weigh(pool, t, b, i, 0, TP).then_inc(one2, 1)

            pool.sem_inc(one2, 2)
            tiles(pool, tile)

        @block.vector
        def _(dve):
            def tile(t, slot, o):
                with dve.Fori(0, NBT // UN) as b:
                    for i in range(UN):
                        n, s = t * NBT + b * UN + i, i % 2
                        pick = lambda half: TI[:, half, bass.ds(t * TT + (b * UN + i) * TB, TB)].unsqueeze(1
                                                          ).to_broadcast([P, NK, TB])
                        dve.wait_ge(one2, n + 1)
                        dve.tensor_tensor(M2[:, s], IO[:], pick(1), ALU.is_equal).then_inc(mark2, 1)
                        dve.wait_ge(one1, n + 1)
                        dve.tensor_tensor(M1[:, s], IO[:], pick(0), ALU.is_equal).then_inc(mark1, 1)
                        dve.wait_ge(mark2, n + 1)
                        dve.wait_ge(gm, n + 1)
                        weigh(dve, t, b, i, TP, TB).then_inc(one2v, 1)

            dve.tensor_copy(IO[:], K[:, C_IOTA:C_IOTA + NK].unsqueeze(2).to_broadcast([P, NK, TB])).then_inc(ranks, 1)
            dve.wait_ge(ranks, 1)
            dve.wait_ge(tr, 9)
            tiles(dve, tile)


def split_stage(nc, HH, HL, d):
    with ExitStack() as ctx:
        S = ctx.enter_context(nc.sbuf_tensor("sp_s", [P, 3, TQ], F32))
        s_in = [ctx.enter_context(nc.semaphore(f"sp_in{i}")) for i in range(3)]
        high, low = (ctx.enter_context(nc.semaphore("sp_" + n)) for n in ("high", "low"))
        block = ctx.enter_context(nc.Block())

        @block.sync
        def _(sp):
            for k in range(KD):
                if k >= 3:
                    sp.wait_ge(low, k - 2)
                sp.dma_start(S[:, k % 3, :], d["s_h"][:, k, :]).then_inc(s_in[k % 3], 16)

        @block.scalar
        def _(act):
            for k in range(KD):
                act.wait_ge(s_in[k % 3], 16 * (k // 3 + 1))
                act.activation(HH[:, k, :], S[:, k % 3, :], ACT.Copy).then_inc(high, 1)

        @block.vector
        def _(dve):
            for k in range(KD):
                dve.wait_ge(high, k + 1)
                dve.tensor_tensor(HL[:, k, :], S[:, k % 3, :], HH[:, k, :].bitcast(F32), ALU.subtract
                                  ).then_inc(low, 1)
            dve.wait_ge(low, KD)


def expert_stage(nc, X, HH, HL, d):
    with ExitStack() as ctx:
        sb = lambda n, s, dt=F32: ctx.enter_context(nc.sbuf_tensor("ex_" + n, s, dt))
        sem = lambda n: ctx.enter_context(nc.semaphore("ex_" + n))
        UR = sb("ur", [P, 2, KD * P])
        VR = sb("vr", [P, D])
        UH = sb("uh", [P, 2, KD * P], F32R)
        UL = sb("ul", [P, 2, KD * P], F32R)
        VHI = sb("vh", [P, 2, GRP, D], F32R)
        VLO = sb("vl", [P, 2, GRP, D], F32R)
        R = sb("r", [P, NT, GRP, TT])
        WH = sb("wh", [P, 2, GRP, TQ], F32R)
        WL = sb("wl", [P, 2, GRP, TQ], F32R)
        G = sb("g", [P, 2, 4 * TT])
        WR = sb("wr", [P, 4 * TT])
        PA = ctx.enter_context(nc.psum_tensor("ex_pa", [P, 3, 512], F32))
        PO = ctx.enter_context(nc.psum_tensor("ex_po", [P, 4, 512], F32))
        u_in = [sem(f"u_in{s}") for s in range(2)]
        v_in, r_in, u_high, u_set, v_high, v_set, a_mm, gelu, w_mul, w_high, w_set, o_mm, o_free, stored = (
            sem(n) for n in ("v_in", "r_in", "u_high", "u_set", "v_high", "v_set", "a_mm", "gelu", "w_mul",
                             "w_high", "w_set", "o_mm", "o_free", "stored"))
        block = ctx.enter_context(nc.Block())
        NG = NK // GRP
        NC = 3 * GRP
        NO = 3 * KD
        CH = [(t * TT, n * TT) for t, n in TILES]
        known = lambda x: isinstance(x, int)

        def schedule(eng, first, second):
            first(0, 0)
            with eng.Fori(0, NG // 2 - 1) as o:
                first(o * 2 + 1, 1)
                second(o * 2, 0)
                first(o * 2 + 2, 0)
                second(o * 2 + 1, 1)
            first(NG - 1, 1)
            second(NG - 2, 0)
            second(NG - 1, 1)

        @block.sync
        def _(sp):
            def load_u(n, slot):
                src = d["u"][n] if known(n) else d["u"][bass.ds(n, 1)].rearrange("o p m -> (o p) m")
                sp.dma_start(UR[:, slot, :], src).then_inc(u_in[slot], 16)

            def load_v(n):
                sp.dma_start(VR[:], d["v"][:, bass.ds(n * D, D)]).then_inc(v_in, 16)

            def load_r(g):
                sp.dma_start(R[:].rearrange("p t g n -> p t (g n)"),
                             d["s_route4"][:, :, bass.ds(g * (GRP * TT), GRP * TT)]).then_inc(r_in, 16)

            def first(g, s):
                for b in range(GRP):
                    m = g * GRP + b
                    if not known(m) or m + 2 < NK:
                        sp.wait_ge(u_set, m + 1)
                        load_u(m + 2, b)
                    if not known(m) or m + 1 < NK:
                        sp.wait_ge(v_set, m + 1)
                        load_v(m + 1)
                if not known(g) or g + 1 < NG:
                    sp.wait_ge(w_mul, (g + 1) * NC)
                    load_r(g + 1)

            load_u(0, 0)
            load_r(0)
            load_u(1, 1)
            load_v(0)
            schedule(sp, first, lambda g, s: None)
            sp.wait_ge(o_free, NG * NO + 4)
            sp.dma_start(d["o_y"], X[:, :, META:T]).then_inc(stored, 16)
            sp.wait_ge(stored, 16)

        @block.tensor
        def _(pe):
            def first(g, s):
                for b in range(GRP):
                    pe.wait_ge(u_set, g * GRP + b + 1)
                    for c, (a, n) in enumerate(CH):
                        j = 3 * b + c
                        if not known(g) or g * NC + j >= 3:
                            pe.wait_ge(gelu, g * NC + j - 2)
                        for k in range(KD):
                            u = slice(k * P, (k + 1) * P)
                            for i, (l, r) in enumerate(((UH, HH), (UH, HL), (UL, HH))):
                                mm = pe.matmul(PA[:, c, 0:n], l[:, b, u], r[:, k, a:a + n],
                                               start=(k == 0 and i == 0), stop=(k == KD - 1 and i == 2))
                        mm.then_inc(a_mm, 1)

            def second(g, s):
                pe.wait_ge(w_set, (g + 1) * NC)
                pe.wait_ge(v_set, (g + 1) * GRP)
                for j in range(NO):
                    k, (a, n) = j // 3, CH[j % 3]
                    pe.wait_ge(o_free, g * NO + j + 1)
                    for b in range(GRP):
                        for i, (l, r) in enumerate(((VHI, WH), (VHI, WL), (VLO, WH))):
                            mm = pe.matmul(PO[:, j % 4, 0:n], l[:, s, b, k * P:(k + 1) * P], r[:, s, b, a:a + n],
                                           start=(b == 0 and i == 0), stop=(b == GRP - 1 and i == 2))
                    mm.then_inc(o_mm, 1)

            schedule(pe, first, second)

        @block.scalar
        def _(act):
            def high_u(n, slot):
                act.wait_ge(u_in[slot], (n // 2 + 1) * 16 if known(n) else (n - slot) * 8 + 16)
                if not known(n) or n >= 2:
                    act.wait_ge(a_mm, n * 3 - 3)
                act.activation(UH[:, slot, :], UR[:, slot, :], ACT.Copy).then_inc(u_high, 1)

            def first(g, s):
                for b in range(GRP):
                    m = g * GRP + b
                    if not known(m) or m + 1 < NK:
                        high_u(m + 1, 1 - b)
                    for c, (a, n) in enumerate(CH):
                        j = 3 * b + c
                        act.wait_ge(a_mm, g * NC + j + 1)
                        if not known(g) or g * NC + j >= 2:
                            act.wait_ge(w_mul, g * NC + j - 1)
                        act.activation(G[:, j % 2, 0:n], PA[:, c, 0:n], ACT.Gelu).then_inc(gelu, 1)
                        if c == 0:
                            act.wait_ge(v_in, m * 16 + 16)
                            if not known(g) or g >= 2:
                                act.wait_ge(o_mm, g * NO - NO)
                            act.activation(VHI[:, s, b, :], VR[:], ACT.Copy).then_inc(v_high, 1)

            high_u(0, 0)
            schedule(act, first, lambda g, s: None)

        @block.vector
        def _(dve):
            def low_u(n, slot):
                dve.wait_ge(u_high, n + 1)
                dve.tensor_tensor(UL[:, slot, :], UR[:, slot, :], UH[:, slot, :].bitcast(F32), ALU.subtract
                                  ).then_inc(u_set, 1)

            def first(g, s):
                for b in range(GRP):
                    m = g * GRP + b
                    if not known(m) or m + 1 < NK:
                        low_u(m + 1, 1 - b)
                    if b == 0:
                        dve.wait_ge(r_in, g * 16 + 16)
                        if not known(g) or g >= 2:
                            dve.wait_ge(o_mm, g * NO - NO)
                    for c, (a, n) in enumerate(CH):
                        j = g * NC + 3 * b + c
                        t, nt = TILES[c]
                        v3 = lambda x: x.rearrange("p (t n) -> p t n", n=TT)
                        dve.wait_ge(gelu, j + 1)
                        if not known(j) or j >= 1:
                            dve.wait_ge(w_set, j)
                        dve.tensor_tensor(v3(WR[:, 0:n]), v3(G[:, (3 * b + c) % 2, 0:n]), R[:, t:t + nt, b, :],
                                          ALU.mult).then_inc(w_mul, 1)
                        dve.wait_ge(w_mul, j + 1)
                        dve.tensor_copy(WH[:, s, b, a:a + n], WR[:, 0:n]).then_inc(w_high, 1)
                        dve.wait_ge(w_high, j + 1)
                        dve.tensor_tensor(WL[:, s, b, a:a + n], WR[:, 0:n], WH[:, s, b, a:a + n].bitcast(F32),
                                          ALU.subtract).then_inc(w_set, 1)
                        if c == 0:
                            dve.wait_ge(v_high, m + 1)
                            dve.tensor_tensor(VLO[:, s, b, :], VR[:], VHI[:, s, b, :].bitcast(F32), ALU.subtract
                                              ).then_inc(v_set, 1)

            def second(g, s):
                for j in range(NO):
                    k, (a, n) = j // 3, CH[j % 3]
                    x = X[:, k, META + a:META + a + n]
                    dve.wait_ge(o_mm, g * NO + j + 1)
                    dve.tensor_tensor(x, PO[:, j % 4, 0:n], x, ALU.add).then_inc(o_free, 1)

            dve.sem_inc(o_free, 4)
            low_u(0, 0)
            schedule(dve, first, second)


def build(nc, d):
    with ExitStack() as ctx:
        X = ctx.enter_context(nc.sbuf_tensor("X", [P, KD, T], F32))
        with ExitStack() as trunk:
            K = trunk.enter_context(nc.sbuf_tensor("K", [P, C_ALL], F32))
            SEL = trunk.enter_context(nc.sbuf_tensor("SEL", [P, NP, 3, PH, TOPK], F32))
            const_in = trunk.enter_context(nc.semaphore("const_in"))
            with nc.Block() as block:
                @block.sync
                def _(sp):
                    sp.dma_start(K[:], d["const"]).then_inc(const_in, 16)
                    sp.wait_ge(const_in, 16)
            with ExitStack() as normed:
                H = normed.enter_context(nc.sbuf_tensor("H", [P, KD, T], F32))
                with ExitStack() as mid:
                    YC = mid.enter_context(nc.sbuf_tensor("YC", [P, CT, TQ], F32))
                    QABS = mid.enter_context(nc.sbuf_tensor("QABS", [P, KT, NSEQ, NH, DSEQ], F32))
                    QRS = mid.enter_context(nc.sbuf_tensor("QRS", [ROPE, NSEQ, NH, DSEQ], F32))
                    CKV = mid.enter_context(nc.sbuf_tensor("CKV", [P, KT, T], F32))
                    KR = mid.enter_context(nc.sbuf_tensor("KR", [P, T], F32))
                    with ExitStack() as heads:
                        CQ = heads.enter_context(nc.sbuf_tensor("CQ", [P, QT, T], F32))
                        CS = heads.enter_context(nc.sbuf_tensor("CS", [P, 2, T], F32))
                        w_head = Ahead(nc, heads, "w_head", [P, 2, QT * HD + KT * NOPE], d["w_head"])
                        with ExitStack() as first:
                            w_lat = Ahead(nc, first, "w_lat", [P, 2, KD, P], d["w_lat"])
                            with ExitStack() as conv:
                                w_conv = Ahead(nc, conv, "w_conv", [P, 2, 3, KD, P],
                                               [d["w_conv"][s].rearrange("a p k n -> p a k n") for s in range(2)])
                                norm_stage(nc, "n1_", X, H, K, d["g_mix"], w_conv, x_dram=d["x"])
                                conv_stage(nc, H, YC, w_conv, w_lat, d)
                            latent_stage(nc, H, K, CQ, CKV, KR, CS, w_lat, w_head, d)
                        query_stage(nc, K, CQ, CKV, KR, CS, QABS, QRS, w_head, d)
                    w_merge = Ahead(nc, mid, "w_merge", [P, 2, 2 * KD + 2 * CT, P], d["w_merge"])
                    with ExitStack() as pages:
                        cached = Cached(nc, pages, d)
                        prompt_stage(nc, K, CKV, KR, cached, d)
                        decode_stage(nc, K, CKV, KR, QABS, QRS, cached, w_merge, d)
                    w_mix = Ahead(nc, mid, "w_mix", [P, 2, KD, P], d["w_mix"])
                    M = mid.enter_context(nc.sbuf_tensor("M", [P, KD, TQ], F32))
                    merge_stage(nc, H, YC, M, w_merge, w_mix, d)
                    mix_stage(nc, X, M, w_mix, d)
                w_peer = Ahead(nc, normed, "w_peer", [P, 2, KD + 1, P], d["w_peer"])
                norm_stage(nc, "n2_", X, H, K, d["g_ffn"], w_peer, h_dram=d["s_h"])
                topk_stage(nc, K, H, SEL, w_peer, d)
            route_stage(nc, K, SEL, d)
        HH = ctx.enter_context(nc.sbuf_tensor("HH", [P, KD, TQ], F32R))
        HL = ctx.enter_context(nc.sbuf_tensor("HL", [P, KD, TQ], F32R))
        split_stage(nc, HH, HL, d)
        expert_stage(nc, X, HH, HL, d)


def constants():
    K = np.zeros((P, C_ALL), np.float32)
    r = np.arange(P)
    K[:, C_ONES:C_ONES + P] = 1
    K[:, C_MEAN:C_MEAN + P] = 1 / D
    K[:, C_KV:C_KV + P] = 1 / KVL
    K[:, C_R32:C_R32 + P] = (r[:, None] // ROPE == r[None] // ROPE) / ROPE
    spread = np.zeros((ROWS, NJ * HD), np.float32)
    for j in range(NJ):
        for row, lo, hi in [(j, 0, NOPE)] if j < 3 else [(2 * j - 3, 0, NOPE), (2 * j - 2, NOPE, HD)]:
            K[lo:hi, C_SUM + j * ROWS + row] = 1 / (hi - lo)
            spread[row, j * HD + lo:j * HD + hi] = 1
    K[:, C_ID:C_ID + P] = np.eye(P)
    for f in range(4):
        K[:, C_SEL + f * NS:C_SEL + (f + 1) * NS] = ((2 * f + r[:, None] // NOPE) == np.arange(NS)[None] // DSEQ) / NOPE
    K[:, C_MASK:C_MASK + P + META] = np.where(np.arange(P + META)[None] <= r[:, None] + META, 0, NEG)
    K[:NS, C_SMASK:C_SMASK + DSEQ] = np.where(np.arange(DSEQ)[None] <= np.arange(NS)[:, None] % DSEQ, 0, NEG)
    K[:, C_IOTA:C_IOTA + P] = r[None]
    K[:, C_EPS] = EPS
    pos = np.concatenate([np.arange(KEYS), np.tile(PAST + np.arange(DSEQ), NSEQ)]).astype(np.float32)
    freq = np.float32(10000.0) ** (-np.arange(0, ROPE, 2, dtype=np.float32) / np.float32(ROPE))
    ang = pos[None, :] * freq[:, None]
    c, s = np.cos(ang).astype(np.float32), np.sin(ang).astype(np.float32)
    cs = np.stack([np.tile(np.concatenate([c, c]), (4, 1)), np.tile(np.concatenate([-s, s]), (4, 1))], 1)
    return K, np.ascontiguousarray(cs), spread


def kernel(**inputs):
    import concourse.bacc as bacc
    from concourse.bass_utils import run_bass_kernel_spmd

    a = {k: np.asarray(v) for k, v in inputs.items()}
    K, cs, spread = constants()
    tiles = lambda w: w.reshape(-1, P, w.shape[1]).transpose(1, 0, 2)
    blocks = lambda w: w.reshape(w.shape[0] // P, P, -1, P).transpose(2, 1, 0, 3)
    w_in = a["w_in"][0]
    edges = np.cumsum([0, CW, CW, CW, QL, KVL, ROPE, D, D])
    wB, wC, wX, wQ, wKV, wKR, wGC, wGA = (w_in[:, edges[i]:edges[i + 1]] for i in range(8))
    cols = lambda g: g.reshape(-1, P).T
    gq = np.concatenate([a["g_q_nope"][0], a["g_q_rope"][0]])
    g_head = np.zeros((P, 2), np.float32)
    g_head[:HD, 0] = gq
    g_head[:NOPE, 1] = a["g_k_nope"][0]
    uq, uk, uv = a["w_uq"][0], a["w_uk"][0], a["w_uv"][0]
    per_head = lambda w: w.reshape(-1, P, NH, w.shape[-1]).transpose(2, 1, 0, 3).reshape(NH, P, -1)
    feeds = {
        "const": K,
        "cossin": cs,
        "spread": spread,
        "x": tiles(np.concatenate([a["meta_tokens"], a["x_prompt"][0], a["x_sample"].reshape(NS, D)]).T),
        "g_mix": cols(a["norm_mix"][0]),
        "g_ffn": cols(a["norm_ffn"][0]),
        "w_conv": np.stack([blocks(wB), blocks(wC), blocks(wX)], 1),
        "taps": a["conv_w"][0].reshape(3, CT, P).transpose(2, 1, 0),
        "state": a["state_conv"][0].reshape(NSEQ, 2, CT, P).transpose(3, 2, 0, 1),
        "w_lat": np.concatenate([blocks(wQ), blocks(wKV), blocks(np.tile(wKR, (1, 4)))]),
        "g_lat": np.concatenate([cols(a["g_q_lat"][0]), cols(a["g_kv_lat"][0]),
                                 np.tile(a["g_k_rope"][0], 4)[:, None]], 1),
        "g_head": g_head,
        "w_head": np.concatenate([per_head(uq), per_head(uk)], 2),
        "w_ukT": uk.transpose(2, 1, 0),
        "w_uk": tiles(uk.reshape(KVL, -1)),
        "w_uv": tiles(uv.reshape(KVL, -1)),
        "pages": a["page_table"].reshape(1, -1),
        "cache": a["cache_ckv"][0],
        "krope": a["cache_krope"][0],
        "w_merge": np.concatenate([blocks(wGC), blocks(wGA), blocks(a["w_conv_out"][0]),
                                   blocks(a["w_attn_out"][0])], 2),
        "w_mix": blocks(a["w_mix_out"][0]),
        "w_peer": np.concatenate([blocks(a["w_peer_q"][0]), a["peer_sub_keys"][0].transpose(1, 0, 3, 2).reshape(
            HC, P, 1, NK)], 2),
        "u": a["peer_u"][0].reshape(NK, NK, KD, P).transpose(1, 3, 2, 0).reshape(NK, P, KD * P),
        "v": a["peer_v"][0].reshape(NK, NK * D),
    }
    nc = bacc.Bacc("TRN2", target_bir_lowering=False, num_devices=1)
    arrays, d = {}, {}
    for name, x in feeds.items():
        x = np.ascontiguousarray(x)
        arrays["in_" + name] = x
        d[name] = nc.dram_tensor("in_" + name, x.shape, mybir.dt.from_np(x.dtype), kind="ExternalInput").ap()
    outs = {"o_y": (P, KD, TQ), "o_ckv": (P, KT, T), "o_kr": (ROPE, T), "o_convp": (P, CT, 2),
            "o_convs": (P, CT, NSEQ, 2)}
    for name, shape in outs.items():
        d[name] = nc.dram_tensor(name, shape, F32, kind="ExternalOutput").ap()
    s_attn = nc.dram_tensor("s_attn", (NH, VH, TQ), F32)
    d["s_attn"] = s_attn.ap()
    d["s_q"] = nc.dram_tensor("s_q", (NH, HD, SEQ), F32).ap()
    d["s_k"] = nc.dram_tensor("s_k", (NH, NOPE, KEYS), F32).ap()
    d["s_h"] = nc.dram_tensor("s_h", (P, KD, TQ), F32).ap()
    s_route = nc.dram_tensor("s_route", (NT, P, NK * TT), F32)
    d["s_route"] = s_route.ap()
    d["s_route4"] = s_route.ap().rearrange("t p n -> p t n")
    build(nc, d)
    r = run_bass_kernel_spmd(nc, [arrays], core_ids=[0]).results[0]
    y = r["o_y"].transpose(2, 1, 0).reshape(TQ, D)
    ckv = r["o_ckv"].transpose(2, 1, 0).reshape(T, KVL)
    kr = r["o_kr"].T
    return (
        y[:SEQ].reshape(1, SEQ, D), y[SEQ:].reshape(NSEQ, DSEQ, D),
        ckv[:KEYS].reshape(1, 1, KEYS, KVL), kr[:KEYS].reshape(1, 1, KEYS, ROPE),
        r["o_convp"].transpose(2, 1, 0).reshape(1, 1, 2, CW),
        ckv[KEYS:].reshape(1, NSEQ, DSEQ, KVL), kr[KEYS:].reshape(1, NSEQ, DSEQ, ROPE),
        r["o_convs"].transpose(2, 3, 1, 0).reshape(1, NSEQ, 2, CW),
    )
```
